# Optimizing a Trainium2 kernel written in Bass

```python
import jax, jax.numpy as jnp
from jax import lax
import numpy as np

D_MODEL = 1024
BATCH = 1
SEQ = 256
DEPTH = 1

HEAD_DIM = 64
ATTN_GROUPS = ((128, 1), (512, 4), (2048, 16))
N_GROUPS = len(ATTN_GROUPS)
ATTN_HEADS_PER_GROUP = 4
ATTN_GROUP_WIDTH = ATTN_HEADS_PER_GROUP * HEAD_DIM
Q_BLOCK = 128
ROPE_THETA = 10000.0
RWKV_HEADS = 8
RWKV_WIDTH = RWKV_HEADS * HEAD_DIM
DECAY_LORA = 32
ICLR_LORA = 32
GATE_LORA = 96
RWKV_GN_EPS = 64e-5
D_FF = 4 * D_MODEL
PLE_DIM = 256
NORM_EPS = 1e-6

ATTN_QKV_COLS = 3 * N_GROUPS * ATTN_GROUP_WIDTH
RWKV_SPLITS = (RWKV_WIDTH, 2 * RWKV_WIDTH, 3 * RWKV_WIDTH,
               3 * RWKV_WIDTH + DECAY_LORA, 3 * RWKV_WIDTH + DECAY_LORA + ICLR_LORA)
RWKV_COLS = 3 * RWKV_WIDTH + DECAY_LORA + ICLR_LORA + GATE_LORA
GATE_COLS = 2 * D_MODEL
IN_COLS = ATTN_QKV_COLS + RWKV_COLS + GATE_COLS


def rmsnorm(x, g):
    xf = x.astype(jnp.float32)
    y = xf * lax.rsqrt(jnp.mean(xf * xf, axis=-1, keepdims=True) + NORM_EPS)
    return (y * g.astype(jnp.float32)).astype(x.dtype)

def rope(x, pos):
    half = HEAD_DIM // 2
    inv_freq = ROPE_THETA ** (-jnp.arange(0, HEAD_DIM, 2, dtype=jnp.float32) / HEAD_DIM)
    ang = pos[:, None] * inv_freq[None, :]
    ang = ang.reshape((pos.shape[0],) + (1,) * (x.ndim - 3) + (half,))
    c, s = jnp.cos(ang), jnp.sin(ang)
    xf = x.astype(jnp.float32)
    x1, x2 = xf[..., :half], xf[..., half:]
    return jnp.concatenate([x1 * c - x2 * s, x2 * c + x1 * s], axis=-1).astype(x.dtype)

def token_shift(z):
    return jnp.pad(z[:, :-1], ((0, 0), (1, 0), (0, 0)))

def dilated_attention_branch(z_attn):
    B, S, _ = z_attn.shape
    qkv = z_attn.reshape(B, S, 3, N_GROUPS, ATTN_HEADS_PER_GROUP, HEAD_DIM)
    pos = jnp.arange(S, dtype=jnp.float32)
    q = rope(qkv[:, :, 0], pos)
    k = rope(qkv[:, :, 1], pos)
    v = qkv[:, :, 2]
    qs = [q[:, :, g] for g in range(N_GROUPS)]
    ks = [k[:, :, g] for g in range(N_GROUPS)]
    vs = [v[:, :, g] for g in range(N_GROUPS)]
    scale = HEAD_DIM ** -0.5

    def block(bi):
        start = bi * Q_BLOCK
        t = start + jnp.arange(Q_BLOCK)
        outs, lses = [], []
        for g, (window, dil) in enumerate(ATTN_GROUPS):
            j = jnp.arange(window // dil + 1)
            idx = t[:, None] - dil * j[None, :]
            valid = idx >= 0
            idx_c = jnp.maximum(idx, 0)
            qb = lax.dynamic_slice_in_dim(qs[g], start, Q_BLOCK, axis=1)
            kg = jnp.take(ks[g], idx_c, axis=1)
            vg = jnp.take(vs[g], idx_c, axis=1)
            s = jnp.einsum('bqhd,bqjhd->bqhj', qb, kg, preferred_element_type=jnp.float32) * scale
            s = jnp.where(valid[None, :, None, :], s, -jnp.inf)
            m = jnp.max(s, axis=-1, keepdims=True)
            e = jnp.exp(s - m)
            den = jnp.sum(e, axis=-1)
            o = jnp.einsum('bqhj,bqjhd->bqhd', e, vg.astype(jnp.float32)) / den[..., None]
            outs.append(o)
            lses.append(m[..., 0] + jnp.log(den))
        alpha = jax.nn.softmax(jnp.stack(lses, axis=0), axis=0)
        o = alpha[0][..., None] * outs[0]
        for g in range(1, N_GROUPS):
            o = o + alpha[g][..., None] * outs[g]
        return o.astype(z_attn.dtype)

    out = lax.map(block, jnp.arange(S // Q_BLOCK))
    return out.transpose(1, 0, 2, 3, 4).reshape(B, S, ATTN_GROUP_WIDTH)

def rwkv7_time_mix(z, mu, w0, w2, a0, a2, g2, k_k, k_a, r_k, ln_w, ln_b):
    B, S, _ = z.shape
    f32 = jnp.float32
    z = z + (token_shift(z) - z) * mu
    r, k, v, xw, xa, xg = jnp.split(z, RWKV_SPLITS, axis=-1)
    logw = -jax.nn.softplus(-(w0 + jnp.tanh(xw) @ w2)) - 0.5
    decay = jnp.exp(-jnp.exp(logw.astype(f32)))
    a = jax.nn.sigmoid(a0 + xa @ a2)
    g = jax.nn.sigmoid(xg) @ g2
    heads = lambda t: t.reshape(B, S, RWKV_HEADS, HEAD_DIM).astype(f32)
    kk = heads(k * k_k)
    kk = kk / jnp.maximum(jnp.sqrt(jnp.sum(kk * kk, axis=-1, keepdims=True)), 1e-12)
    k = k * (1.0 + (a - 1.0) * k_a)
    r_h, k_h, v_h, a_h, w_h = heads(r), heads(k), heads(v), heads(a), heads(decay)
    seq = tuple(jnp.moveaxis(t, 1, 0) for t in (r_h, w_h, k_h, v_h, -kk, kk * a_h))

    def step(state, inp):
        r_t, w_t, k_t, v_t, a_t, b_t = inp
        sa = jnp.einsum('bhvk,bhk->bhv', state, a_t)
        state = (state * w_t[:, :, None, :] + sa[..., None] * b_t[:, :, None, :]
                 + v_t[..., None] * k_t[:, :, None, :])
        y = jnp.einsum('bhvk,bhk->bhv', state, r_t)
        return state, y

    state0 = jnp.zeros((B, RWKV_HEADS, HEAD_DIM, HEAD_DIM), f32)
    _, y = lax.scan(step, state0, seq)
    y = jnp.moveaxis(y, 0, 1)
    mean = jnp.mean(y, axis=-1, keepdims=True)
    var = jnp.mean(jnp.square(y - mean), axis=-1, keepdims=True)
    y = (y - mean) * lax.rsqrt(var + RWKV_GN_EPS)
    y = y.reshape(B, S, RWKV_WIDTH) * ln_w.astype(f32) + ln_b.astype(f32)
    bonus = jnp.sum(r_h * k_h * r_k.astype(f32), axis=-1, keepdims=True) * v_h
    y = (y + bonus.reshape(B, S, RWKV_WIDTH)) * g.astype(f32)
    return y.astype(z.dtype)

def first_inputs(seed: int = 0) -> dict:
    key = jax.random.key(seed)
    ks = jax.random.split(key, 32)
    f32 = jnp.float32
    nrm = lambda k, shape, scale: jax.random.normal(k, shape, f32) * scale
    gain = lambda k, n: 1.0 + 0.02 * jax.random.normal(k, (DEPTH, n), f32)
    L = DEPTH
    return {
        'x': jax.random.normal(ks[0], (BATCH, SEQ, D_MODEL), f32),
        'p': jax.random.normal(ks[1], (DEPTH, BATCH, SEQ, PLE_DIM), f32),
        'mix_pre_norm': gain(ks[2], D_MODEL),
        'w_in': nrm(ks[3], (L, D_MODEL, IN_COLS), D_MODEL ** -0.5),
        'rwkv_mu': jax.random.uniform(ks[4], (L, RWKV_COLS), f32, 0.2, 0.8),
        'rwkv_w0': jax.random.uniform(ks[5], (L, RWKV_WIDTH), f32, -4.0, 0.0),
        'rwkv_w2': nrm(ks[6], (L, DECAY_LORA, RWKV_WIDTH), 0.5 * DECAY_LORA ** -0.5),
        'rwkv_a0': nrm(ks[7], (L, RWKV_WIDTH), 0.1),
        'rwkv_a2': nrm(ks[8], (L, ICLR_LORA, RWKV_WIDTH), 0.5 * ICLR_LORA ** -0.5),
        'rwkv_g2': nrm(ks[9], (L, GATE_LORA, RWKV_WIDTH), GATE_LORA ** -0.5),
        'rwkv_k_k': 0.85 + 0.02 * jax.random.normal(ks[10], (L, RWKV_WIDTH), f32),
        'rwkv_k_a': 1.0 + 0.02 * jax.random.normal(ks[11], (L, RWKV_WIDTH), f32),
        'rwkv_r_k': nrm(ks[12], (L, RWKV_HEADS, HEAD_DIM), 0.1),
        'rwkv_ln_w': gain(ks[13], RWKV_WIDTH),
        'rwkv_ln_b': nrm(ks[14], (L, RWKV_WIDTH), 0.02),
        'w_attn_up': nrm(ks[15], (L, ATTN_GROUP_WIDTH, D_MODEL), ATTN_GROUP_WIDTH ** -0.5),
        'w_rwkv_up': nrm(ks[16], (L, RWKV_WIDTH, D_MODEL), RWKV_WIDTH ** -0.5),
        'w_out': nrm(ks[17], (L, D_MODEL, D_MODEL), D_MODEL ** -0.5),
        'mix_post_norm': gain(ks[18], D_MODEL),
        'ffn_pre_norm': gain(ks[19], D_MODEL),
        'w_ff_in': nrm(ks[20], (L, D_MODEL, D_FF), D_MODEL ** -0.5),
        'w_ff_out': nrm(ks[21], (L, D_FF, D_MODEL), D_FF ** -0.5),
        'ffn_post_norm': gain(ks[22], D_MODEL),
        'w_ple': nrm(ks[23], (L, PLE_DIM, D_MODEL), PLE_DIM ** -0.5),
        'w_ple_gate': nrm(ks[24], (L, D_MODEL, D_MODEL), D_MODEL ** -0.5),
        'ple_post_norm': gain(ks[25], D_MODEL),
    }

def first_block(x, p, mix_pre_norm, w_in, rwkv_mu, rwkv_w0, rwkv_w2, rwkv_a0, rwkv_a2, rwkv_g2,
              rwkv_k_k, rwkv_k_a, rwkv_r_k, rwkv_ln_w, rwkv_ln_b, w_attn_up, w_rwkv_up, w_out,
              mix_post_norm, ffn_pre_norm, w_ff_in, w_ff_out, ffn_post_norm, w_ple, w_ple_gate,
              ple_post_norm):
    h = x
    for i in range(DEPTH):
        u = rmsnorm(h, mix_pre_norm[i])
        z = u @ w_in[i]
        z_attn = z[..., :ATTN_QKV_COLS]
        z_rwkv = z[..., ATTN_QKV_COLS:ATTN_QKV_COLS + RWKV_COLS]
        z_gate = z[..., ATTN_QKV_COLS + RWKV_COLS:]
        o_attn = dilated_attention_branch(z_attn)
        o_rwkv = rwkv7_time_mix(z_rwkv, rwkv_mu[i], rwkv_w0[i], rwkv_w2[i], rwkv_a0[i],
                                rwkv_a2[i], rwkv_g2[i], rwkv_k_k[i], rwkv_k_a[i], rwkv_r_k[i],
                                rwkv_ln_w[i], rwkv_ln_b[i])
        gate_attn, gate_rwkv = jnp.split(jax.nn.sigmoid(z_gate), 2, axis=-1)
        merged = gate_attn * (o_attn @ w_attn_up[i]) + gate_rwkv * (o_rwkv @ w_rwkv_up[i])
        h = h + rmsnorm(merged @ w_out[i], mix_post_norm[i])
        f = rmsnorm(h, ffn_pre_norm[i])
        f = jnp.square(jax.nn.relu(f @ w_ff_in[i])) @ w_ff_out[i]
        h = h + rmsnorm(f, ffn_post_norm[i])
        e = (p[i] @ w_ple[i]) * jax.nn.sigmoid(h @ w_ple_gate[i])
        h = h + rmsnorm(e, ple_post_norm[i])
    return h


SB_HEADS = 4
DSA_HEADS = 4
NSA_HEADS = 4
BRANCH_WIDTH = 4 * HEAD_DIM
IDX_HEADS = 4
IDX_DIM = 64
DSA_TOPK = 256
CMP_LEN = 32
CMP_STRIDE = 16
CMP_HIDDEN = 128
SEL_LEN = 64
SEL_TOPN = 16
WINDOW = 512
N_MEM = 256
MEM_HEADS = 4
MEM_HEAD_DIM = 64
D_FF_2 = ((8 * D_MODEL + 3 * 256 - 1) // (3 * 256)) * 256
RMS_EPS = 1e-6
FORCED_SCORE = 1e4

IN_SPLITS = (
    ('q_a', SB_HEADS * HEAD_DIM), ('k_a', SB_HEADS * HEAD_DIM), ('v_a', SB_HEADS * HEAD_DIM),
    ('q_b', DSA_HEADS * HEAD_DIM), ('k_b', HEAD_DIM), ('v_b', HEAD_DIM),
    ('q_idx', IDX_HEADS * IDX_DIM), ('k_idx', IDX_DIM), ('w_idx', IDX_HEADS),
    ('q_c', NSA_HEADS * HEAD_DIM), ('k_cmp', HEAD_DIM), ('v_cmp', HEAD_DIM),
    ('k_sel', HEAD_DIM), ('v_sel', HEAD_DIM), ('k_win', HEAD_DIM), ('v_win', HEAD_DIM),
    ('g_c', NSA_HEADS * 3),
    ('g_merge', 3 * D_MODEL),
)
D_IN = sum(w for _, w in IN_SPLITS)


def _rmsnorm(x, g):
    xf = x.astype(jnp.float32)
    y = xf * lax.rsqrt(jnp.mean(xf * xf, axis=-1, keepdims=True) + RMS_EPS)
    return (y * g.astype(jnp.float32)).astype(x.dtype)

def _rope(x):
    S, hd = x.shape[1], x.shape[-1]
    inv = ROPE_THETA ** (-jnp.arange(0, hd, 2, dtype=jnp.float32) / hd)
    ang = jnp.arange(S, dtype=jnp.float32)[:, None] * inv[None, :]
    cos = jnp.cos(ang)[None, :, None, :]
    sin = jnp.sin(ang)[None, :, None, :]
    xf = x.astype(jnp.float32)
    x1, x2 = xf[..., : hd // 2], xf[..., hd // 2:]
    return jnp.concatenate([x1 * cos - x2 * sin, x2 * cos + x1 * sin], axis=-1).astype(x.dtype)

def _masked_softmax(s, mask):
    s = jnp.where(mask, s.astype(jnp.float32), -jnp.inf)
    m = jnp.max(s, axis=-1, keepdims=True)
    m = jnp.where(jnp.isfinite(m), m, 0.0)
    e = jnp.where(mask, jnp.exp(s - m), 0.0)
    den = jnp.sum(e, axis=-1, keepdims=True)
    return e / jnp.maximum(den, 1e-30)

def _sweep(block_fn, S):
    out = lax.map(block_fn, jnp.arange(S // Q_BLOCK))
    out = jnp.moveaxis(out, 0, 1)
    return out.reshape((out.shape[0], S) + out.shape[3:])

def _split_columns(p):
    parts, off = {}, 0
    for name, w in IN_SPLITS:
        parts[name] = p[..., off:off + w]
        off += w
    return parts

def _stick_breaking(q, k, v):
    B, S, H, hd = q.shape
    scale = hd ** -0.5
    kpos = jnp.arange(S)

    def block(i):
        q0 = i * Q_BLOCK
        qpos = q0 + jnp.arange(Q_BLOCK)
        qb = lax.dynamic_slice_in_dim(q, q0, Q_BLOCK, axis=1)
        z = jnp.einsum('bqhd,bkhd->bhqk', qb, k).astype(jnp.float32) * scale
        strict = kpos[None, :] < qpos[:, None]
        log_1m = jnp.where(strict, jax.nn.log_sigmoid(-z), 0.0)
        suffix = lax.cumsum(log_1m, axis=3, reverse=True) - log_1m
        w = jnp.where(strict, jnp.exp(jax.nn.log_sigmoid(z) + suffix), 0.0)
        return jnp.einsum('bhqk,bkhd->bqhd', w.astype(v.dtype), v)

    return _sweep(block, S)

def _dsa_attention(q, k, v, q_idx, k_idx, w_idx):
    B, S, H, hd = q.shape
    topk = min(DSA_TOPK, S // 4)
    kpos = jnp.arange(S)
    bidx = jnp.arange(B)[:, None, None]
    w_scale = (IDX_HEADS * IDX_DIM) ** -0.5
    scale = hd ** -0.5

    def block(i):
        q0 = i * Q_BLOCK
        qpos = q0 + jnp.arange(Q_BLOCK)
        qi = lax.dynamic_slice_in_dim(q_idx, q0, Q_BLOCK, axis=1)
        wi = lax.dynamic_slice_in_dim(w_idx, q0, Q_BLOCK, axis=1).astype(jnp.float32) * w_scale
        rel = jax.nn.relu(jnp.einsum('bqhd,bkd->bqhk', qi, k_idx).astype(jnp.float32))
        score = jnp.einsum('bqh,bqhk->bqk', wi, rel)
        score = jnp.where(kpos[None, None, :] <= qpos[None, :, None], score, -jnp.inf)
        _, sel = lax.top_k(score, topk)
        kg = k[bidx, sel]
        vg = v[bidx, sel]
        qb = lax.dynamic_slice_in_dim(q, q0, Q_BLOCK, axis=1)
        s = jnp.einsum('bqhd,bqkd->bhqk', qb, kg).astype(jnp.float32) * scale
        valid = (sel <= qpos[None, :, None])[:, None]
        p = _masked_softmax(s, valid)
        return jnp.einsum('bhqk,bqkd->bqhd', p.astype(v.dtype), vg)

    return _sweep(block, S)

def _compress(tok, pos_emb, w1, w2):
    B, S, hd = tok.shape
    n_cmp = (S - CMP_LEN) // CMP_STRIDE + 1
    idx = np.arange(n_cmp)[:, None] * CMP_STRIDE + np.arange(CMP_LEN)[None, :]
    blocks = tok[:, idx] + pos_emb
    hid = jax.nn.gelu(blocks.reshape(B, n_cmp, CMP_LEN * hd) @ w1)
    return hid @ w2

def _nsa_attention(q, k_cmp, v_cmp, k_sel, v_sel, k_win, v_win, gates,
                   cmp_pos_k, cmp_w1_k, cmp_w2_k, cmp_pos_v, cmp_w1_v, cmp_w2_v):
    B, S, H, hd = q.shape
    scale = hd ** -0.5
    kc = _compress(k_cmp, cmp_pos_k, cmp_w1_k, cmp_w2_k)
    vc = _compress(v_cmp, cmp_pos_v, cmp_w1_v, cmp_w2_v)
    n_cmp = kc.shape[1]
    cmp_end = jnp.arange(n_cmp) * CMP_STRIDE + CMP_LEN - 1
    n_sel = S // SEL_LEN
    topn = min(SEL_TOPN, n_sel)
    cs = np.arange(n_cmp) * CMP_STRIDE
    ss = np.arange(n_sel) * SEL_LEN
    overlap = jnp.asarray(((cs[:, None] < ss[None, :] + SEL_LEN) &
                           (cs[:, None] + CMP_LEN > ss[None, :])).astype(np.float32))
    k_blocks = k_sel.reshape(B, n_sel, SEL_LEN, hd)
    v_blocks = v_sel.reshape(B, n_sel, SEL_LEN, hd)
    k_pad = jnp.pad(k_win, ((0, 0), (WINDOW, 0), (0, 0)))
    v_pad = jnp.pad(v_win, ((0, 0), (WINDOW, 0), (0, 0)))
    sel_ids = jnp.arange(n_sel)
    offs = jnp.arange(SEL_LEN)
    band_offs = jnp.arange(WINDOW + Q_BLOCK)
    bidx = jnp.arange(B)[:, None, None]

    def block(i):
        q0 = i * Q_BLOCK
        qpos = q0 + jnp.arange(Q_BLOCK)
        qb = lax.dynamic_slice_in_dim(q, q0, Q_BLOCK, axis=1)
        gb = lax.dynamic_slice_in_dim(gates, q0, Q_BLOCK, axis=1)
        s_c = jnp.einsum('bqhd,bnd->bhqn', qb, kc).astype(jnp.float32) * scale
        p_c = _masked_softmax(s_c, (cmp_end[None, :] <= qpos[:, None])[None, None])
        o_cmp = jnp.einsum('bhqn,bnd->bqhd', p_c.astype(vc.dtype), vc)
        imp = jnp.einsum('bhqn,nj->bqj', p_c, overlap)
        cur = qpos // SEL_LEN
        forced = ((sel_ids[None, :] == 0) | (sel_ids[None, :] == cur[:, None]) |
                  (sel_ids[None, :] == cur[:, None] - 1))
        admissible = sel_ids[None, :] * SEL_LEN <= qpos[:, None]
        imp = jnp.where(forced[None], FORCED_SCORE, imp)
        imp = jnp.where(admissible[None], imp, -jnp.inf)
        _, sel = lax.top_k(imp, topn)
        kg = k_blocks[bidx, sel].reshape(B, Q_BLOCK, topn * SEL_LEN, hd)
        vg = v_blocks[bidx, sel].reshape(B, Q_BLOCK, topn * SEL_LEN, hd)
        tok = (sel[..., None] * SEL_LEN + offs).reshape(B, Q_BLOCK, topn * SEL_LEN)
        s_s = jnp.einsum('bqhd,bqkd->bhqk', qb, kg).astype(jnp.float32) * scale
        p_s = _masked_softmax(s_s, (tok <= qpos[None, :, None])[:, None])
        o_sel = jnp.einsum('bhqk,bqkd->bqhd', p_s.astype(vg.dtype), vg)
        kw = lax.dynamic_slice_in_dim(k_pad, q0, WINDOW + Q_BLOCK, axis=1)
        vw = lax.dynamic_slice_in_dim(v_pad, q0, WINDOW + Q_BLOCK, axis=1)
        wpos = q0 - WINDOW + band_offs
        diff = qpos[:, None] - wpos[None, :]
        wmask = (diff >= 0) & (diff < WINDOW) & (wpos[None, :] >= 0)
        s_w = jnp.einsum('bqhd,bkd->bhqk', qb, kw).astype(jnp.float32) * scale
        p_w = _masked_softmax(s_w, wmask[None, None])
        o_win = jnp.einsum('bhqk,bkd->bqhd', p_w.astype(vw.dtype), vw)
        return gb[..., 0:1] * o_cmp + gb[..., 1:2] * o_sel + gb[..., 2:3] * o_win

    return _sweep(block, S)

def _hybrid_mixer(u, w_in, cmp_pos_k, cmp_w1_k, cmp_w2_k, cmp_pos_v, cmp_w1_v, cmp_w2_v, w_up, w_out):
    B, S, _ = u.shape
    p = _split_columns(u @ w_in)

    def heads(t, h, d=HEAD_DIM):
        return t.reshape(B, S, h, d)

    def rope1(t):
        return _rope(t[:, :, None, :])[:, :, 0]

    o_a = _stick_breaking(heads(p['q_a'], SB_HEADS), heads(p['k_a'], SB_HEADS), heads(p['v_a'], SB_HEADS))
    o_b = _dsa_attention(_rope(heads(p['q_b'], DSA_HEADS)), rope1(p['k_b']), p['v_b'],
                         _rope(heads(p['q_idx'], IDX_HEADS, IDX_DIM)), rope1(p['k_idx']), p['w_idx'])
    gates_c = jax.nn.sigmoid(p['g_c'].reshape(B, S, NSA_HEADS, 3))
    o_c = _nsa_attention(_rope(heads(p['q_c'], NSA_HEADS)), rope1(p['k_cmp']), p['v_cmp'],
                         rope1(p['k_sel']), p['v_sel'], rope1(p['k_win']), p['v_win'], gates_c,
                         cmp_pos_k, cmp_w1_k, cmp_w2_k, cmp_pos_v, cmp_w1_v, cmp_w2_v)
    g = jax.nn.sigmoid(p['g_merge'].reshape(B, S, 3, D_MODEL))
    merged = (g[:, :, 0] * (o_a.reshape(B, S, BRANCH_WIDTH) @ w_up[0]) +
              g[:, :, 1] * (o_b.reshape(B, S, BRANCH_WIDTH) @ w_up[1]) +
              g[:, :, 2] * (o_c.reshape(B, S, BRANCH_WIDTH) @ w_up[2]))
    return merged @ w_out

def _memory_attention(h, mem, g_q, g_kv, w_q, w_kv, w_o):
    B, S, _ = h.shape
    M = mem.shape[1]
    q = (_rmsnorm(h, g_q) @ w_q).reshape(B, S, MEM_HEADS, MEM_HEAD_DIM)
    kv = (_rmsnorm(mem, g_kv) @ w_kv).reshape(B, M, 2, MEM_HEADS, MEM_HEAD_DIM)
    s = jnp.einsum('bshd,bmhd->bhsm', q, kv[:, :, 0]).astype(jnp.float32) * MEM_HEAD_DIM ** -0.5
    pr = jax.nn.softmax(s, axis=-1)
    o = jnp.einsum('bhsm,bmhd->bshd', pr.astype(h.dtype), kv[:, :, 1])
    return o.reshape(B, S, MEM_HEADS * MEM_HEAD_DIM) @ w_o

def _swiglu(u, w_in, w_out):
    a = u @ w_in
    return (jax.nn.silu(a[..., :D_FF_2]) * a[..., D_FF_2:]) @ w_out

def second_inputs(seed: int = 0) -> dict:
    key = jax.random.key(seed)
    ks = jax.random.split(key, 21)

    def nrm(k, shape, fan_in):
        return jax.random.normal(k, shape, jnp.float32) * fan_in ** -0.5

    def gain(k, shape):
        return 1.0 + 0.05 * jax.random.normal(k, shape, jnp.float32)

    L = DEPTH
    mem_w = MEM_HEADS * MEM_HEAD_DIM
    return {
        'x': jax.random.normal(ks[0], (BATCH, SEQ, D_MODEL), jnp.float32),
        'mem': jax.random.normal(ks[1], (BATCH, N_MEM, D_MODEL), jnp.float32),
        'norm_mix': gain(ks[2], (L, D_MODEL)),
        'w_in': nrm(ks[3], (L, D_MODEL, D_IN), D_MODEL),
        'cmp_pos_k': 0.1 * jax.random.normal(ks[4], (L, CMP_LEN, HEAD_DIM), jnp.float32),
        'cmp_w1_k': nrm(ks[5], (L, CMP_LEN * HEAD_DIM, CMP_HIDDEN), CMP_LEN * HEAD_DIM),
        'cmp_w2_k': nrm(ks[6], (L, CMP_HIDDEN, HEAD_DIM), CMP_HIDDEN),
        'cmp_pos_v': 0.1 * jax.random.normal(ks[7], (L, CMP_LEN, HEAD_DIM), jnp.float32),
        'cmp_w1_v': nrm(ks[8], (L, CMP_LEN * HEAD_DIM, CMP_HIDDEN), CMP_LEN * HEAD_DIM),
        'cmp_w2_v': nrm(ks[9], (L, CMP_HIDDEN, HEAD_DIM), CMP_HIDDEN),
        'w_up': nrm(ks[10], (L, 3, BRANCH_WIDTH, D_MODEL), BRANCH_WIDTH),
        'w_out': nrm(ks[11], (L, D_MODEL, D_MODEL), D_MODEL),
        'norm_mem_q': gain(ks[12], (L, D_MODEL)),
        'norm_mem_kv': gain(ks[13], (L, D_MODEL)),
        'w_mem_q': nrm(ks[14], (L, D_MODEL, mem_w), D_MODEL),
        'w_mem_kv': nrm(ks[15], (L, D_MODEL, 2 * mem_w), D_MODEL),
        'w_mem_o': nrm(ks[16], (L, mem_w, D_MODEL), mem_w),
        'norm_ffn': gain(ks[17], (L, D_MODEL)),
        'w_ffn_in': nrm(ks[18], (L, D_MODEL, 2 * D_FF_2), D_MODEL),
        'w_ffn_out': nrm(ks[19], (L, D_FF_2, D_MODEL), D_FF_2),
        'norm_final': gain(ks[20], (D_MODEL,)),
    }

def second_block(x, mem, norm_mix, w_in, cmp_pos_k, cmp_w1_k, cmp_w2_k, cmp_pos_v, cmp_w1_v, cmp_w2_v,
              w_up, w_out, norm_mem_q, norm_mem_kv, w_mem_q, w_mem_kv, w_mem_o,
              norm_ffn, w_ffn_in, w_ffn_out, norm_final):
    h = x
    for l in range(DEPTH):
        h = h + _hybrid_mixer(_rmsnorm(h, norm_mix[l]), w_in[l],
                              cmp_pos_k[l], cmp_w1_k[l], cmp_w2_k[l],
                              cmp_pos_v[l], cmp_w1_v[l], cmp_w2_v[l], w_up[l], w_out[l])
        h = h + _memory_attention(h, mem, norm_mem_q[l], norm_mem_kv[l], w_mem_q[l], w_mem_kv[l], w_mem_o[l])
        h = h + _swiglu(_rmsnorm(h, norm_ffn[l]), w_ffn_in[l], w_ffn_out[l])
    return _rmsnorm(h, norm_final)


def setup_inputs(seed=0):
    out = dict(first_inputs(seed))
    for name, value in second_inputs(seed + 1).items():
        if name != "x":
            out[name + "_2"] = value
    return out


def reference(
    x, p, mix_pre_norm, w_in, rwkv_mu, rwkv_w0, rwkv_w2, rwkv_a0, rwkv_a2, rwkv_g2, rwkv_k_k,
    rwkv_k_a, rwkv_r_k, rwkv_ln_w, rwkv_ln_b, w_attn_up, w_rwkv_up, w_out, mix_post_norm,
    ffn_pre_norm, w_ff_in, w_ff_out, ffn_post_norm, w_ple, w_ple_gate, ple_post_norm, mem_2,
    norm_mix_2, w_in_2, cmp_pos_k_2, cmp_w1_k_2, cmp_w2_k_2, cmp_pos_v_2, cmp_w1_v_2,
    cmp_w2_v_2, w_up_2, w_out_2, norm_mem_q_2, norm_mem_kv_2, w_mem_q_2, w_mem_kv_2, w_mem_o_2,
    norm_ffn_2, w_ffn_in_2, w_ffn_out_2, norm_final_2,
):
    x = first_block(
        x, p, mix_pre_norm, w_in, rwkv_mu, rwkv_w0, rwkv_w2, rwkv_a0, rwkv_a2, rwkv_g2,
        rwkv_k_k, rwkv_k_a, rwkv_r_k, rwkv_ln_w, rwkv_ln_b, w_attn_up, w_rwkv_up, w_out,
        mix_post_norm, ffn_pre_norm, w_ff_in, w_ff_out, ffn_post_norm, w_ple, w_ple_gate,
        ple_post_norm,
    )
    return second_block(
        x, mem_2, norm_mix_2, w_in_2, cmp_pos_k_2, cmp_w1_k_2, cmp_w2_k_2, cmp_pos_v_2,
        cmp_w1_v_2, cmp_w2_v_2, w_up_2, w_out_2, norm_mem_q_2, norm_mem_kv_2, w_mem_q_2,
        w_mem_kv_2, w_mem_o_2, norm_ffn_2, w_ffn_in_2, w_ffn_out_2, norm_final_2,
    )


_drawn_inputs = setup_inputs


def setup_inputs(seed=0):
    import zlib

    import numpy as np

    out = dict(_drawn_inputs(seed))
    spreads = {}
    factors = {'rwkv_k_k': 6.16,
     'rwkv_k_a': 3.393,
     'rwkv_ln_w': 3.925,
     'rwkv_ln_b': 4.059,
     'mix_post_norm': 3.843,
     'ffn_pre_norm': 4.05,
     'ffn_post_norm': 4.598,
     'ple_post_norm': 4.829,
     'norm_mix_2': 3.307,
     'cmp_pos_k_2': 8.0,
     'cmp_w1_k_2': 3.588,
     'cmp_w2_k_2': 3.198,
     'cmp_pos_v_2': 6.583,
     'norm_mem_q_2': 8.0,
     'norm_mem_kv_2': 8.0,
     'norm_ffn_2': 2.813}
    for name, (base, spread) in spreads.items():
        noise = np.random.default_rng([zlib.crc32(name.encode()), seed]).standard_normal(out[name].shape)
        drawn = base * np.exp(spread * noise) if base else spread * noise
        out[name] = __import__('jax').numpy.asarray(drawn.astype(out[name].dtype))
    for name, factor in factors.items():
        out[name] = (out[name] * factor).astype(out[name].dtype)
    return out
```

```python
from contextlib import ExitStack
import math

import numpy as np
import concourse.bass as bass
from concourse import mybir

F32 = mybir.dt.float32
ALU = mybir.AluOpType
ACT = mybir.ActivationFunctionType
AX = mybir.AxisListType.X

NEG = -1e30
TAKEN = -3e38
EPS = 1e-6
GN_EPS = 64e-5
S0 = math.exp(-0.5)

C_ID, C_SU, C_IU, C_LI, C_ONE, C_BLK, C_ROT, C_M0, C_M0T = [128 * i for i in range(9)]
C_LV = 128 * 9
C_MA = C_LV + 768
C_CA = C_MA + 768
C_ST = C_CA + 256
C_CMA = C_ST + 384
C_CMM = C_CMA + 30
C_COS = C_CMM + 30
C_SIN = C_COS + 256
C_COSC = C_SIN + 256
C_SINC = C_COSC + 256
C_END = C_SINC + 256

VEC = [("mix_pre_norm", 8), ("rwkv_mu", 14), ("rwkv_w0", 4), ("rwkv_a0", 4), ("rwkv_k_k", 4), ("rwkv_k_a", 4),
       ("rwkv_r_k", 4), ("rwkv_ln_w", 4), ("rwkv_ln_b", 4), ("ffn_pre_norm", 8), ("norm_mix_2", 8),
       ("norm_mem_q_2", 8), ("norm_mem_kv_2", 8), ("norm_ffn_2", 8), ("pos", 32)]
VOFF = {}
for _name, _n in VEC:
    VOFF[_name] = sum(n for m, n in VEC[:len(VOFF)])


def shape_constants():
    c = np.zeros((128, C_END), np.float32)
    i = np.arange(128)
    r, s = i[:, None], i[None, :]
    c[:, C_ID:C_ID + 128] = r == s
    c[:, C_SU:C_SU + 128] = r < s
    c[:, C_IU:C_IU + 128] = r <= s
    c[:, C_LI:C_LI + 128] = r >= s
    c[:, C_ONE:C_ONE + 128] = 1
    c[:, C_BLK:C_BLK + 128] = r // 64 == s // 64
    same = r // 64 == s // 64
    c[:, C_ROT:C_ROT + 128] = (same & (r % 64 < 32) & (s % 64 == r % 64 + 32)) * 1.0 \
        - (same & (r % 64 >= 32) & (s % 64 == r % 64 - 32)) * 1.0
    for n in range(7):
        b = 1 << n
        m = (r // (2 * b) == s // (2 * b)) & (r // b % 2 == 1) & (s // b % 2 == 0)
        if n == 0:
            c[:, C_M0:C_M0 + 128] = m
            c[:, C_M0T:C_M0T + 128] = m.T
        else:
            c[:, C_LV + 128 * (n - 1):C_LV + 128 * n] = m | (r == s)
    for n, keep in enumerate([s >= r, s <= r, (r - s) % 4 == 0, ((r - s) % 4 == 0) & (s <= r),
                              (r - s) % 16 == 0, ((r - s) % 16 == 0) & (s <= r)]):
        c[:, C_MA + 128 * n:C_MA + 128 * (n + 1)] = np.where(keep, 0, NEG)
    c[:, C_CA + 128:C_CA + 256] = np.where(s <= r, 0, NEG)
    c[:, C_ST:C_ST + 128] = np.where(r < s, 0, NEG)
    c[:, C_ST + 256:C_ST + 384] = np.where(r < s, 0, NEG)
    n = np.arange(15)[None, :] * 16 + 31
    for t in range(2):
        keep = n <= r + 128 * t
        c[:, C_CMA + 15 * t:C_CMA + 15 * (t + 1)] = np.where(keep, 0, NEG)
        c[:, C_CMM + 15 * t:C_CMM + 15 * (t + 1)] = keep
    inv = np.float32(10000.0) ** (-np.arange(0, 64, 2, dtype=np.float32) / np.float32(64))
    ang = (np.arange(256, dtype=np.float32)[None, :] * inv[:, None]).astype(np.float32)
    cos, sin = np.cos(ang), np.sin(ang)
    c[:, C_COS:C_COS + 256] = np.tile(cos, (4, 1))
    c[:, C_SIN:C_SIN + 256] = np.tile(sin, (4, 1))
    c[0:64, C_COSC:C_COSC + 256] = np.tile(cos, (2, 1))
    c[64:128, C_COSC:C_COSC + 256] = 1
    c[0:64, C_SINC:C_SINC + 256] = np.tile(sin, (2, 1))
    return c


class Engine:

    def __init__(self, sem):
        self.sem, self.n, self.todo, self.seen = sem, 0, [], {}

    def wait(self, toks):
        for t in toks:
            if t is None or len(t) == 0:
                continue
            if isinstance(t, list) or not isinstance(t[0], str):
                self.wait(t)
            elif self.seen.get(t[0], 0) < t[2]:
                self.seen[t[0]] = t[2]
                self.todo.append(lambda e, t=t: e.wait_ge(t[1], t[2]))

    def __call__(self, fn, toks, signal=True):
        self.wait(toks)
        if signal:
            self.n += 1
            self.todo.append(lambda e: fn(e).then_inc(self.sem[1], 1))
            return (self.sem[0], self.sem[1], self.n)
        self.todo.append(fn)
        return None

    def run(self, e):
        for f in self.todo:
            f(e)


class Banks:

    def __init__(self, banks):
        self.free = [(b, None) for b in banks]

    def get(self):
        return self.free.pop(0)

    def put(self, bank, *toks):
        self.free.append((bank, list(toks)))


def program(nc, A, consts, out):
    with ExitStack() as ctx:
        def sem(name):
            return (name, ctx.enter_context(nc.semaphore(name)))

        PSUM = ctx.enter_context(nc.psum_tensor("psum", [128, 8, 512], F32))
        NARENA = 52700
        arena = ctx.enter_context(nc.sbuf_tensor("arena", [128, NARENA], F32))

        PE, V, S, G = [Engine(sem(n)) for n in ("s_pe", "s_dve", "s_act", "s_pool")]
        SP = Engine(None)

        def view(off, n):
            return arena[:, off:off + n]

        def view3(off, a, b):
            return arena[:, off:off + a * b].rearrange("p (a b) -> p a b", a=a)

        def bc(ap, n):
            return ap.unsqueeze(2).broadcast_to([ap.shape[0], ap.shape[1], n])

        def rep(ap, n):
            return ap.unsqueeze(1).broadcast_to([ap.shape[0], n, ap.shape[1]])

        def tt(E, o, a, b, op, *toks):
            return E(lambda e: e.tensor_tensor(o, a, b, op), toks)

        def ts(E, o, a, s1, s2, op0, op1, *toks):
            if op1 is None:
                return E(lambda e: e.tensor_scalar(o, a, s1, None, op0), toks)
            return E(lambda e: e.tensor_scalar(o, a, s1, s2, op0, op1), toks)

        def stt(o, a, s, b, op0, op1, *toks):
            return V(lambda e: e.scalar_tensor_tensor(out=o, in0=a, scalar=s, in1=b, op0=op0, op1=op1), toks)

        def cp(E, o, a, *toks):
            if E is S:
                return S(lambda e: e.activation(o, a, ACT.Copy), toks)
            return E(lambda e: e.tensor_copy(o, a), toks)

        def act(o, a, f, *toks, bias=0.0, scale=1.0, accum=None):
            if accum is None:
                return S(lambda e: e.activation(o, a, f, bias=bias, scale=scale), toks)
            return S(lambda e: e.activation(o, a, f, bias=bias, scale=scale, accum_out=accum), toks)

        def red(o, a, op, *toks):
            return V(lambda e: e.tensor_reduce(o, a, AX, op), toks)

        def recip(o, a, *toks):
            return V(lambda e: e.reciprocal(o, a), toks)

        def mset(E, o, v, *toks):
            return E(lambda e: e.memset(o, v), toks)

        def mm(o, l, r, start, stop, *toks, sig=False):
            return PE(lambda e: e.matmul(o, l, r, start=start, stop=stop), toks, signal=sig)

        def tr(o, a, *toks, sig=False):
            n = a.shape[0]
            b = a.base_partition()
            idn = arena[b:b + n, OC + C_ID + b:OC + C_ID + b + n]
            return PE(lambda e: e.transpose(o, a, idn), toks, signal=sig)

        dma_count = {}

        def dma(E, o, a, sm, *toks):
            E.wait(toks)
            dma_count[sm[0]] = dma_count.get(sm[0], 0) + 16
            E.todo.append(lambda e: e.dma_start(o, a).then_inc(sm[1], 16))
            return (sm[0], sm[1], dma_count[sm[0]])

        NR = 7
        OR, OC = 0, NR * 2048
        OV = OC + C_END
        OS = OV + 128
        OU = OS + 512
        P = OU + 2048
        small_at = [OS]
        assert P + 30720 <= NARENA - 512, (P, NARENA)

        def small(n):
            o = small_at[0]
            small_at[0] += n
            assert small_at[0] <= OU, "small"
            return arena[:, o:o + n]

        uT = view3(OU, 8, 256)
        ident = view(OC + C_ID, 128)

        def const(off, n):
            return arena[:, OC + off:OC + off + n]

        def vec(name, i, n=1, p=128):
            o = OV + VOFF[name] + i
            return arena[0:p, o:o + n]

        ring_sem = [sem(f"s_w{i}") for i in range(NR)]
        ring_free = [None] * NR
        ring_at = [0]

        def wload(pieces):
            n = ring_at[0] % NR
            ring_at[0] += 1
            slot = view(OR + 2048 * n, 2048)
            tok = None
            for put, src in pieces:
                tok = dma(SP, put(slot), src, ring_sem[n], ring_free[n])
            ring_free[n] = [(None,)]
            return n, slot, tok

        def wfree(n, *toks):
            ring_free[n] = list(toks)

        def wcols(W, c0, w, k0, nk, d0, width):
            src = W[128 * k0:128 * (k0 + nk), c0:c0 + w].rearrange("(k p) n -> p k n", p=128)
            return (lambda s: s[:, 0:nk * width].rearrange("p (k n) -> p k n", k=nk)[:, :, d0:d0 + w], src)

        PG = Banks([PSUM[:, i, :] for i in (0, 1)])
        PA = Banks([PSUM[:, i, :] for i in (2, 3, 4)])
        PB = Banks([PSUM[:, i, :] for i in (5, 6, 7)])

        def halves(bank):
            return bank.rearrange("p (a b) -> p a b", a=2)

        def quarters(bank):
            return bank.rearrange("p (a b) -> p a b", a=4)

        def gemm_f(W, plan, K, evac, rhs, dep, pool=None, grain=1):
            pool = pool or PG
            for n, (pieces, widths) in enumerate(plan):
                wn, slot, wt = wload([wcols(W, c0, w, 0, K, d0, 256) for c0, w, d0 in pieces])
                w3 = slot[:, 0:K * 256].rearrange("p (k n) -> p k n", k=K)
                bank, bt = pool.get()
                off = 0
                for j, m in enumerate(widths):
                    for k in range(K):
                        t = mm(bank[0:m, 256 * j:256 * j + 256], w3[:, k, off:off + m], rhs[:, k, :], k == 0, k == K - 1,
                               dep, wt, bt, sig=(k == K - 1))
                    off += 128 if m == 128 else m
                    if j + 1 < len(widths):
                        yield
                wfree(wn, t)
                pool.put(bank, *evac(bank, n, t))
                yield

        def gemm_t(slots, lhs, dep, banks, w, K):
            k = 0
            for pieces, nk in slots:
                wn, slot, wt = wload(pieces)
                w3 = slot[:, 0:nk * w].rearrange("p (k n) -> p k n", k=nk)
                for kk in range(nk):
                    for i in range(2):
                        b, bt = banks[i]
                        t = mm(b[:, 0:w], lhs[:, k, 128 * i:128 * i + 128], w3[:, kk, :], k == 0, k == K - 1,
                               dep, wt, bt, sig=(kk == nk - 1 and i == 1))
                    k += 1
                    if kk % 2 == 1:
                        yield
                wfree(wn, t)
            return t

        def rstd(ss, o, n, eps, *toks):
            t = ts(V, o, ss, 1.0 / n, eps, ALU.mult, ALU.add, *toks)
            return tt(G, o, o, mh.broadcast_to([128, o.shape[1]]), ALU.pow, t)

        def norm_t(src, xn, gname, dst, toks, gain=True):
            ss, rs = small(2), small(2)
            last = []
            for i in range(2):
                if gain:
                    t = act(xn[:, i, :], src[:, i, :], ACT.Square, toks[i], accum=ss[:, i:i + 1])
                    t = rstd(ss[:, i:i + 1], rs[:, i:i + 1], 1024, EPS, t)
                    t = ts(V, xn[:, i, :], src[:, i, :], rs[:, i:i + 1], None, ALU.mult, None, t)
                    x = xn
                else:
                    t, x = toks[i], src
                for b in range(2):
                    bank, bt = PB.get()
                    for c in range(4):
                        tp = tr(bank[:, 128 * c:128 * c + 128], x[:, i, 512 * b + 128 * c:512 * b + 128 * c + 128],
                                t, bt, sig=(c == 3))
                    o = dst[:, 4 * b:4 * b + 4, 128 * i:128 * i + 128]
                    if gain:
                        te = tt(V, o, quarters(bank), bc(vec(gname, 4 * b, 4), 128), ALU.mult, tp)
                    else:
                        te = cp(S, o, quarters(bank), tp)
                    PB.put(bank, te)
                    last.append(te)
                    yield
            return last

        def post_norm(y, gname, h, hsrc, toks, htoks, tmp):
            wn, slot, wt = wload([(lambda s: s[:, 0:1024], A[gname].rearrange("a n -> (a n)").partition_broadcast(128))])
            ss, rs = small(4), small(2)
            done, read = [], []
            for i in range(2):
                for n in range(2):
                    t = act(tmp[:, i, 512 * n:512 * n + 512], y[i][n], ACT.Square, toks[i][n],
                            accum=ss[:, 2 * i + n:2 * i + n + 1])
                t = tt(V, rs[:, i:i + 1], ss[:, 2 * i:2 * i + 1], ss[:, 2 * i + 1:2 * i + 2], ALU.add, t)
                t = rstd(rs[:, i:i + 1], rs[:, i:i + 1], 1024, EPS, t)
                r = []
                for n in range(2):
                    c = slice(512 * n, 512 * n + 512)
                    t2 = stt(tmp[:, i, c], y[i][n], rs[:, i:i + 1], slot[:, c], ALU.mult, ALU.mult, t, wt)
                    r.append(t2)
                    t3 = tt(G, h[:, i, c], hsrc[:, i, c], tmp[:, i, c], ALU.add, t2, htoks)
                done.append(t3)
                read.append(r)
                yield
            wfree(wn, t2)
            return done, read

        def rope(bank, n, tok, dst, cos, sin, zs, t1, prev):
            t_z = cp(S, zs, halves(bank)[:, 0:n, :], tok, prev)
            t_c = tt(G, t1, zs, rep(cos, n), ALU.mult, t_z, prev)
            b2, bt = PB.get()
            t_r = mm(b2[:, 0:256 * n], const(C_ROT, 128), zs, True, True, t_z, bt, sig=True)
            t_s = tt(V, dst, halves(b2)[:, 0:n, :], rep(sin, n), ALU.mult, t_r)
            PB.put(b2, t_s)
            t_d = tt(G, dst, dst, t1, ALU.add, t_s, t_c)
            return [t_z], t_d

        def drive(main, *sides):
            live = [main, *sides]
            while live:
                for g in list(live):
                    try:
                        next(g)
                    except StopIteration:
                        live.remove(g)

        def alone(g):
            while True:
                try:
                    next(g)
                except StopIteration as e:
                    return e.value

        s_i, s_c, s_x, s_v = sem("s_i"), sem("s_c"), sem("s_x"), sem("s_v")
        mh = small(1)
        t_mh = mset(G, mh, -0.5)
        x_sb = view3(P + 24576, 2, 1024)
        xn = view3(P + 26624, 2, 1024)
        x_d = A["x"][0].rearrange("(i p) d -> p i d", p=128)
        t_x = [dma(SP, x_sb[:, i, :], x_d[:, i, :], s_x) for i in range(2)]
        t_x = [t_x[1], t_x[1]]
        t_id = dma(S, const(0, 128), consts[:, 0:128], s_i)
        vrow = view(P, 128)
        t0 = mset(G, vrow, 0.0)
        for name, n in VEC[:-1]:
            o = VOFF[name]
            src = A[name]
            if name == "rwkv_mu":
                dma(S, vrow[o:o + 12, :], src[0, 0:1536].rearrange("(c p) -> c p", p=128), s_v, t0)
                dma(S, vrow[o + 12:o + 13, 0:64], src[0:1, 1536:1600], s_v)
                dma(S, vrow[o + 13:o + 14, 0:96], src[0:1, 1600:1696], s_v)
                continue
            flat = src.rearrange("a h d -> (a h d)") if name == "rwkv_r_k" else src.rearrange("a n -> (a n)")
            dma(S, vrow[o:o + n, :], flat.rearrange("(c p) -> c p", p=128), s_v, t0)
        o = VOFF["pos"]
        dma(S, vrow[o:o + 32, 0:64], A["cmp_pos_k_2"][0], s_v)
        t_vr = dma(S, vrow[o:o + 32, 64:128], A["cmp_pos_v_2"][0], s_v)
        t_c = dma(S, const(128, C_END - 128), consts[:, 128:C_END], s_c)
        bank, bt = PB.get()
        tp = tr(bank[:, 0:128], vrow, t_vr, t_id, sig=True)
        t_v = cp(V, view(OV, 128), bank[:, 0:128], tp)
        PB.put(bank, t_v)
        PE.wait([t_c])
        V.wait([t_c])
        S.wait([t_v])
        G.wait([t_c, t_v])
        omka = small(4)
        G.wait([t_mh])
        t_omka = ts(V, omka, vec("rwkv_k_a", 0, 4), -1.0, 1.0, ALU.mult, ALU.add, t_v)

        t_u = alone(norm_t(x_sb, xn, "mix_pre_norm", uT, t_x))

        R = P + 11776
        zm = view3(R, 14, 256)
        oE, oCS, oCSC, oQ, oQi, oQx, oA, oKK, oKM, oAR, oG, oBON, oVT, oBK = [
            P + 15360 + 1024 * i for i in range(10)] + [P + 26624, P + 27648, P + 28672, P + 29696]
        ZS = [view3(oQ + 514 * i, 2, 257) for i in range(2)]
        D = [view3(oQ + 1028 + 512 * i, 2, 256) for i in range(2)]
        t_zs0 = [mset(G, z[:, :, 0:1], 0.0) for z in ZS]
        w_in = A["w_in"][0]
        zprev = [None, None]
        t_zm = {}

        def evac_rwkv(bank, n, tok):
            b = n % 2
            z, d = ZS[b], D[b]
            if n < 6:
                ps = [(128, 0, 2)]
            else:
                ps = [(64, 0, 1), (96, 1, 1)]
            frees, last = [], None
            for p, j, m in ps:
                t1 = cp(S, z[0:p, j:j + m, 1:257], halves(bank)[0:p, j:j + m, :], tok, zprev[b], t_zs0)
                frees.append(t1)
                t2 = tt(G, d[0:p, j:j + m, :], z[0:p, j:j + m, 0:256], z[0:p, j:j + m, 1:257], ALU.subtract, t1, zprev[b])
                for q in range(m):
                    c = 2 * n + j + q
                    last = stt(zm[0:p, c, :], d[0:p, j + q, :], vec("rwkv_mu", c, 1, p), z[0:p, j + q, 1:257],
                               ALU.mult, ALU.add, t2)
                    t_zm[c] = last
            zprev[b] = last
            return frees

        B0 = 2304
        plan = [([(B0 + 256 * n, 256, 0)], [128, 128]) for n in range(6)]
        plan = plan[2:4] + plan[0:2] + plan[4:6]
        order = [2, 3, 0, 1, 4, 5]
        plan = [([(B0 + 1536, 160, 0)], [64, 96])] + plan
        order = [6] + order
        alone(gemm_f(w_in, plan, 8, lambda b, n, t: evac_rwkv(b, order[n], t), uT, t_u))

        lo_n, lo, t_lo = wload([
            (lambda s: s[0:32, 0:512], A["rwkv_w2"][0]), (lambda s: s[32:64, 0:512], A["rwkv_a2"][0]),
            (lambda s: s[0:96, 512:1024], A["rwkv_g2"][0])])

        o_attn = view3(NARENA - 512, 2, 256)
        o_rwkv = view3(P + 13824, 4, 256)

        E4, CS, CSC, Q4, Qi, Qx, A4, KK, KM = [view(o, 1024) for o in (oE, oCS, oCSC, oQ, oQi, oQx, oA, oKK, oKM)]
        G4, BON = view(oG, 1024), view(oBON, 1024)
        TMP = view(oBK, 1024)

        def v4(x):
            return x.rearrange("p (c t) -> p c t", c=4)

        def v42(x):
            return x.rearrange("p (c i t) -> p c i t", c=4, i=2)

        def v8(x):
            return x.rearrange("p (c t) -> p c t", c=8)

        AR = arena[:, oAR:oAR + 2048].rearrange("p (c i w t) -> p c i w t", c=4, i=2, w=2)
        VT = view3(oVT, 2, 512)
        BK = view3(oBK, 2, 512)
        zr, zk, zv = zm[:, 0:4, :], zm[:, 4:8, :], zm[:, 8:12, :]
        zk_f = view(R + 1024, 1024)
        zv_f = view(R + 2048, 1024)

        def chunk_pairs(mk, ev, pool, *toks):
            for b in range(2):
                bank, bt = pool.get()
                for j in range(2):
                    t = mk(bank[:, 256 * j:256 * j + 256], 2 * b + j, bt, toks, j == 1)
                pool.put(bank, *ev(bank, b, t))
                yield

        rw = {}

        def rwkv_side():
            t_th = act(zm[0:32, 12, :], zm[0:32, 12, :], ACT.Tanh, t_zm[12])
            t_sg = act(zm[0:96, 13, :], zm[0:96, 13, :], ACT.Sigmoid, t_zm[13])
            onez = view(oVT, 1024)
            t_one = mset(G, onez, 1.0)
            t_one = mset(G, onez.rearrange("p (c t) -> p c t", c=8)[:, :, 0:1], 0.0, t_one)
            yield
            te = []

            def ev_w(bank, b, t):
                for j in range(2):
                    te.append(act(E4[:, 512 * b + 256 * j:512 * b + 256 * j + 256], bank[:, 256 * j:256 * j + 256],
                                  ACT.Sigmoid, t, bias=vec("rwkv_w0", 2 * b + j)))
                return [te[-1]]

            yield from chunk_pairs(lambda o, c, bt, tk, sg: mm(o, lo[0:32, 128 * c:128 * c + 128], zm[0:32, 12, :], True, True,
                                                               bt, tk, sig=sg), ev_w, PB, t_th, t_lo)
            ta = []

            def ev_a(bank, b, t):
                for j in range(2):
                    ta.append(act(A4[:, 512 * b + 256 * j:512 * b + 256 * j + 256], bank[:, 256 * j:256 * j + 256],
                                  ACT.Sigmoid, t, bias=vec("rwkv_a0", 2 * b + j)))
                return [ta[-1]]

            yield from chunk_pairs(lambda o, c, bt, tk, sg: mm(o, lo[32:64, 128 * c:128 * c + 128], zm[32:64, 12, :], True, True,
                                                               bt, tk, sig=sg), ev_a, PB, t_zm[12], t_lo)
            tg = []

            def ev_g(bank, b, t):
                tg.append(cp(S, G4[:, 512 * b:512 * b + 512], bank, t))
                return [tg[-1]]

            yield from chunk_pairs(lambda o, c, bt, tk, sg: mm(o, lo[0:96, 512 + 128 * c:512 + 128 * c + 128], zm[0:96, 13, :],
                                                               True, True, bt, tk, sig=sg), ev_g, PB, t_sg, t_lo)
            wfree(lo_n, (PE.sem[0], PE.sem[1], PE.n))
            t_cs = V(lambda e: e.tensor_tensor_scan(CS, onez, E4, 0.0, ALU.mult, ALU.add), [te, t_one])
            mid = v8(CS)[:, :, 63:64].broadcast_to([128, 8, 128])
            t_cc = tt(V, v8(CSC), v8(CS), mid, ALU.subtract, t_cs)
            fct = small(4)
            t_f = tt(V, fct.unsqueeze(2), v42(CSC)[:, :, 0, 127:128], v42(CS)[:, :, 1, 63:64], ALU.add, t_cc)
            t_qx = tt(G, Qx, CSC, E4, ALU.subtract, t_cc)
            t_q = act(Q4, CSC, ACT.Exp, t_cc, scale=-S0)
            t_qi = act(Qi, CSC, ACT.Exp, t_cc, scale=S0)
            t_qx = act(Qx, Qx, ACT.Exp, t_qx, scale=-S0)
            t_f = act(fct, fct, ACT.Exp, t_f, scale=-S0)
            zks = [t_zm[c] for c in range(12)]
            t_kk = tt(V, v4(KK), zk, bc(vec("rwkv_k_k", 0, 4), 256), ALU.mult, zks)
            t_k2 = tt(V, TMP, KK, KK, ALU.mult, t_kk)
            yield
            tn = []

            def ev_n(bank, b, t):
                c = slice(512 * b, 512 * b + 512)
                t = ts(V, CS[:, c], bank, 1e-24, None, ALU.max, None, t)
                tn.append(tt(G, CS[:, c], CS[:, c], mh.broadcast_to([128, 512]), ALU.pow, t))
                return [t]

            yield from chunk_pairs(lambda o, c, bt, tk, sg: mm(o, const(C_BLK, 128), TMP[:, 256 * c:256 * c + 256], True, True,
                                                               bt, tk, sig=sg), ev_n, PB, t_k2, t_f)
            t_kn = tt(V, KK, KK, CS, ALU.mult, tn)
            for c in range(4):
                s = slice(256 * c, 256 * c + 256)
                t = ts(V, KM[:, s], A4[:, s], vec("rwkv_k_a", c), omka[:, c:c + 1], ALU.mult, ALU.add, ta, t_omka)
            t_km = tt(V, KM, KM, zk_f, ALU.mult, t)
            yield
            for c in range(4):
                t_ar = stt(AR[:, c, :, 0, :], v42(KK)[:, c], -1.0, v42(Qx)[:, c], ALU.mult, ALU.mult, t_kn, t_qx)
            t_b = tt(G, A4, A4, KK, ALU.mult, t_kn, t)
            t_b = tt(V, A4, A4, Qi, ALU.mult, t_b, t_qi)
            for c in range(4):
                t_r = tt(V, AR[:, c, :, 1, :], zm[:, c, :].rearrange("p (i t) -> p i t", i=2), v42(Q4)[:, c], ALU.mult, t_q)
            for c in range(4):
                t = stt(TMP[:, 256 * c:256 * c + 256], zm[:, c, :], vec("rwkv_r_k", c), KM[:, 256 * c:256 * c + 256],
                        ALU.mult, ALU.mult, t_km, tn)
            t_kt = tt(V, KM, KM, Qi, ALU.mult, t, t_qi)
            yield
            tb = []

            def ev_b(bank, b, t):
                c = slice(512 * b, 512 * b + 512)
                tb.append(tt(V, BON[:, c], bank, zv_f[:, c], ALU.mult, t))
                return [tb[-1]]

            yield from chunk_pairs(lambda o, c, bt, tk, sg: mm(o, const(C_BLK, 128), TMP[:, 256 * c:256 * c + 256], True, True,
                                                               bt, tk, sig=sg), ev_b, PB, t)
            t_vt = []
            for i in range(2):
                bank, bt = PB.get()
                for c in range(4):
                    t = tr(bank[:, 128 * c:128 * c + 128], zm[:, 8 + c, 128 * i:128 * i + 128], bt, zks, sig=(c == 3))
                t = cp(S, VT[:, i, :], bank, t, t_cs)
                PB.put(bank, t)
                t_vt.append(t)
                yield
            t_bk = []
            for n, (src, tk) in enumerate(((A4, t_b), (KM, t_kt))):
                bank, bt = PB.get()
                for c in range(4):
                    t = tr(bank[:, 128 * c:128 * c + 128], src[:, 256 * c:256 * c + 128], bt, tk, sig=(c == 3))
                t = cp(S, BK[:, n, :], bank, t, tb)
                PB.put(bank, t)
                t_bk.append(t)
                yield
            H0 = arena[:, R + 3072:R + 3072 + 512].rearrange("p (c w v) -> p c w v", c=4, w=2)
            t_h0 = mset(G, view(R + 3072, 512), 0.0, t_ar, tg)
            chain_off = [(P + 15360, P + 16384, P + 17408, P + 17920, P + 18432),
                         (P + 18944, R, P + 19968, P + 20480, P + 20992)]
            RHS, U = view(oKK, 512), view(oKK + 512, 512)
            Y, YC = view(R + 1024, 512), view(R + 1536, 512)

            def h8(x):
                return x.rearrange("p (h v) -> p h v", h=8)

            for i in range(2):
                res = {}

                def chain(p):
                    half = slice(64 * p, 64 * p + 64)
                    LN, MN, Xa, Xt, T = [view(o, n) for o, n in zip(chain_off[p], (1024, 1024, 512, 512, 512))]
                    LN4, MN4 = [x.rearrange("p (c w t) -> p c w t", c=4, w=2) for x in (LN, MN)]
                    bt_ = v42(A4)[half, :, i, :]
                    kt_ = v42(KM)[half, :, i, :]
                    a_ = AR[half, :, i, :, :]
                    first = [t_ar, t_r, t_b, t_kt, rw.get("chain_free")]
                    msk = const(C_SU, 256).unsqueeze(1).broadcast_to([128, 2, 256])
                    for dst, src in ((LN, bt_), (MN, kt_)):
                        for b in range(2):
                            bank, bt = PB.get()
                            for j in range(2):
                                c = 2 * b + j
                                t = mm(bank[:, 256 * j:256 * j + 256], src[:, c, :], a_[:, c, :, :].rearrange("p w t -> p (w t)"),
                                       True, True, first, bt, sig=(j == 1))
                            t = tt(V, halves(dst[:, 512 * b:512 * b + 512]), halves(bank), msk, ALU.mult, t)
                            PB.put(bank, t)
                        t_dst = t
                        yield
                    bank, bt = PB.get()
                    for c in range(4):
                        t = mm(bank[:, 128 * c:128 * c + 128], a_[:, c, 0, :], bt_[:, c, :], True, True, bt, sig=(c == 3))
                    t = tt(V, quarters(Xa), quarters(bank), rep(const(C_M0, 128), 4), ALU.mult, t, first)
                    PB.put(bank, t)
                    tx = tt(G, quarters(Xa), quarters(Xa), rep(ident, 4), ALU.add, t)
                    t = tt(V, quarters(Xt), LN4[:, :, 0, :], rep(const(C_M0T, 128), 4), ALU.mult, t_dst)
                    txt = tt(G, quarters(Xt), quarters(Xt), rep(ident, 4), ALU.add, t)
                    yield
                    tmm = None
                    for lv in range(6):
                        bank, bt = PB.get()
                        for c in range(4):
                            o = bank[:, 128 * c:128 * c + 128]
                            mm(o, ident, ident, True, False, bt)
                            t = mm(o, LN4[:, c, 0, :], Xa[:, 128 * c:128 * c + 128], False, True, tx, t_dst, sig=(c == 3))
                        tT = tt(V, quarters(T), quarters(bank), rep(const(C_LV + 128 * lv, 128), 4), ALU.mult, t, tmm)
                        PB.put(bank, tT)
                        yield
                        bank, bt = PB.get()
                        for c in range(4):
                            s = slice(128 * c, 128 * c + 128)
                            t = mm(bank[:, s], T[:, s], Xt[:, s], True, True, tT, txt, bt, sig=(c == 3))
                        if lv < 5:
                            bank2, bt = PB.get()
                            for c in range(4):
                                s = slice(128 * c, 128 * c + 128)
                                t2 = mm(bank2[:, s], Xt[:, s], T[:, s], True, True, tT, txt, bt, sig=(c == 3))
                            tmm = t2
                            txt = cp(S, Xt, bank, t2)
                            tx = cp(S, Xa, bank2, t2)
                            PB.put(bank2, tx)
                        else:
                            txt = cp(S, Xt, bank, t)
                        PB.put(bank, txt)
                        yield
                    res[p] = (LN4, MN4, Xt, [txt, t_dst])

                gs = [chain(0), chain(1)]
                while gs:
                    for g in list(gs):
                        try:
                            next(g)
                        except StopIteration:
                            gs.remove(g)
                    yield
                both = [res[0][3], res[1][3], t_vt]
                bank, bt = PB.get()
                for h in range(8):
                    c, p = h // 2, h % 2
                    o = bank[:, 64 * h:64 * h + 64]
                    t = mm(o, res[p][1][:, c, 0, :], VT[:, i, 64 * h:64 * h + 64], True, i == 0, both, bt, sig=(h == 7))
                    if i == 1:
                        t = mm(o, AR[:, c, 1, 0, :], H0[:, c, p, :], False, True, t_h0, sig=(h == 7))
                t = cp(V, RHS, bank, t, rw.get("rhs_free"))
                PB.put(bank, t)
                yield
                bank, bt = PB.get()
                for h in range(8):
                    c, p = h // 2, h % 2
                    t = mm(bank[:, 64 * h:64 * h + 64], res[p][2][:, 128 * c:128 * c + 128], RHS[:, 64 * h:64 * h + 64],
                           True, True, t, bt, sig=(h == 7))
                t_U = cp(V, U, bank, t)
                PB.put(bank, t_U)
                yield
                bank, bt = PB.get()
                for h in range(8):
                    c, p = h // 2, h % 2
                    s = slice(64 * h, 64 * h + 64)
                    mm(bank[:, s], res[p][0][:, c, 1, :], U[:, s], True, False, t_U, bt)
                    t = mm(bank[:, s], res[p][1][:, c, 1, :], VT[:, i, s], False, i == 0, sig=(h == 7))
                    if i == 1:
                        t = mm(bank[:, s], AR[:, c, 1, 1, :], H0[:, c, p, :], False, True, sig=(h == 7))
                rw["chain_free"] = t
                tY = cp(S, Y, bank, t, rw.get("y_free"))
                PB.put(bank, tY)
                if i == 0:
                    bank, bt = PB.get()
                    for h in range(8):
                        c, p = h // 2, h % 2
                        s = slice(64 * h, 64 * h + 64)
                        o = bank[64 * p:64 * p + 64, 64 * c:64 * c + 64]
                        mm(o, BK[:, 0, s], U[:, s], True, False, t_bk, bt)
                        t = mm(o, BK[:, 1, s], VT[:, 0, s], False, True, sig=(h == 7))
                    hb = bank[:, 0:256].rearrange("p (c v) -> p c v", c=4)
                    for p in range(2):
                        q = slice(64 * p, 64 * p + 64)
                        t_hh = tt(V, H0[q, :, p, :], hb[q], bc(fct[q, :], 64), ALU.mult, t, t_f, t_h0)
                    t_h0 = t_hh
                    PB.put(bank, t_hh)
                    rw["rhs_free"] = t
                mean, var = small(8), small(8)
                t = red(mean, h8(Y), ALU.add, tY)
                t = ts(V, mean, mean, 1.0 / 64, None, ALU.mult, None, t)
                t = tt(V, h8(Y), h8(Y), bc(mean, 64), ALU.subtract, t)
                t = act(YC, Y, ACT.Square, t)
                t = red(var, h8(YC), ALU.add, t)
                t = rstd(var, var, 64, GN_EPS, t)
                t = tt(V, h8(YC), h8(Y), bc(var, 64), ALU.mult, t)
                rw["y_free"] = t
                yield
                bank, bt = PB.get()
                for c in range(4):
                    tp = tr(bank[:, 128 * c:128 * c + 128], YC[:, 128 * c:128 * c + 128], t, bt, sig=(c == 3))
                for c in range(4):
                    t = act(o_rwkv[:, c, 128 * i:128 * i + 128], bank[:, 128 * c:128 * c + 128], ACT.Identity, tp, tb, t_vt,
                            scale=vec("rwkv_ln_w", c), bias=vec("rwkv_ln_b", c))
                PB.put(bank, t)
                rw["y_free"] = tp
                o_ = o_rwkv[:, :, 128 * i:128 * i + 128]
                t = tt(V, o_, o_, v4(BON)[:, :, 128 * i:128 * i + 128], ALU.add, t)
                t = tt(V, o_, o_, v4(G4)[:, :, 128 * i:128 * i + 128], ALU.mult, t, tg)
                yield
            rw["out"] = t

        qk = view3(P + 4096, 12, 256)
        vtok = view3(P + 7168, 2, 768)
        rz = [view3(P + 8704 + 1024 * i, 2, 256) for i in range(2)]
        rt = [view3(P + 9216 + 1024 * i, 2, 256) for i in range(2)]
        t_qk, rprev, t_vtok = [], [None, None], []

        def evac_qk(bank, n, tok):
            fr, td = rope(bank, 2, tok, qk[:, 2 * n:2 * n + 2, :], const(C_COS, 256), const(C_SIN, 256),
                          rz[n % 2], rt[n % 2], rprev[n % 2])
            rprev[n % 2] = td
            t_qk.append(td)
            return fr

        gates = view3(P, 16, 256)
        t_gate = []

        def evac_gate(dst, lst):
            def f(bank, n, tok):
                t = act(dst[:, 2 * n:2 * n + 2, :], halves(bank), ACT.Sigmoid, tok, t_v)
                lst.append(t)
                return [t]
            return f

        def qkv_main():
            yield from gemm_f(w_in, [([(256 * n, 256, 0)], [128, 128]) for n in range(6)], 8, evac_qk, uT, t_u)
            for c0, w in ((1536, 512), (2048, 256)):
                banks = [PG.get() for _ in range(2)]
                nk = 2048 // w
                slots = [([wcols(w_in, c0, w, k, nk, 0, w)], nk) for k in range(0, 8, nk)]
                t = yield from gemm_t(slots, uT, t_u, banks, w, 8)
                for i in range(2):
                    te = cp(S, vtok[:, i, c0 - 1536:c0 - 1536 + w], banks[i][0][:, 0:w], t)
                    PG.put(banks[i][0], te)
                    t_vtok.append(te)

        def softmax_e(e, pieces, nm, den, rden, gate, *toks):
            t = None
            for n, (ps, mask, dst) in enumerate(pieces):
                init = 3e38 if n == 0 else nm[:, n - 1:n]
                t = V(lambda e_, ps=ps, mask=mask, dst=dst, init=init, n=n: e_.tensor_tensor_reduce(
                    dst, ps, mask, -0.125, init, ALU.add, ALU.min, nm[:, n:n + 1]), [toks, t])
            free = t
            t = act(e, e, ACT.Exp, t, scale=-1.0, bias=nm[:, len(pieces) - 1:len(pieces)], accum=den)
            t = recip(rden, den, t)
            if gate is not None:
                t = tt(V, rden, rden, gate, ALU.mult, t)
            t = ts(V, e, e, rden, None, ALU.mult, None, t)
            return free, t

        def attn_side(par):
            sm = view(P + 8704 + 1536 * par, 768)
            eT = view(P + 8704 + 1536 * par + 768, 768)
            e_free = et_free = None
            half = slice(64 * par, 64 * par + 64)
            nm, den, rden = small(2), small(1), small(1)
            ma = const(C_MA, 768)
            for i in range(2):
                for hh in range(2):
                    h = 2 * hh + par
                    W = 128 * (i + 1)
                    banks = [PA.get() for _ in range(i + 1)]
                    for g in range(3):
                        b, bt = banks[(g * W) // 512]
                        o = (g * W) % 512
                        t = mm(b[:, o:o + W], qk[half, 2 * g + hh, 128 * i:128 * i + 128], qk[half, 6 + 2 * g + hh, 0:W],
                               True, True, t_qk, bt, sig=True)
                    if i == 0:
                        pieces = [(banks[0][0][:, 0:384].rearrange("p (g t) -> p g t", g=3),
                                   ma.rearrange("p (g w t) -> p g w t", g=3, w=2)[:, :, 1, :],
                                   sm[:, 0:384].rearrange("p (g t) -> p g t", g=3))]
                    else:
                        pieces = [(banks[0][0], ma[:, 0:512], sm[:, 0:512]), (banks[1][0][:, 0:256], ma[:, 512:768], sm[:, 512:768])]
                    free, te = softmax_e(sm[:, 0:3 * W], pieces, nm, den, rden, None, t, e_free, rprev)
                    for b, _ in banks:
                        PA.put(b, free)
                    yield
                    nb = 3 * (i + 1)
                    for b0 in range(0, nb, 4):
                        k = min(4, nb - b0)
                        bank, bt = PA.get()
                        for j in range(k):
                            t = tr(bank[:, 128 * j:128 * j + 128], sm[:, 128 * (b0 + j):128 * (b0 + j) + 128], te, bt, sig=(j == k - 1))
                        tT = cp(S, eT[:, 128 * b0:128 * (b0 + k)], bank[:, 0:128 * k], t, et_free, rprev)
                        PA.put(bank, tT)
                    e_free = t
                    yield
                    bank, bt = PA.get()
                    for n in range(nb):
                        g, j = n // (i + 1), n % (i + 1)
                        t = mm(bank[half, 0:128], vtok[:, j, 64 * (4 * g + h):64 * (4 * g + h) + 64], eT[:, 128 * n:128 * n + 128],
                               n == 0, n == nb - 1, tT, bt, t_vtok, sig=(n == nb - 1))
                    et_free = t
                    t = cp(S, o_attn[half, hh, 128 * i:128 * i + 128], bank[half, 0:128], t)
                    PA.put(bank, t)
                    rw.setdefault("attn", []).append(t)
                    yield

        side = rwkv_side()
        drive_live = [qkv_main(), side]
        drive_main = drive_live[0]
        while True:
            try:
                next(drive_main)
            except StopIteration:
                break
            try:
                next(side)
            except StopIteration:
                pass
        gate_main = gemm_f(w_in, [([(4000 + 256 * n, 256, 0)], [128, 128]) for n in range(8)], 8, evac_gate(gates, t_gate), uT, t_u)
        drive(gate_main, side, attn_side(0), attn_side(1))

        mT = view3(P + 4096, 8, 256)
        tm = [view3(P + 8704 + 512 * i, 2, 256) for i in range(4)]
        t_m = {}
        mfree = [None] * 4

        def evac_up1(bank, n, tok):
            t = tt(V, mT[:, 2 * n:2 * n + 2, :], halves(bank), gates[:, 2 * n:2 * n + 2, :], ALU.mult, tok, t_gate)
            t_m[n] = t
            return [t]

        def evac_up2(bank, n, tok):
            t = tt(V, tm[n], halves(bank), gates[:, 8 + 2 * n:10 + 2 * n, :], ALU.mult, tok, t_gate)
            t_m[n] = tt(G, mT[:, 2 * n:2 * n + 2, :], mT[:, 2 * n:2 * n + 2, :], tm[n], ALU.add, t, t_m[n])
            return [t]

        wide = [([(256 * n, 256, 0)], [128, 128]) for n in range(4)]
        alone(gemm_f(A["w_attn_up"][0], wide, 2, evac_up1, o_attn, rw["attn"]))
        alone(gemm_f(A["w_rwkv_up"][0], wide, 4, evac_up2, o_rwkv, rw["out"]))

        H = view3(P + 7168, 2, 1024)
        XN = view3(P + 9216, 2, 1024)

        def full(W, lhs, dep, K, pools):
            got = [[None] * 2 for _ in range(2)]
            t = None
            for n in range(2):
                banks = [pools[n].get() for _ in range(2)]
                slots = [([wcols(W, 512 * n, 512, k, min(4, K - k), 0, 512)], min(4, K - k)) for k in range(0, K, 4)]
                t = yield from gemm_t(slots, lhs, dep, banks, 512, K)
                for i in range(2):
                    got[i][n] = (banks[i][0], t, pools[n])
            return got

        def finish(got, read):
            for i in range(2):
                for n in range(2):
                    got[i][n][2].put(got[i][n][0], read[i][n])

        def proj_norm(W, lhs, dep, K, gname, hsrc, htoks):
            got = alone(full(W, lhs, dep, K, (PG, PA)))
            done, read = alone(post_norm([[g[0] for g in r] for r in got], gname, H, hsrc, [[g[1] for g in r] for r in got],
                                         htoks, XN))
            finish(got, read)
            return done

        xr = view3(P + 19968, 2, 1024)
        s_xr = sem("s_xr")
        t_xr = dma(SP, xr, x_d, s_xr, rw["out"], t_m[3])
        t_h = proj_norm(A["w_out"][0], mT, [t_m[n] for n in range(4)], 8, "mix_post_norm", xr, [t_xr, t_m[3]])

        hid = view3(P + 11776, 32, 256)
        t_u = alone(norm_t(H, XN, "ffn_pre_norm", uT, t_h))
        t_hid = []
        rl = [view3(P + 512 * i, 2, 256) for i in range(2)]
        rlf = [None, None]

        def evac_relu2(bank, n, tok):
            t = act(rl[n % 2], halves(bank), ACT.Relu, tok, rlf[n % 2])
            t2 = tt(V, hid[:, 2 * n:2 * n + 2, :], halves(bank), rl[n % 2], ALU.mult, t)
            rlf[n % 2] = t2
            t_hid.append(t2)
            return [t2]

        alone(gemm_f(A["w_ff_in"][0], [([(256 * n, 256, 0)], [128, 128]) for n in range(16)], 8, evac_relu2, uT, t_u))

        def down(W, lhs, dep, K):
            banks = [[PG.get(), PA.get()] for _ in range(2)]
            for k0 in range(0, K, 2):
                wn, slot, wt = wload([wcols(W, 0, 1024, k0, 2, 0, 1024)])
                w3 = slot.rearrange("p (k n) -> p k n", k=2)
                for kk in range(2):
                    k = k0 + kk
                    for i in range(2):
                        for n in range(2):
                            b, bt = banks[i][n]
                            t = mm(b, lhs[:, k, 128 * i:128 * i + 128], w3[:, kk, 512 * n:512 * n + 512], k == 0, k == K - 1,
                                   dep[k // 2], wt, bt, sig=(kk == 1 and i == 1 and n == 1))
                    yield
                wfree(wn, t)
            return [[(banks[i][n][0], t, (PG, PA)[n]) for n in range(2)] for i in range(2)]

        def after(got, gname):
            done, read = alone(post_norm([[g[0] for g in r] for r in got], gname, H, H, [[g[1] for g in r] for r in got],
                                         None, XN))
            finish(got, read)
            return done

        s_p = sem("s_p")
        pT = view3(P + 2048, 2, 256)
        ptok = view3(P + 2560, 2, 256)
        pE = view3(P + 3072, 2, 1024)
        t_p = dma(SP, ptok, A["p"][0, 0].rearrange("(i p) d -> p i d", p=128), s_p, t_h)

        def ple_in():
            bank, bt = PB.get()
            for c in range(2):
                for i in range(2):
                    t = tr(bank[:, 256 * c + 128 * i:256 * c + 128 * i + 128], ptok[:, i, 128 * c:128 * c + 128], t_p, bt,
                           sig=(c == 1 and i == 1))
            t_pT = cp(S, pT, halves(bank), t)
            PB.put(bank, t_pT)
            wn, slot, wt = wload([wcols(A["w_ple"][0], 0, 1024, 0, 2, 0, 1024)])
            w3 = slot.rearrange("p (k n) -> p k n", k=2)
            te = []
            for n in range(2):
                for i in range(2):
                    b, bt = PB.get()
                    for k in range(2):
                        t = mm(b, pT[:, k, 128 * i:128 * i + 128], w3[:, k, 512 * n:512 * n + 512], k == 0, k == 1, t_pT, wt, bt,
                               sig=(k == 1))
                    te.append(cp(S, pE[:, i, 512 * n:512 * n + 512], b, t))
                    PB.put(b, te[-1])
                    yield
            wfree(wn, t)
            return te

        got = alone(down(A["w_ff_out"][0], hid, t_hid, 32))
        t_pe = alone(ple_in())
        t_h = after(got, "ffn_post_norm")
        hT = uT
        t_hT = alone(norm_t(H, XN, None, hT, t_h, gain=False))
        got = alone(full(A["w_ple_gate"][0], hT, t_hT, 8, (PG, PA)))
        te = [[None] * 2 for _ in range(2)]
        for i in range(2):
            for n in range(2):
                b, t, pool = got[i][n]
                c = slice(512 * n, 512 * n + 512)
                t = act(XN[:, i, c], b, ACT.Sigmoid, t)
                pool.put(b, t)
                te[i][n] = tt(V, pE[:, i, c], pE[:, i, c], XN[:, i, c], ALU.mult, t, t_pe)
        t_h, _ = alone(post_norm([[pE[:, i, 512 * n:512 * n + 512] for n in range(2)] for i in range(2)], "ple_post_norm",
                                 H, H, te, None, XN))

        mem_sb = view3(P + 11776, 2, 1024)
        mem_n = view3(P + 13824, 2, 1024)
        memT = view3(P + 15872, 8, 256)
        memK = view3(P + 25128, 2, 256)
        memV = view3(P + 25640, 2, 256)
        s_m = sem("s_m")
        t_mem = dma(SP, mem_sb, A["mem_2"][0].rearrange("(i p) d -> p i d", p=128), s_m, t_hT)
        t_mT = alone(norm_t(mem_sb, mem_n, "norm_mem_kv_2", memT, [t_mem, t_mem]))
        t_mk, t_mv = [], []

        def evac_mk(bank, n, tok):
            t_mk.append(cp(S, memK, halves(bank), tok))
            return [t_mk[-1]]

        w_kv = A["w_mem_kv_2"][0]
        alone(gemm_f(w_kv, [([(0, 256, 0)], [128, 128])], 8, evac_mk, memT, t_mT))
        banks = [PG.get() for _ in range(2)]
        t = alone(gemm_t([([wcols(w_kv, 256, 256, 0, 8, 0, 256)], 8)], memT, t_mT, banks, 256, 8))
        for i in range(2):
            t_mv.append(cp(S, memV[:, i, :], banks[i][0][:, 0:256], t))
            PG.put(banks[i][0], t_mv[-1])

        t_u = alone(norm_t(H, XN, "norm_mix_2", uT, t_h))
        w2in = A["w_in_2"][0]
        gate2 = view3(P + 11776, 24, 256)
        RC = view3(P + 17920, 11, 256)
        QA = view3(P + 20736, 4, 256)
        vt = view3(P + 21760, 2, 660)
        rz = [view3(P + 23080 + 1024 * i, 2, 256) for i in range(2)]
        rt = [view3(P + 23592 + 1024 * i, 2, 256) for i in range(2)]
        oC = view3(P, 6, 256)
        t_rc, t_qa, rprev2 = {}, [], [None, None]
        t_vt2 = []

        def evac_a(bank, n, tok):
            if n < 2:
                t = cp(S, QA[:, 2 * n:2 * n + 2, :], halves(bank), tok)
                t_qa.append(t)
                return [t]
            m = 1 if n == 7 else 2
            c = 2 * (n - 2)
            cc, sc = (C_COSC, C_SINC) if n == 7 else (C_COS, C_SIN)
            fr, td = rope(bank, m, tok, RC[:, c:c + m, :], const(cc, 256), const(sc, 256),
                          rz[n % 2][:, 0:m, :], rt[n % 2][:, 0:m, :], rprev2[n % 2])
            rprev2[n % 2] = td
            for j in range(m):
                t_rc[c + j] = td
            return fr

        dup = lambda c, d: [(c, 64, d), (c, 64, d + 64)]
        plan2 = [([(0, 256, 0)], [128, 128]), ([(256, 256, 0)], [128, 128]), ([(768, 256, 0)], [128, 128]),
                 ([(1152, 256, 0)], [128, 128]), ([(1476, 256, 0)], [128, 128]),
                 (dup(1024, 0) + dup(1408, 128), [128, 128]), (dup(1860, 0) + dup(1988, 128), [128, 128]),
                 ([(1732, 128, 0)], [128])]

        VP = [(512, 256, 0), (1088, 64, 256), (1924, 64, 320), (2052, 76, 384), (1472, 4, 460)]
        banks = [PG.get() for _ in range(2)]
        slots = [([wcols(w2in, c0, w, k, 4, d0, 464) for c0, w, d0 in VP], 4) for k in (0, 4)]
        t = alone(gemm_t(slots, uT, t_u, banks, 464, 8))
        wsc, g12 = small(8), small(24)
        for i in range(2):
            b = banks[i][0]
            fr = [cp(S, vt[:, i, 0:256], b[:, 0:256], t)]
            fr.append(act(g12[:, 12 * i:12 * i + 12], b[:, 448:460], ACT.Sigmoid, t))
            for d in range(2):
                fr.append(cp(V, vt[:, i, 256:640].rearrange("p (n d v) -> p n d v", n=3, d=2)[:, :, d, :],
                             b[:, 256:448].rearrange("p (n v) -> p n v", n=3), t, fr[1]))
            fr.append(ts(V, wsc[:, 4 * i:4 * i + 4], b[:, 460:464], 0.0625, None, ALU.mult, None, t))
            PG.put(b, fr)
            t_vt2 += fr
        alone(gemm_f(w2in, plan2, 8, evac_a, uT, t_u))

        t_oc = {0: [], 1: [], 2: []}

        def stick():
            Z = view(P + 26152, 1536)
            SPL = view(P + 27688, 1536)
            TM = view(P + 29224, 1536)
            z4 = Z.rearrange("p (h t) -> p h t", h=4)
            s4 = SPL.rearrange("p (h t) -> p h t", h=4)
            st = const(C_ST, 384)
            tz = []
            for par in range(2):
                half = slice(64 * par, 64 * par + 64)
                b0, bt0 = PA.get()
                b1, bt1 = PA.get()
                for hh in range(2):
                    kT = QA[half, 2 + hh, :]
                    qT = QA[half, hh, :]
                    mm(b0[:, 256 * hh:256 * hh + 256], kT[:, 0:128], qT[:, 0:256], True, True, t_qa, bt0)
                    t = mm(b1[:, 128 * hh:128 * hh + 128], kT[:, 128:256], qT[:, 128:256], True, True, bt1, sig=True)
                zz = z4[:, par::2, :]
                ta = stt(zz[:, :, 0:256], halves(b0), 0.125, rep(st[:, 0:256], 2), ALU.mult, ALU.add, t)
                tb_ = stt(zz[:, :, 256:384], b1[:, 0:256].rearrange("p (h t) -> p h t", h=2), 0.125, rep(st[:, 256:384], 2),
                          ALU.mult, ALU.add, t)
                PA.put(b0, ta)
                PA.put(b1, tb_)
                tz += [ta, tb_]
                yield
            t = act(TM, Z, ACT.Abs, tz)
            t = act(TM, TM, ACT.Exp, t, scale=-1.0)
            t = act(TM, TM, ACT.Ln, t, bias=1.0)
            t_sp = stt(SPL, Z, 0.0, TM, ALU.max, ALU.add, t)
            yield
            LI, ONE = const(C_LI, 128), const(C_ONE, 128)
            tw = []
            for hp in range(2):
                hs = slice(2 * hp, 2 * hp + 2)
                b0, bt0 = PA.get()
                for q in range(2):
                    h = 2 * hp + q
                    mm(b0[:, 256 * q:256 * q + 256], LI, s4[:, h, 0:256], True, False, t_sp, bt0)
                    t = mm(b0[:, 256 * q + 128:256 * q + 256], ONE, s4[:, h, 256:384], False, True, sig=True)
                ta = tt(V, z4[:, hs, 0:256], z4[:, hs, 0:256], halves(b0), ALU.subtract, t)
                PA.put(b0, ta)
                b1, bt1 = PA.get()
                for q in range(2):
                    t = mm(b1[:, 128 * q:128 * q + 128], LI, s4[:, 2 * hp + q, 256:384], True, True, bt1, sig=True)
                tb_ = tt(V, z4[:, hs, 256:384], z4[:, hs, 256:384], b1[:, 0:256].rearrange("p (h t) -> p h t", h=2), ALU.subtract, t)
                PA.put(b1, tb_)
                tw += [ta, tb_]
                yield
            tw = act(Z, Z, ACT.Exp, tw)
            yield
            for par in range(2):
                half = slice(64 * par, 64 * par + 64)
                b0, bt0 = PA.get()
                for hh in range(2):
                    h = 2 * hh + par
                    o = 256 * hh
                    mm(b0[half, o:o + 256], vt[:, 0, 64 * h:64 * h + 64], z4[:, h, 0:256], True, False, tw, t_vt2, bt0)
                    t = mm(b0[half, o + 128:o + 256], vt[:, 1, 64 * h:64 * h + 64], z4[:, h, 256:384], False, True, sig=True)
                t = cp(S, oC[half, 0:2, :], halves(b0)[half], t)
                PA.put(b0, t)
                t_oc[0].append(t)
                yield

        def scores4(i, qc, kc, W, pool, *toks):
            banks = [pool.get() for _ in range(2)]
            ts_ = []
            for par in range(2):
                half = slice(64 * par, 64 * par + 64)
                b, bt = banks[par]
                for hh in range(2):
                    t = mm(b[:, 256 * hh:256 * hh + W], RC[half, qc + hh, 128 * i:128 * i + 128], RC[half, kc, 0:W],
                           True, True, toks, bt, sig=True)
                ts_.append(t)
            return banks, ts_

        def turn4(E, eT, W, te, pool, et_free, toks=None):
            out_ = []
            for j in range(W // 128):
                bank, bt = pool.get()
                for h in range(4):
                    t = tr(bank[:, 128 * h:128 * h + 128], E[:, h, 128 * j:128 * j + 128], te, bt, sig=(h == 3))
                tc_ = cp(S, eT[:, 512 * j:512 * j + 512], bank, t, et_free)
                pool.put(bank, tc_)
                out_.append(tc_)
            return t, out_

        def spread(bank, br, i, t, pool):
            fr = []
            for par in range(2):
                half = slice(64 * par, 64 * par + 64)
                fr.append(cp(V, oC[half, 2 * br:2 * br + 2, 128 * i:128 * i + 128], quarters(bank)[half, par::2, :], t))
            pool.put(bank, fr)
            t_oc[br] += fr

        ca = const(C_CA, 256)

        def dsa():
            W0 = P + 1536
            rel = view3(W0, 4, 256)
            acc, wk, add = view(W0 + 1024, 256), view(W0 + 1280, 256), view(W0 + 1536, 256)
            m8 = view(W0 + 1792, 8)
            E = view3(W0 + 1856, 4, 256)
            eT = view(W0 + 2880, 1024)
            nm, den, rden = small(4), small(4), small(4)
            r_free = e_free = et_free = a_free = None
            kr = [t_rc[2], t_rc[3], t_rc[7]]
            ks = [t_rc[0], t_rc[1], t_rc[6]]
            for i in range(2):
                W = 128 * (i + 1)
                msk = ca[:, 256 - W:256]
                banks, t = scores4(i, 2, 7, W, PA, kr)
                tr_ = []
                for par in range(2):
                    b = banks[par][0]
                    t1 = act(rel[:, par::2, 0:W], halves(b)[:, :, 0:W], ACT.Relu, t[par], r_free)
                    PA.put(b, t1)
                    tr_.append(t1)
                src = msk
                for h in range(4):
                    ta = stt(acc[:, 0:W], rel[:, h, 0:W], wsc[:, 4 * i + h:4 * i + h + 1], src, ALU.mult, ALU.add,
                             tr_, t_vt2, None if h == 0 else ta)
                    src = acc[:, 0:W]
                r_free = ta
                yield
                cur = acc
                for r in range(8):
                    a, w = acc[:, 0:W], cur[:, 0:W]
                    t = V(lambda e, w=w: e.max(m8, w), [ta])
                    ta = V(lambda e, a=a, w=w: e.match_replace(a, m8, w, TAKEN), [t])
                    if r % 2:
                        yield
                t = ts(V, add[:, 0:W], acc[:, 0:W], TAKEN, NEG, ALU.is_gt, ALU.mult, ta)
                ta = tt(V, add[:, 0:W], add[:, 0:W], msk, ALU.add, t)
                banks, t = scores4(i, 0, 6, W, PA, ks)
                te = []
                for h in range(4):
                    b = banks[h % 2][0]
                    hh = h // 2
                    free, t_ = softmax_e(E[:, h, 0:W], [(b[:, 256 * hh:256 * hh + W], add[:, 0:W], E[:, h, 0:W])],
                                         nm[:, h:h + 1], den[:, h:h + 1], rden[:, h:h + 1], None, t, ta, e_free)
                    te.append(t_)
                    if hh == 1:
                        PA.put(b, free)
                yield
                e_free, tT = turn4(E, eT, W, te, PA, et_free)
                yield
                bank, bt = PA.get()
                for j in range(i + 1):
                    t = mm(bank, vt[:, j, 256:384], eT[:, 512 * j:512 * j + 512], j == 0, j == i, tT, t_vt2, bt, sig=(j == i))
                et_free = t
                spread(bank, 1, i, t, PA)
                yield

        def nsa():
            blk = view(P + 5300, 480)
            tokT = RC[:, 10, :]
            b3 = blk.rearrange("p (l n) -> p l n", l=32)
            tb_ = []
            for n in range(15):
                tb_.append(tt(G, b3[:, :, n], tokT[:, 16 * n:16 * n + 32], vec("pos", 0, 32), ALU.add, t_rc[10]))
            tb_ = [tb_[-1]]
            yield
            bk, btk = PB.get()
            bv, btv = PB.get()
            for s in range(2):
                w1 = [(lambda sl, q=q: sl[64 * q:64 * q + 64, :].rearrange("p (l n) -> p l n", l=16),
                       A[nm_][0][1024 * s:1024 * s + 1024, :].rearrange("(l d) n -> d l n", d=64))
                      for q, nm_ in enumerate(("cmp_w1_k_2", "cmp_w1_v_2"))]
                wn, slot, wt = wload(w1)
                w3 = slot.rearrange("p (l n) -> p l n", l=16)
                for q, (b, bt) in enumerate(((bk, btk), (bv, btv))):
                    half = slice(64 * q, 64 * q + 64)
                    for l in range(16):
                        t = mm(b[0:15, 0:128], b3[half, 16 * s + l, :], w3[half, l, :], s == 0 and l == 0, s == 1 and l == 15,
                               tb_, wt, bt, sig=(l == 15))
                    if q == 0:
                        t_k = t
                wfree(wn, t)
                yield
            hd = view3(P + 5780, 2, 128)
            tmp = view3(P + 6036, 2, 128)
            th = []
            for q, (b, t_) in enumerate(((bk, t_k), (bv, t))):
                x, y = hd[0:15, q, :], tmp[0:15, q, :]
                t1 = cp(V, x, b[0:15, 0:128], t_)
                PB.put(b, t1)
                t2 = tt(V, y, x, x, ALU.mult, t1)
                t2 = ts(V, y, y, 0.044715, 1.0, ALU.mult, ALU.add, t2)
                t2 = tt(V, y, y, x, ALU.mult, t2)
                t2 = act(y, y, ACT.Sigmoid, t2, scale=2.0 * math.sqrt(2.0 / math.pi))
                th.append(tt(V, x, x, y, ALU.mult, t2))
            yield
            bank, bt = PB.get()
            for q in range(2):
                t = tr(bank[:, 16 * q:16 * q + 15], hd[0:15, q, :], th[q], bt, sig=True)
            hT_ = view(P + 6292, 32)
            t1 = [cp(V, hT_[:, 16 * q:16 * q + 15], bank[:, 16 * q:16 * q + 15], t) for q in range(2)]
            PB.put(bank, *t1)
            wn, slot, wt = wload([(lambda s, o=o: s[:, o:o + 64], A[nm_][0])
                                  for o, nm_ in ((0, "cmp_w2_k_2"), (64, "cmp_w2_k_2"), (128, "cmp_w2_v_2"), (192, "cmp_w2_v_2"))])
            bank, bt = PB.get()
            t = mm(bank[:, 0:15], slot[:, 0:128], hT_[:, 0:15], True, True, t1, wt, bt, sig=True)
            t2 = mm(bank[0:15, 128:256], hT_[:, 16:31], slot[:, 128:256], True, True, sig=True)
            wfree(wn, t2)
            kc = view(P + 6324, 16)
            vc = view(P + 6340, 128)
            t_kc = cp(V, kc[:, 0:15], bank[:, 0:15], t2)
            t_vc = cp(V, vc[0:15, :], bank[0:15, 128:256], t2)
            PB.put(bank, t_kc, t_vc)
            yield
            E = view3(P + 9216, 4, 256)
            eT = view(P + 10240, 1024)
            EC = view(P + 6468, 60).rearrange("p (h n) -> p h n", h=4)
            eTc = view(P + 6528, 512)
            nm, den, rden = small(4), small(4), small(4)
            mx = small(4)
            e_free = et_free = ec_free = None
            for i in range(2):
                W = 128 * (i + 1)
                msk = ca[:, 256 - W:256]
                o_bank, obt = PB.get()
                sb_, sbt = PB.get()
                sb2, sbt2 = PB.get()
                for par, (b, bt) in enumerate(((sb_, sbt), (sb2, sbt2))):
                    half = slice(64 * par, 64 * par + 64)
                    for hh in range(2):
                        t = mm(b[:, 16 * hh:16 * hh + 15], RC[half, 4 + hh, 128 * i:128 * i + 128], kc[half, 0:15], True, True,
                               t_kc, t_rc[4], bt, sig=True)
                    b3_ = b[:, 0:32].rearrange("p (h n) -> p h n", h=2)[:, :, 0:15]
                    tc_ = stt(EC[:, par::2, :], b3_, 0.125, rep(const(C_CMA + 15 * i, 15), 2), ALU.mult, ALU.add, t, ec_free)
                    PB.put(b, tc_)
                t = red(mx, EC, ALU.max, tc_)
                t = tt(V, EC, EC, bc(mx, 15), ALU.subtract, t)
                t = act(EC, EC, ACT.Exp, t)
                t = tt(V, EC, EC, rep(const(C_CMM + 15 * i, 15), 4), ALU.mult, t)
                t = red(mx, EC, ALU.add, t)
                t = ts(V, mx, mx, 1e-30, None, ALU.max, None, t)
                t = recip(mx, mx, t)
                gi = g12[:, 12 * i:12 * i + 12].rearrange("p (h b) -> p h b", b=3)
                t = tt(V, mx, mx, gi[:, :, 0], ALU.mult, t, t_vt2)
                t_ec = tt(V, EC, EC, bc(mx, 15), ALU.mult, t)
                yield
                bank, bt = PB.get()
                for h in range(4):
                    t = tr(bank[0:15, 128 * h:128 * h + 128], EC[:, h, :], t_ec, bt, sig=(h == 3))
                ec_free = t
                t = cp(S, eTc[0:15, :], bank[0:15, :], t, et_free)
                PB.put(bank, t)
                mm(o_bank, vc[0:15, :], eTc[0:15, :], True, False, t, t_vc, obt)
                yield
                for br in (1, 2):
                    banks, t = scores4(i, 4, 7 + br, W, PB, t_rc[4], t_rc[7 + br])
                    te = []
                    for h in range(4):
                        b = banks[h % 2][0]
                        hh = h // 2
                        free, t_ = softmax_e(E[:, h, 0:W], [(b[:, 256 * hh:256 * hh + W], msk, E[:, h, 0:W])],
                                             nm[:, h:h + 1], den[:, h:h + 1], rden[:, h:h + 1], gi[:, h, br:br + 1],
                                             t, t_vt2, e_free)
                        te.append(t_)
                        if hh == 1:
                            PB.put(b, free)
                    yield
                    e_free, tT = turn4(E, eT, W, te, PB, et_free)
                    yield
                    for j in range(i + 1):
                        lastmm = br == 2 and j == i
                        t = mm(o_bank, vt[:, j, 256 + 128 * br:384 + 128 * br], eT[:, 512 * j:512 * j + 512], False, lastmm,
                               tT, sig=(j == i))
                    et_free = t
                    yield
                spread(o_bank, 2, i, t, PB)

        t_g2 = []
        gate_main2 = gemm_f(w2in, [([(2128 + 256 * n, 256, 0)], [128, 128]) for n in range(12)], 8, evac_gate(gate2, t_g2), uT, t_u)

        def two(a, b):
            yield from a
            yield from b

        drive(gate_main2, two(stick(), dsa()), nsa())

        mT = view3(P + 17920, 8, 256)
        tm = [view3(P + 19968 + 512 * i, 2, 256) for i in range(4)]
        t_m = {}
        tmr = [None] * 4

        def evac_up(br):
            def f(bank, n, tok):
                g = gate2[:, 8 * br + 2 * n:8 * br + 2 * n + 2, :]
                m = mT[:, 2 * n:2 * n + 2, :]
                if br == 0:
                    t_m[n] = t = tt(V, m, halves(bank), g, ALU.mult, tok, t_g2)
                    return [t]
                t = tt(V, tm[n], halves(bank), g, ALU.mult, tok, tmr[n])
                t_m[n] = tmr[n] = tt(G, m, m, tm[n], ALU.add, t, t_m[n])
                return [t]
            return f

        for br in range(3):
            alone(gemm_f(A["w_up_2"][0, br], wide, 2, evac_up(br), oC[:, 2 * br:2 * br + 2, :], t_oc[br]))

        def add_h(got, done):
            for i in range(2):
                for n in range(2):
                    b, t, pool = got[i][n]
                    c = slice(512 * n, 512 * n + 512)
                    t = tt(V, H[:, i, c], H[:, i, c], b, ALU.add, t, done)
                    pool.put(b, t)
            return [t, t]

        got = alone(full(A["w_out_2"][0], mT, [t_m[n] for n in range(4)], 8, (PG, PA)))
        t_h = add_h(got, None)

        t_u = alone(norm_t(H, XN, "norm_mem_q_2", uT, t_h))
        mq = view3(P + 17920, 2, 256)
        oM = view3(P + 18432, 2, 256)
        t_mq = []

        def evac_mq(bank, n, tok):
            t_mq.append(cp(S, mq, halves(bank), tok))
            return [t_mq[-1]]

        alone(gemm_f(A["w_mem_q_2"][0], [([(0, 256, 0)], [128, 128])], 8, evac_mq, uT, t_u))
        t_om = []

        def mem_side(i):
            o = P + 11776 + 2048 * i
            E, eT = view3(o, 4, 256), view(o + 1024, 1024)
            nm, den, rden = small(4), small(4), small(4)
            zero = ca[:, 0:1].broadcast_to([128, 256])
            pool = (PA, PB)[i]
            banks = [pool.get() for _ in range(2)]
            te = []
            for par in range(2):
                half = slice(64 * par, 64 * par + 64)
                b, bt = banks[par]
                for hh in range(2):
                    t = mm(b[:, 256 * hh:256 * hh + 256], mq[half, hh, 128 * i:128 * i + 128], memK[half, hh, :], True, True,
                           t_mq, t_mk, bt, sig=True)
                for hh in range(2):
                    h = 2 * hh + par
                    free, t_ = softmax_e(E[:, h, :], [(b[:, 256 * hh:256 * hh + 256], zero, E[:, h, :])], nm[:, h:h + 1],
                                         den[:, h:h + 1], rden[:, h:h + 1], None, t)
                    te.append(t_)
                pool.put(b, free)
            yield
            _, tT = turn4(E, eT, 256, te, pool, None)
            yield
            e4 = eT.rearrange("p (j h t) -> p j h t", j=2, h=4)
            for par in range(2):
                half = slice(64 * par, 64 * par + 64)
                bank, bt = pool.get()
                for hh in range(2):
                    h = 2 * hh + par
                    for j in range(2):
                        t = mm(bank[half, 128 * hh:128 * hh + 128], memV[:, j, 64 * h:64 * h + 64], e4[:, j, h, :], j == 0, j == 1,
                               tT, t_mv, bt, sig=(j == 1))
                t = cp(S, oM[half, :, 128 * i:128 * i + 128], bank[half, 0:256].rearrange("p (h t) -> p h t", h=2), t)
                pool.put(bank, t)
                t_om.append(t)
            yield

        drive(mem_side(0), mem_side(1))
        got = alone(full(A["w_mem_o_2"][0], oM, t_om, 2, (PG, PA)))
        t_h = add_h(got, None)

        t_u = alone(norm_t(H, XN, "norm_ffn_2", uT, t_h))
        hid = view3(P + 11776, 22, 256)
        sl = [view(P + 256 * i, 256) for i in range(2)]
        slf = [None, None]
        t_hid = []

        def evac_swiglu(bank, n, tok):
            a, b = bank[:, 0:256], bank[:, 256:512]
            s_ = sl[n % 2]
            t = act(s_, a, ACT.Sigmoid, tok, slf[n % 2])
            t = tt(V, s_, s_, a, ALU.mult, t)
            t = tt(V, hid[:, n, :], s_, b, ALU.mult, t)
            slf[n % 2] = t
            if n % 2:
                t_hid.append(t)
            return [t]

        alone(gemm_f(A["w_ffn_in_2"][0], [([(128 * n, 128, 0), (2816 + 128 * n, 128, 128)], [128, 128]) for n in range(22)],
                     8, evac_swiglu, uT, t_u))
        got = alone(down(A["w_ffn_out_2"][0], hid, t_hid, 22))
        t_h = add_h(got, None)

        wn, slot, wt = wload([(lambda s: s[:, 0:1024], A["norm_final_2"].partition_broadcast(128))])
        s_out = sem("s_out")
        ss, rs = small(2), small(2)
        o_d = out[0].rearrange("(i p) d -> p i d", p=128)
        for i in range(2):
            t = act(XN[:, i, :], H[:, i, :], ACT.Square, t_h, accum=ss[:, i:i + 1])
            t = rstd(ss[:, i:i + 1], rs[:, i:i + 1], 1024, EPS, t)
            t = stt(XN[:, i, :], H[:, i, :], rs[:, i:i + 1], slot[:, 0:1024], ALU.mult, ALU.mult, t, wt)
            t_o = dma(SP, o_d[:, i, :], XN[:, i, :], s_out, t)
        SP.wait([t_o])

        block = ctx.enter_context(nc.Block())

        @block.sync
        def _(e):
            SP.run(e)

        @block.gpsimd
        def _(e):
            G.run(e)

        @block.scalar
        def _(e):
            S.run(e)

        @block.tensor
        def _(e):
            PE.run(e)

        @block.vector
        def _(e):
            V.run(e)


_INS = ['x', 'p', 'mix_pre_norm', 'w_in', 'rwkv_mu', 'rwkv_w0', 'rwkv_w2', 'rwkv_a0', 'rwkv_a2', 'rwkv_g2', 'rwkv_k_k',
        'rwkv_k_a', 'rwkv_r_k', 'rwkv_ln_w', 'rwkv_ln_b', 'w_attn_up', 'w_rwkv_up', 'w_out', 'mix_post_norm',
        'ffn_pre_norm', 'w_ff_in', 'w_ff_out', 'ffn_post_norm', 'w_ple', 'w_ple_gate', 'ple_post_norm', 'mem_2',
        'norm_mix_2', 'w_in_2', 'cmp_pos_k_2', 'cmp_w1_k_2', 'cmp_w2_k_2', 'cmp_pos_v_2', 'cmp_w1_v_2', 'cmp_w2_v_2',
        'w_up_2', 'w_out_2', 'norm_mem_q_2', 'norm_mem_kv_2', 'w_mem_q_2', 'w_mem_kv_2', 'w_mem_o_2', 'norm_ffn_2',
        'w_ffn_in_2', 'w_ffn_out_2', 'norm_final_2']


def kernel(**inputs):
    import numpy as _np
    import concourse.bacc as _bacc
    from concourse import mybir as _mybir
    from concourse.bass_utils import run_bass_kernel_spmd as _run

    nc = _bacc.Bacc("TRN2", target_bir_lowering=False, num_devices=1)
    arrays, args = {}, {}
    for name in _INS:
        a = _np.ascontiguousarray(inputs[name])
        arrays[f"in_{name}_dram"] = a
        args[name] = nc.dram_tensor(f"in_{name}_dram", a.shape, _mybir.dt.from_np(a.dtype), kind="ExternalInput").ap()
    c = shape_constants()
    arrays["consts_dram"] = c
    consts = nc.dram_tensor("consts_dram", c.shape, _mybir.dt.float32, kind="ExternalInput").ap()
    out = nc.dram_tensor("out_0_dram", (1, 256, 1024), _mybir.dt.float32, kind="ExternalOutput").ap()
    program(nc, args, consts, out)
    r = _run(nc, [arrays], core_ids=[0])
    return r.results[0]["out_0_dram"]
```

```python
from contextlib import ExitStack
import math

import numpy as np
import concourse.bass as bass
from concourse import mybir

F32 = mybir.dt.float32
F32R = mybir.dt.float32r
ALU = mybir.AluOpType
ACT = mybir.ActivationFunctionType
AX = mybir.AxisListType.X

NEG = -1e30
TAKEN = -3e38
EPS = 1e-6
GN_EPS = 64e-5
S0 = math.exp(-0.5)

C_ID, C_SU, C_IU, C_LI, C_ONE, C_BLK, C_ROT, C_M0, C_M0T = [128 * i for i in range(9)]
C_LV = 128 * 9
C_MA = C_LV + 768
C_CA = C_MA + 768
C_ST = C_CA + 256
C_CMA = C_ST + 384
C_CMM = C_CMA + 30
C_COS = C_CMM + 30
C_SIN = C_COS + 256
C_COSC = C_SIN + 256
C_SINC = C_COSC + 256
C_END = C_SINC + 256

VEC = [("mix_pre_norm", 8), ("rwkv_mu", 14), ("rwkv_w0", 4), ("rwkv_a0", 4), ("rwkv_k_k", 4), ("rwkv_k_a", 4),
       ("rwkv_r_k", 4), ("rwkv_ln_w", 4), ("rwkv_ln_b", 4), ("ffn_pre_norm", 8), ("norm_mix_2", 8),
       ("norm_mem_q_2", 8), ("norm_mem_kv_2", 8), ("norm_ffn_2", 8), ("pos", 32)]
VOFF = {}
for _name, _n in VEC:
    VOFF[_name] = sum(n for m, n in VEC[:len(VOFF)])


def shape_constants():
    c = np.zeros((128, C_END), np.float32)
    i = np.arange(128)
    r, s = i[:, None], i[None, :]
    c[:, C_ID:C_ID + 128] = r == s
    c[:, C_SU:C_SU + 128] = r < s
    c[:, C_IU:C_IU + 128] = r <= s
    c[:, C_LI:C_LI + 128] = r >= s
    c[:, C_ONE:C_ONE + 128] = 1
    c[:, C_BLK:C_BLK + 128] = r // 64 == s // 64
    same = r // 64 == s // 64
    c[:, C_ROT:C_ROT + 128] = (same & (r % 64 < 32) & (s % 64 == r % 64 + 32)) * 1.0 \
        - (same & (r % 64 >= 32) & (s % 64 == r % 64 - 32)) * 1.0
    for n in range(7):
        b = 1 << n
        m = (r // (2 * b) == s // (2 * b)) & (r // b % 2 == 1) & (s // b % 2 == 0)
        if n == 0:
            c[:, C_M0:C_M0 + 128] = m
            c[:, C_M0T:C_M0T + 128] = m.T
        else:
            c[:, C_LV + 128 * (n - 1):C_LV + 128 * n] = m | (r == s)
    for n, keep in enumerate([s >= r, s <= r, (r - s) % 4 == 0, ((r - s) % 4 == 0) & (s <= r),
                              (r - s) % 16 == 0, ((r - s) % 16 == 0) & (s <= r)]):
        c[:, C_MA + 128 * n:C_MA + 128 * (n + 1)] = np.where(keep, 0, NEG)
    c[:, C_CA + 128:C_CA + 256] = np.where(s <= r, 0, NEG)
    c[:, C_ST:C_ST + 128] = np.where(r < s, 0, NEG)
    c[:, C_ST + 256:C_ST + 384] = np.where(r < s, 0, NEG)
    n = np.arange(15)[None, :] * 16 + 31
    for t in range(2):
        keep = n <= r + 128 * t
        c[:, C_CMA + 15 * t:C_CMA + 15 * (t + 1)] = np.where(keep, 0, NEG)
        c[:, C_CMM + 15 * t:C_CMM + 15 * (t + 1)] = keep
    inv = np.float32(10000.0) ** (-np.arange(0, 64, 2, dtype=np.float32) / np.float32(64))
    ang = (np.arange(256, dtype=np.float32)[None, :] * inv[:, None]).astype(np.float32)
    cos, sin = np.cos(ang), np.sin(ang)
    c[:, C_COS:C_COS + 256] = np.tile(cos, (4, 1))
    c[:, C_SIN:C_SIN + 256] = np.tile(sin, (4, 1))
    c[0:64, C_COSC:C_COSC + 256] = np.tile(cos, (2, 1))
    c[64:128, C_COSC:C_COSC + 256] = 1
    c[0:64, C_SINC:C_SINC + 256] = np.tile(sin, (2, 1))
    return c


def vectors(inputs):
    v = np.zeros((128, 128), np.float32)
    for name, n in VEC[:-1]:
        a, o = np.asarray(inputs[name]).reshape(-1), VOFF[name]
        if name == "rwkv_mu":
            v[:, o:o + 12] = a[:1536].reshape(12, 128).T
            v[0:64, o + 12] = a[1536:1600]
            v[0:96, o + 13] = a[1600:1696]
        else:
            v[:, o:o + n] = a.reshape(n, 128).T
    o = VOFF["pos"]
    v[0:64, o:o + 32] = np.asarray(inputs["cmp_pos_k_2"])[0].T
    v[64:128, o:o + 32] = np.asarray(inputs["cmp_pos_v_2"])[0].T
    return v


def p_by_features(inputs):
    return np.ascontiguousarray(np.asarray(inputs["p"])[0, 0].T.reshape(2, 128, 256).transpose(1, 0, 2))


class Engine:

    def __init__(self, sem):
        self.sem, self.n, self.todo, self.seen = sem, 0, [], {}

    def wait(self, toks):
        for t in toks:
            if t is None or len(t) == 0:
                continue
            if isinstance(t, list) or not isinstance(t[0], str):
                self.wait(t)
            elif self.seen.get(t[0], 0) < t[2]:
                self.seen[t[0]] = t[2]
                self.todo.append(lambda e, t=t: e.wait_ge(t[1], t[2]))

    def __call__(self, fn, toks, signal=True):
        self.wait(toks)
        if signal:
            self.n += 1
            self.todo.append(lambda e: fn(e).then_inc(self.sem[1], 1))
            return (self.sem[0], self.sem[1], self.n)
        self.todo.append(fn)
        return None

    def run(self, e):
        for f in self.todo:
            f(e)


class Banks:

    def __init__(self, banks):
        self.free = [(b, None) for b in banks]

    def get(self):
        return self.free.pop(0)

    def put(self, bank, *toks):
        self.free.append((bank, list(toks)))


def program(nc, A, consts, vecs, pt, out):
    with ExitStack() as ctx:
        def sem(name):
            return (name, ctx.enter_context(nc.semaphore(name)))

        PSUM = ctx.enter_context(nc.psum_tensor("psum", [128, 8, 512], F32))
        NR = 6
        OR, OC = 0, NR * 2048
        OV = OC + C_END
        OS = OV + 128
        OU = OS + 512
        OPE = OU + 2048
        P = OPE + 2048
        PX = P + 11776
        NX = 19488
        arena = ctx.enter_context(nc.sbuf_tensor("arena", [128, PX], F32))

        PE, V, S, G = [Engine(sem(n)) for n in ("s_pe", "s_dve", "s_act", "s_pool")]
        SP = Engine(None)

        identb = ctx.enter_context(nc.sbuf_tensor("identb", [128, 128], mybir.dt.bfloat16))[:, :]
        phase = {}

        def enter_phase(name, n, nr=0):
            if phase:
                phase["stack"].close()
            st = phase["stack"] = ExitStack()
            phase["f"] = st.enter_context(nc.sbuf_tensor("p_" + name, [128, n], F32))
            if nr:
                phase["r"] = st.enter_context(nc.sbuf_tensor("r_" + name, [128, nr], F32R))

        ctx.callback(lambda: phase["stack"].close())
        enter_phase("a", NX)

        def view(off, n):
            if off >= PX:
                return phase["f"][:, off - PX:off - PX + n]
            assert off + n <= PX
            return arena[:, off:off + n]

        def view3(off, a, b):
            return view(off, a * b).rearrange("p (a b) -> p a b", a=a)

        def bc(ap, n):
            return ap.unsqueeze(2).broadcast_to([ap.shape[0], ap.shape[1], n])

        def rep(ap, n):
            return ap.unsqueeze(1).broadcast_to([ap.shape[0], n, ap.shape[1]])

        def tt(E, o, a, b, op, *toks):
            return E(lambda e: e.tensor_tensor(o, a, b, op), toks)

        def ts(E, o, a, s1, s2, op0, op1, *toks):
            if op1 is None:
                return E(lambda e: e.tensor_scalar(o, a, s1, None, op0), toks)
            return E(lambda e: e.tensor_scalar(o, a, s1, s2, op0, op1), toks)

        def stt(o, a, s, b, op0, op1, *toks):
            return V(lambda e: e.scalar_tensor_tensor(out=o, in0=a, scalar=s, in1=b, op0=op0, op1=op1), toks)

        def cp(E, o, a, *toks):
            if E is S:
                return S(lambda e: e.activation(o, a, ACT.Copy), toks)
            return E(lambda e: e.tensor_copy(o, a), toks)

        def act(o, a, f, *toks, bias=0.0, scale=1.0, accum=None):
            if accum is None:
                return S(lambda e: e.activation(o, a, f, bias=bias, scale=scale), toks)
            return S(lambda e: e.activation(o, a, f, bias=bias, scale=scale, accum_out=accum), toks)

        def red(o, a, op, *toks):
            return V(lambda e: e.tensor_reduce(o, a, AX, op), toks)

        def recip(o, a, *toks):
            return V(lambda e: e.reciprocal(o, a), toks)

        def mset(E, o, v, *toks):
            return E(lambda e: e.memset(o, v), toks)

        def mm(o, l, r, start, stop, *toks, sig=False):
            return PE(lambda e: e.matmul(o, l, r, start=start, stop=stop), toks, signal=sig)

        def tr(o, a, *toks, sig=False):
            n = a.shape[0]
            b = a.base_partition()
            idn = arena[b:b + n, OC + C_ID + b:OC + C_ID + b + n]
            return PE(lambda e: e.transpose(o, a, idn), toks, signal=sig)

        dma_count = {}

        def dma(E, o, a, sm, *toks):
            E.wait(toks)
            dma_count[sm[0]] = dma_count.get(sm[0], 0) + 16
            E.todo.append(lambda e: e.dma_start(o, a).then_inc(sm[1], 16))
            return (sm[0], sm[1], dma_count[sm[0]])

        small_at = [OS]

        def small(n):
            o = small_at[0]
            small_at[0] += n
            assert small_at[0] <= OU, "small"
            return arena[:, o:o + n]

        uT = view3(OU, 8, 256)
        ident = view(OC + C_ID, 128)

        def const(off, n):
            return arena[:, OC + off:OC + off + n]

        def vec(name, i, n=1, p=128):
            o = OV + VOFF[name] + i
            return arena[0:p, o:o + n]

        ring_sem = [sem(f"s_w{i}") for i in range(NR)]
        ring_free = [None] * NR
        ring_at = [0]

        def wload(pieces):
            n = ring_at[0] % NR
            ring_at[0] += 1
            slot = view(OR + 2048 * n, 2048)
            assert ring_free[n] != 0, "the slot is still in use"
            tok = None
            for put, src in pieces:
                tok = dma(SP, put(slot), src, ring_sem[n], ring_free[n])
            ring_free[n] = 0
            return n, slot, tok

        def wfree(n, *toks):
            ring_free[n] = list(toks)

        def wcols(W, c0, w, k0, nk, d0, width):
            src = W[128 * k0:128 * (k0 + nk), c0:c0 + w].rearrange("(k p) n -> p k n", p=128)
            return (lambda s: s[:, 0:nk * width].rearrange("p (k n) -> p k n", k=nk)[:, :, d0:d0 + w], src)

        PG = Banks([PSUM[:, i, :] for i in (0, 1)])
        PA = Banks([PSUM[:, i, :] for i in (2, 3, 4)])
        PB = Banks([PSUM[:, i, :] for i in (5, 6, 7)])

        class P4:
            @staticmethod
            def get():
                return (PG if PG.free else PA).get()

            @staticmethod
            def put(bank, *toks):
                (PG if len(PG.free) < 2 else PA).put(bank, *toks)


        def halves(bank):
            return bank.rearrange("p (a b) -> p a b", a=2)

        def quarters(bank):
            return bank.rearrange("p (a b) -> p a b", a=4)

        def gemm_f(W, plan, K, evac, rhs, dep, head=0, pool=None, mid=None):
            def load(n):
                wn, slot, wt = wload([wcols(W, c0, w, 0, K, d0, 256) for c0, w, d0 in plan[n][0]])
                return wn, slot[:, 0:K * 256].rearrange("p (k n) -> p k n", k=K), wt

            pool = pool or PG
            if head:
                got = []
                for n in range(head):
                    got.append((load(n), pool.get()))
                last = [None] * head
                for i in range(2):
                    for n in range(head):
                        (wn, w3, wt), (bank, bt) = got[n]
                        off = 0
                        for j, m in enumerate(plan[n][1]):
                            for k in range(K):
                                o = 256 * j + 128 * i
                                last[n] = mm(bank[0:m, o:o + 128], w3[:, k, off:off + m], rhs[:, k, 128 * i:128 * i + 128],
                                             k == 0, k == K - 1, dep[i], wt, bt, sig=(k == K - 1))
                            off += 128 if m == 128 else m
                            yield
                        if i == 1:
                            wfree(wn, last[n])
                            turn_waiting()
                            pool.put(bank, *evac(bank, n, last[n]))
                            if n == 0 and mid:
                                mid()
            for n in range(head, len(plan)):
                wn, w3, wt = load(n)
                bank, bt = pool.get()
                off = 0
                for j, m in enumerate(plan[n][1]):
                    for k in range(K):
                        t = mm(bank[0:m, 256 * j:256 * j + 256], w3[:, k, off:off + m], rhs[:, k, :], k == 0, k == K - 1,
                               dep, wt, bt, sig=(k == K - 1))
                        if K == 8 and k == 3:
                            turn_waiting()
                            yield
                    off += 128 if m == 128 else m
                    if j + 1 < len(plan[n][1]):
                        yield
                wfree(wn, t)
                pool.put(bank, *evac(bank, n, t))
                yield

        def gemm_t(slots, lhs, dep, banks, w, K):
            k = 0
            for pieces, nk in slots:
                wn, slot, wt = wload(pieces)
                w3 = slot[:, 0:nk * w].rearrange("p (k n) -> p k n", k=nk)
                for kk in range(nk):
                    for i in range(2):
                        b, bt = banks[i]
                        t = mm(b[:, 0:w], lhs[:, k, 128 * i:128 * i + 128], w3[:, kk, :], k == 0, k == K - 1,
                               dep, wt, bt, sig=(kk == nk - 1 and i == 1))
                    k += 1
                    if kk % 2 == 1:
                        turn_waiting()
                        yield
                wfree(wn, t)
            return t

        def rstd(ss, o, n, eps, *toks):
            t = ts(V, o, ss, 1.0 / n, eps, ALU.mult, ALU.add, *toks)
            return tt(G, o, o, mh.broadcast_to([128, o.shape[1]]), ALU.pow, t)

        def norm_x(i, src, xn, ss, rs, *toks):
            t = act(xn[:, i, :], src[:, i, :], ACT.Square, *toks, accum=ss)
            t = rstd(ss, rs, 1024, EPS, t)
            return ts(V, xn[:, i, :], src[:, i, :], rs, None, ALU.mult, None, t)

        def turn_x(i, x, gname, dst, t):
            last = []
            for b in range(2):
                bank, bt = PB.get()
                for c in range(4):
                    tp = tr(bank[:, 128 * c:128 * c + 128], x[:, i, 512 * b + 128 * c:512 * b + 128 * c + 128],
                            t, bt, sig=(c == 3))
                o = dst[:, 4 * b:4 * b + 4, 128 * i:128 * i + 128]
                if gname is None:
                    te = cp(S, o, quarters(bank), tp)
                else:
                    te = tt(V, o, quarters(bank), bc(vec(gname, 4 * b, 4), 128), ALU.mult, tp)
                PB.put(bank, te)
                last.append(te)
                yield
            return last

        def norm_t(i, src, xn, gname, dst, *toks):
            t = norm_x(i, src, xn, small(1), small(1), *toks)
            yield
            return (yield from turn_x(i, xn, gname, dst, t))

        def gain_load(gname, off, *toks):
            a = A[gname].rearrange("a n -> (a n)") if gname != "norm_final_2" else A[gname]
            dst = view(off, 1024)
            return dst, dma(SP, dst, a.partition_broadcast(128), sem("s_" + gname), toks)

        def post_norm(i, y, gain, h, hsrc, tmp, t, *toks):
            slot, wt = gain
            ss, rs = small(2), small(1)
            for n in range(2):
                tq = act(tmp[:, i, 512 * n:512 * n + 512], y[n], ACT.Square, t, accum=ss[:, n:n + 1])
            tq = tt(V, rs, ss[:, 0:1], ss[:, 1:2], ALU.add, tq)
            tq = rstd(rs, rs, 1024, EPS, tq)
            r = []
            for n in range(2):
                c = slice(512 * n, 512 * n + 512)
                r.append(stt(tmp[:, i, c], y[n], rs, slot[:, c], ALU.mult, ALU.mult, tq, wt))
            return tt(V, h[:, i, :], hsrc[:, i, :], tmp[:, i, :], ALU.add, r, toks), r

        def beside(main, side, lag):
            res = [None, None]
            live = [True, True]

            def step(q, g):
                if live[q]:
                    try:
                        next(g)
                    except StopIteration as e:
                        live[q], res[q] = False, e.value

            step(1, side)
            n = 0
            while live[0]:
                step(0, main)
                n += 1
                if n > lag:
                    step(1, side)
            while live[1]:
                step(1, side)
            return res

        waiting = []

        def turn_waiting():
            while waiting:
                alone(waiting.pop(0))

        def rope(bank, n, tok, dst, cos, sin, zs, t1, prev, done):
            t_z = cp(S, zs, halves(bank)[:, 0:n, :], tok, prev)
            t_c = tt(G, t1, zs, rep(cos, n), ALU.mult, t_z, prev)
            yield [t_z]
            b2, bt = PB.get()
            t_r = mm(b2[:, 0:256 * n], const(C_ROT, 128), zs, True, True, t_z, bt, sig=True)
            t_s = tt(V, dst, halves(b2)[:, 0:n, :], rep(sin, n), ALU.mult, t_r)
            PB.put(b2, t_s)
            done(tt(G, dst, dst, t1, ALU.add, t_s, t_c))

        def drive(main, *turns):
            turns, k, more = list(turns), 0, True
            while more or turns:
                if more:
                    try:
                        next(main)
                    except StopIteration:
                        more = False
                if turns:
                    g = turns[k % len(turns)]
                    try:
                        next(g)
                        k += 1
                    except StopIteration:
                        k %= len(turns)
                        turns = [x for x in turns[k:] + turns[:k] if x is not g]
                        k = 0

        def alone(g):
            while True:
                try:
                    next(g)
                except StopIteration as e:
                    return e.value

        s_i, s_c, s_x, s_v, s_p = sem("s_i"), sem("s_c"), [sem("s_x0"), sem("s_x1")], sem("s_v"), sem("s_p")
        mh = small(1)
        t_mh = mset(G, mh, -0.5)
        x_sb = view3(P + 24576, 2, 1024)
        xn = view3(P + 26624, 2, 1024)
        x_d = A["x"][0].rearrange("(i p) d -> p i d", p=128)
        pT = view3(P + 21504, 2, 256)
        t_p = dma(SP, pT, pt, s_p)
        ple_n, ple_w, t_pw = wload([wcols(A["w_ple"][0], 0, 1024, 0, 2, 0, 1024)])
        t_x = [dma(S, x_sb[:, i, :], x_d[:, i, :], s_x[i]) for i in range(2)]
        t_id = dma(S, const(0, 128), consts[:, 0:128], s_i)
        t_v = dma(S, view(OV, 128), vecs, s_v)
        t_c = dma(S, const(128, C_END - 128), consts[:, 128:C_END], s_c)
        omka = small(4)
        G.wait([t_mh])
        V.wait([t_v])
        t_omka = ts(V, omka, vec("rwkv_k_a", 0, 4), -1.0, 1.0, ALU.mult, ALU.add, t_v)

        pE = view3(OPE, 2, 1024)
        t_pe = []

        def ple_in():
            w3 = ple_w.rearrange("p (k n) -> p k n", k=2)
            for i in range(2):
                for n in range(2):
                    b, bt = PA.get()
                    for k in range(2):
                        t = mm(b, pT[:, k, 128 * i:128 * i + 128], w3[:, k, 512 * n:512 * n + 512], k == 0, k == 1, t_p, t_pw,
                               bt, sig=(k == 1))
                    t_pe.append(cp(S, pE[:, i, 512 * n:512 * n + 512], b, t))
                    PA.put(b, t_pe[-1])
                    yield
            wfree(ple_n, t)

        n0 = norm_t(0, x_sb, xn, "mix_pre_norm", uT, t_x[0])
        n1 = norm_t(1, x_sb, xn, "mix_pre_norm", uT, t_x[1])
        next(n0)
        next(n1)
        alone(ple_in())
        PE.wait([t_id])
        t_u = [alone(n0)]
        PE.wait([t_c])
        S.wait([t_v])

        R = P + 11776
        zm = view3(R, 14, 256)
        oE, oCS, oCSC, oQ, oQi, oQx, oA, oKK, oKM, oAR, oG, oBON, oVT, oBK = [
            P + 15360 + 1024 * i for i in range(10)] + [P + 26624, P + 27648, P + 28672, P + 29696]
        ZS = [view3(oQ + 514 * i, 2, 257) for i in range(2)]
        D = [view3(oQ + 1028 + 512 * i, 2, 256) for i in range(2)]
        t_zs0 = [mset(G, z[:, :, 0:1], 0.0) for z in ZS]
        w_in = A["w_in"][0]
        zprev = [None, None]
        t_zm = {}

        def evac_rwkv(bank, n, tok):
            b = n % 2
            z, d = ZS[b], D[b]
            if n < 6:
                ps = [(128, 0, 2)]
            else:
                ps = [(64, 0, 1), (96, 1, 1)]
            frees, last = [], None
            for p, j, m in ps:
                t1 = cp(S, z[0:p, j:j + m, 1:257], halves(bank)[0:p, j:j + m, :], tok, zprev[b], t_zs0)
                frees.append(t1)
                t2 = tt(G, d[0:p, j:j + m, :], z[0:p, j:j + m, 0:256], z[0:p, j:j + m, 1:257], ALU.subtract, t1, zprev[b])
                for q in range(m):
                    c = 2 * n + j + q
                    last = stt(zm[0:p, c, :], d[0:p, j + q, :], vec("rwkv_mu", c, 1, p), z[0:p, j + q, 1:257],
                               ALU.mult, ALU.add, t2)
                    t_zm[c] = last
            zprev[b] = last
            return frees

        B0 = 2304
        plan = [([(B0 + 256 * n, 256, 0)], [128, 128]) for n in range(6)]
        plan = plan[2:4] + plan[0:2] + plan[4:6]
        order = [2, 3, 0, 1, 4, 5]
        plan = [([(B0 + 1536, 160, 0)], [64, 96])] + plan
        order = [6] + order
        t_u.append([])

        def norm1():
            t_u[1] += yield from n1

        zg = gemm_f(w_in, plan, 8, lambda b, n, t: evac_rwkv(b, order[n], t), uT, t_u, head=2)
        nn = norm1()
        for _ in range(2):
            next(zg)
        alone(nn)
        alone(zg)
        V.wait([t_c])
        G.wait([t_c, t_v])

        lo_n, lo, t_lo = wload([
            (lambda s: s[0:32, 0:512], A["rwkv_w2"][0]), (lambda s: s[32:64, 0:512], A["rwkv_a2"][0]),
            (lambda s: s[0:96, 512:1024], A["rwkv_g2"][0])])

        o_attn = view3(P + 30720, 2, 256)
        o_rwkv = view3(P + 13824, 4, 256)

        t_idb = cp(V, identb, ident, t_c)

        E4, CS, CSC, Q4, Qi, Qx, A4, KK, KM = [view(o, 1024) for o in (oE, oCS, oCSC, oQ, oQi, oQx, oA, oKK, oKM)]
        G4, BON = view(oG, 1024), view(oBON, 1024)
        TMP = view(oBK, 1024)

        def v4(x):
            return x.rearrange("p (c t) -> p c t", c=4)

        def v42(x):
            return x.rearrange("p (c i t) -> p c i t", c=4, i=2)

        def v8(x):
            return x.rearrange("p (c t) -> p c t", c=8)

        AR = view(oAR, 2048).rearrange("p (c i w t) -> p c i w t", c=4, i=2, w=2)
        VT = view3(oVT, 2, 512)
        BK = view3(oBK, 2, 512)
        zr, zk, zv = zm[:, 0:4, :], zm[:, 4:8, :], zm[:, 8:12, :]
        zk_f = view(R + 1024, 1024)
        zv_f = view(R + 2048, 1024)

        def chunk_pairs(mk, ev, pool, *toks):
            for b in range(2):
                bank, bt = pool.get()
                for j in range(2):
                    t = mk(bank[:, 256 * j:256 * j + 256], 2 * b + j, bt, toks, j == 1)
                pool.put(bank, *ev(bank, b, t))
                yield

        rw = {}

        def rwkv_side():
            t_th = act(zm[0:32, 12, :], zm[0:32, 12, :], ACT.Tanh, t_zm[12])
            t_sg = act(zm[0:96, 13, :], zm[0:96, 13, :], ACT.Sigmoid, t_zm[13])
            onez = view(oVT, 1024)
            t_one = mset(G, onez, 1.0)
            t_one = mset(G, onez.rearrange("p (c t) -> p c t", c=8)[:, :, 0:1], 0.0, t_one)
            yield
            te = []

            def ev_w(bank, b, t):
                for j in range(2):
                    te.append(act(E4[:, 512 * b + 256 * j:512 * b + 256 * j + 256], bank[:, 256 * j:256 * j + 256],
                                  ACT.Sigmoid, t, bias=vec("rwkv_w0", 2 * b + j)))
                return [te[-1]]

            yield from chunk_pairs(lambda o, c, bt, tk, sg: mm(o, lo[0:32, 128 * c:128 * c + 128], zm[0:32, 12, :], True, True,
                                                               bt, tk, sig=sg), ev_w, PB, t_th, t_lo)
            ta = []

            def ev_a(bank, b, t):
                for j in range(2):
                    ta.append(act(A4[:, 512 * b + 256 * j:512 * b + 256 * j + 256], bank[:, 256 * j:256 * j + 256],
                                  ACT.Sigmoid, t, bias=vec("rwkv_a0", 2 * b + j)))
                return [ta[-1]]

            yield from chunk_pairs(lambda o, c, bt, tk, sg: mm(o, lo[32:64, 128 * c:128 * c + 128], zm[32:64, 12, :], True, True,
                                                               bt, tk, sig=sg), ev_a, PB, t_zm[12], t_lo)
            tg = []

            def ev_g(bank, b, t):
                tg.append(cp(S, G4[:, 512 * b:512 * b + 512], bank, t))
                return [tg[-1]]

            yield from chunk_pairs(lambda o, c, bt, tk, sg: mm(o, lo[0:96, 512 + 128 * c:512 + 128 * c + 128], zm[0:96, 13, :],
                                                               True, True, bt, tk, sig=sg), ev_g, PB, t_sg, t_lo)
            wfree(lo_n, (PE.sem[0], PE.sem[1], PE.n))
            t_cs = V(lambda e: e.tensor_tensor_scan(CS, onez, E4, 0.0, ALU.mult, ALU.add), [te, t_one])
            mid = v8(CS)[:, :, 63:64].broadcast_to([128, 8, 128])
            t_cc = tt(V, v8(CSC), v8(CS), mid, ALU.subtract, t_cs)
            fct = small(4)
            t_f = tt(V, fct.unsqueeze(2), v42(CSC)[:, :, 0, 127:128], v42(CS)[:, :, 1, 63:64], ALU.add, t_cc)
            t_qx = tt(G, Qx, CSC, E4, ALU.subtract, t_cc)
            t_q = act(Q4, CSC, ACT.Exp, t_cc, scale=-S0)
            t_qi = act(Qi, CSC, ACT.Exp, t_cc, scale=S0)
            t_qx = act(Qx, Qx, ACT.Exp, t_qx, scale=-S0)
            t_f = act(fct, fct, ACT.Exp, t_f, scale=-S0)
            zks = [t_zm[c] for c in range(12)]
            t_kk = tt(V, v4(KK), zk, bc(vec("rwkv_k_k", 0, 4), 256), ALU.mult, zks)
            t_k2 = tt(V, TMP, KK, KK, ALU.mult, t_kk)
            t_vt = []
            for i in range(2):
                bank, bt = PB.get()
                for c in range(4):
                    t = tr(bank[:, 128 * c:128 * c + 128], zm[:, 8 + c, 128 * i:128 * i + 128], bt, zks, sig=(c == 3))
                t = cp(S, VT[:, i, :], bank, t, t_cs)
                PB.put(bank, t)
                t_vt.append(t)
                yield
            yield
            yield
            tn = []

            def ev_n(bank, b, t):
                c = slice(512 * b, 512 * b + 512)
                t = ts(V, CS[:, c], bank, 1e-24, None, ALU.max, None, t)
                t2 = act(CS[:, c], CS[:, c], ACT.Sqrt, t)
                tn.append(recip(CS[:, c], CS[:, c], t2))
                return [t]

            yield from chunk_pairs(lambda o, c, bt, tk, sg: mm(o, const(C_BLK, 128), TMP[:, 256 * c:256 * c + 256], True, True,
                                                               bt, tk, sig=sg), ev_n, PB, t_k2, t_f)
            t_kn = tt(V, KK, KK, CS, ALU.mult, tn)
            for c in range(4):
                s = slice(256 * c, 256 * c + 256)
                t = ts(V, KM[:, s], A4[:, s], vec("rwkv_k_a", c), omka[:, c:c + 1], ALU.mult, ALU.add, ta, t_omka)
            t_km = tt(V, KM, KM, zk_f, ALU.mult, t)
            yield
            for c in range(4):
                t_ar = stt(AR[:, c, :, 0, :], v42(KK)[:, c], -1.0, v42(Qx)[:, c], ALU.mult, ALU.mult, t_kn, t_qx)
            t_b = tt(G, A4, A4, KK, ALU.mult, t_kn, t)
            t_b = tt(V, A4, A4, Qi, ALU.mult, t_b, t_qi)
            for c in range(4):
                t_r = tt(V, AR[:, c, :, 1, :], zm[:, c, :].rearrange("p (i t) -> p i t", i=2), v42(Q4)[:, c], ALU.mult, t_q)
            for c in range(4):
                t = stt(TMP[:, 256 * c:256 * c + 256], zm[:, c, :], vec("rwkv_r_k", c), KM[:, 256 * c:256 * c + 256],
                        ALU.mult, ALU.mult, t_km, tn)
            t_kt = tt(V, KM, KM, Qi, ALU.mult, t, t_qi)
            for _ in range(4):
                yield
            tb = []

            def ev_b(bank, b, t):
                c = slice(512 * b, 512 * b + 512)
                tb.append(tt(V, BON[:, c], bank, zv_f[:, c], ALU.mult, t))
                return [tb[-1]]

            yield from chunk_pairs(lambda o, c, bt, tk, sg: mm(o, const(C_BLK, 128), TMP[:, 256 * c:256 * c + 256], True, True,
                                                               bt, tk, sig=sg), ev_b, PB, t)
            t_bk = []
            for n, (src, tk) in enumerate(((A4, t_b), (KM, t_kt))):
                bank, bt = PB.get()
                for c in range(4):
                    t = tr(bank[:, 128 * c:128 * c + 128], src[:, 256 * c:256 * c + 128], bt, tk, sig=(c == 3))
                t = cp(S, BK[:, n, :], bank, t, tb)
                PB.put(bank, t)
                t_bk.append(t)
                yield
            H0 = view(R + 3072, 512).rearrange("p (c w v) -> p c w v", c=4, w=2)
            t_h0 = mset(G, view(R + 3072, 512), 0.0, t_ar, tg)
            chain_off = [(P + 15360, P + 16384, P + 17408, P + 17920, P + 18432),
                         (P + 18944, R, P + 19968, P + 20480, P + 20992)]
            RHS, U = view(oKK, 512), view(oKK + 512, 512)
            Y, YC = view(R + 1024, 512), view(R + 1536, 512)

            def h8(x):
                return x.rearrange("p (h v) -> p h v", h=8)

            for i in range(2):
                res = {}

                def chain(p):
                    half = slice(64 * p, 64 * p + 64)
                    LN, MN, Xa, Xt, T = [view(o, n) for o, n in zip(chain_off[p], (1024, 1024, 512, 512, 512))]
                    LN4, MN4 = [x.rearrange("p (c w t) -> p c w t", c=4, w=2) for x in (LN, MN)]
                    bt_ = v42(A4)[half, :, i, :]
                    kt_ = v42(KM)[half, :, i, :]
                    a_ = AR[half, :, i, :, :]
                    first = [t_ar, t_r, t_b, t_kt, rw.get("chain_free")]
                    msk = const(C_SU, 256).unsqueeze(1).broadcast_to([128, 2, 256])
                    for dst, src in ((LN, bt_), (MN, kt_)):
                        for b in range(2):
                            bank, bt = PB.get()
                            for j in range(2):
                                c = 2 * b + j
                                t = mm(bank[:, 256 * j:256 * j + 256], src[:, c, :], a_[:, c, :, :].rearrange("p w t -> p (w t)"),
                                       True, True, first, bt, sig=(j == 1))
                            t = tt(V, halves(dst[:, 512 * b:512 * b + 512]), halves(bank), msk, ALU.mult, t)
                            PB.put(bank, t)
                        t_dst = t
                        yield
                    bank, bt = PB.get()
                    for c in range(4):
                        t = mm(bank[:, 128 * c:128 * c + 128], a_[:, c, 0, :], bt_[:, c, :], True, True, bt, sig=(c == 3))
                    t = tt(V, quarters(Xa), quarters(bank), rep(const(C_M0, 128), 4), ALU.mult, t, first)
                    PB.put(bank, t)
                    tx = tt(G, quarters(Xa), quarters(Xa), rep(ident, 4), ALU.add, t)
                    t = tt(V, quarters(Xt), LN4[:, :, 0, :], rep(const(C_M0T, 128), 4), ALU.mult, t_dst)
                    txt = tt(G, quarters(Xt), quarters(Xt), rep(ident, 4), ALU.add, t)
                    yield
                    tmm = None
                    for lv in range(6):
                        bank, bt = PB.get()
                        mm(quarters(bank), identb, rep(identb, 4), True, False, bt, t_idb)
                        for c in range(4):
                            o = bank[:, 128 * c:128 * c + 128]
                            t = mm(o, LN4[:, c, 0, :], Xa[:, 128 * c:128 * c + 128], False, c == 3, tx, t_dst, sig=(c == 3))
                        tT = tt(V, quarters(T), quarters(bank), rep(const(C_LV + 128 * lv, 128), 4), ALU.mult, t, tmm)
                        PB.put(bank, tT)
                        yield
                        bank, bt = PB.get()
                        for c in range(4):
                            s = slice(128 * c, 128 * c + 128)
                            t = mm(bank[:, s], T[:, s], Xt[:, s], True, True, tT, txt, bt, sig=(c == 3))
                        if lv < 5:
                            bank2, bt = PB.get()
                            for c in range(4):
                                s = slice(128 * c, 128 * c + 128)
                                t2 = mm(bank2[:, s], Xt[:, s], T[:, s], True, True, tT, txt, bt, sig=(c == 3))
                            tmm = t2
                            txt = cp(S, Xt, bank, t2)
                            tx = cp(S, Xa, bank2, t2)
                            PB.put(bank2, tx)
                        else:
                            txt = cp(S, Xt, bank, t)
                        PB.put(bank, txt)
                        yield
                    res[p] = (LN4, MN4, Xt, [txt, t_dst])

                gs = [chain(0), chain(1)]
                while gs:
                    for g in list(gs):
                        try:
                            next(g)
                        except StopIteration:
                            gs.remove(g)
                    yield
                both = [res[0][3], res[1][3], t_vt]
                bank, bt = PB.get()
                for h in range(8):
                    c, p = h // 2, h % 2
                    o = bank[:, 64 * h:64 * h + 64]
                    t = mm(o, res[p][1][:, c, 0, :], VT[:, i, 64 * h:64 * h + 64], True, i == 0, both, bt, sig=(h == 7))
                    if i == 1:
                        t = mm(o, AR[:, c, 1, 0, :], H0[:, c, p, :], False, True, t_h0, sig=(h == 7))
                t = cp(V, RHS, bank, t, rw.get("rhs_free"))
                PB.put(bank, t)
                yield
                bank, bt = PB.get()
                for h in range(8):
                    c, p = h // 2, h % 2
                    t = mm(bank[:, 64 * h:64 * h + 64], res[p][2][:, 128 * c:128 * c + 128], RHS[:, 64 * h:64 * h + 64],
                           True, True, t, bt, sig=(h == 7))
                t_U = cp(V, U, bank, t)
                PB.put(bank, t_U)
                yield
                bank, bt = PB.get()
                for h in range(8):
                    c, p = h // 2, h % 2
                    s = slice(64 * h, 64 * h + 64)
                    mm(bank[:, s], res[p][0][:, c, 1, :], U[:, s], True, False, t_U, bt)
                    t = mm(bank[:, s], res[p][1][:, c, 1, :], VT[:, i, s], False, i == 0, sig=(h == 7))
                    if i == 1:
                        t = mm(bank[:, s], AR[:, c, 1, 1, :], H0[:, c, p, :], False, True, sig=(h == 7))
                rw["chain_free"] = t
                tY = cp(S, Y, bank, t, rw.get("y_free"))
                PB.put(bank, tY)
                if i == 0:
                    bank, bt = PB.get()
                    for h in range(8):
                        c, p = h // 2, h % 2
                        s = slice(64 * h, 64 * h + 64)
                        o = bank[64 * p:64 * p + 64, 64 * c:64 * c + 64]
                        mm(o, BK[:, 0, s], U[:, s], True, False, t_bk, bt)
                        t = mm(o, BK[:, 1, s], VT[:, 0, s], False, True, sig=(h == 7))
                    hb = bank[:, 0:256].rearrange("p (c v) -> p c v", c=4)
                    for p in range(2):
                        q = slice(64 * p, 64 * p + 64)
                        t_hh = tt(V, H0[q, :, p, :], hb[q], bc(fct[q, :], 64), ALU.mult, t, t_f, t_h0)
                    t_h0 = t_hh
                    PB.put(bank, t_hh)
                    rw["rhs_free"] = t
                mean, var = small(8), small(8)
                t = red(mean, h8(Y), ALU.add, tY)
                t = ts(V, mean, mean, 1.0 / 64, None, ALU.mult, None, t)
                t = tt(V, h8(Y), h8(Y), bc(mean, 64), ALU.subtract, t)
                t = act(YC, Y, ACT.Square, t)
                t = red(var, h8(YC), ALU.add, t)
                t = rstd(var, var, 64, GN_EPS, t)
                t = tt(V, h8(YC), h8(Y), bc(var, 64), ALU.mult, t)
                rw["y_free"] = t
                yield
                bank, bt = PB.get()
                for c in range(4):
                    tp = tr(bank[:, 128 * c:128 * c + 128], YC[:, 128 * c:128 * c + 128], t, bt, sig=(c == 3))
                for c in range(4):
                    t = act(o_rwkv[:, c, 128 * i:128 * i + 128], bank[:, 128 * c:128 * c + 128], ACT.Identity, tp, tb, t_vt,
                            scale=vec("rwkv_ln_w", c), bias=vec("rwkv_ln_b", c))
                PB.put(bank, t)
                rw["y_free"] = tp
                o_ = o_rwkv[:, :, 128 * i:128 * i + 128]
                t = tt(V, o_, o_, v4(BON)[:, :, 128 * i:128 * i + 128], ALU.add, t)
                t = tt(V, o_, o_, v4(G4)[:, :, 128 * i:128 * i + 128], ALU.mult, t, tg)
                yield
            rw["out"] = t

        qk = view3(P + 4096, 12, 256)
        vtok = view3(P + 7168, 2, 768)
        rz = [view3(P + 8704 + 1024 * i, 2, 256) for i in range(2)]
        rt = [view3(P + 9216 + 1024 * i, 2, 256) for i in range(2)]
        t_qk, rprev, t_vtok = [], [None, None], []

        def evac_qk(bank, n, tok):
            def done(t):
                rprev[n % 2] = t
                t_qk.append(t)
            g = rope(bank, 2, tok, qk[:, 2 * n:2 * n + 2, :], const(C_COS, 256), const(C_SIN, 256),
                     rz[n % 2], rt[n % 2], rprev[n % 2], done)
            waiting.append(g)
            return next(g)

        gates = view3(P, 16, 256)
        t_gate = []

        def evac_gate(dst, lst):
            def f(bank, n, tok):
                t = act(dst[:, 2 * n:2 * n + 2, :], halves(bank), ACT.Sigmoid, tok, t_v)
                lst.append(t)
                return [t]
            return f

        def qkv_main():
            yield from gemm_f(w_in, [([(256 * n, 256, 0)], [128, 128]) for n in range(6)], 8, evac_qk, uT, t_u)
            for c0, w in ((1536, 512), (2048, 256)):
                banks = [PG.get() for _ in range(2)]
                nk = 2048 // w
                slots = [([wcols(w_in, c0, w, k, nk, 0, w)], nk) for k in range(0, 8, nk)]
                t = yield from gemm_t(slots, uT, t_u, banks, w, 8)
                for i in range(2):
                    te = cp(S, vtok[:, i, c0 - 1536:c0 - 1536 + w], banks[i][0][:, 0:w], t)
                    PG.put(banks[i][0], te)
                    t_vtok.append(te)

        def softmax_e(e, pieces, nm, den, rden, gate, *toks):
            t = None
            for n, (ps, mask, dst) in enumerate(pieces):
                init = 3e38 if n == 0 else nm[:, n - 1:n]
                t = V(lambda e_, ps=ps, mask=mask, dst=dst, init=init, n=n: e_.tensor_tensor_reduce(
                    dst, ps, mask, -0.125, init, ALU.add, ALU.min, nm[:, n:n + 1]), [toks, t])
            free = t
            t = act(e, e, ACT.Exp, t, scale=-1.0, bias=nm[:, len(pieces) - 1:len(pieces)], accum=den)
            t = recip(rden, den, t)
            if gate is not None:
                t = tt(V, rden, rden, gate, ALU.mult, t)
            t = ts(V, e, e, rden, None, ALU.mult, None, t)
            return free, t

        def attn_side(par):
            sm = view(P + 8704 + 1536 * par, 768)
            eT = view(P + 8704 + 1536 * par + 768, 768)
            e_free = et_free = None
            half = slice(64 * par, 64 * par + 64)
            nm, den, rden = small(2), small(1), small(1)
            ma = const(C_MA, 768)
            for i in range(2):
                for hh in range(2):
                    h = 2 * hh + par
                    W = 128 * (i + 1)
                    banks = [PA.get() for _ in range(i + 1)]
                    for g in range(3):
                        b, bt = banks[(g * W) // 512]
                        o = (g * W) % 512
                        t = mm(b[:, o:o + W], qk[half, 2 * g + hh, 128 * i:128 * i + 128], qk[half, 6 + 2 * g + hh, 0:W],
                               True, True, t_qk, bt, sig=True)
                    if i == 0:
                        pieces = [(banks[0][0][:, 0:384].rearrange("p (g t) -> p g t", g=3),
                                   ma.rearrange("p (g w t) -> p g w t", g=3, w=2)[:, :, 1, :],
                                   sm[:, 0:384].rearrange("p (g t) -> p g t", g=3))]
                    else:
                        pieces = [(banks[0][0], ma[:, 0:512], sm[:, 0:512]), (banks[1][0][:, 0:256], ma[:, 512:768], sm[:, 512:768])]
                    free, te = softmax_e(sm[:, 0:3 * W], pieces, nm, den, rden, None, t, e_free, rprev)
                    for b, _ in banks:
                        PA.put(b, free)
                    yield
                    nb = 3 * (i + 1)
                    for b0 in range(0, nb, 4):
                        k = min(4, nb - b0)
                        bank, bt = PA.get()
                        for j in range(k):
                            t = tr(bank[:, 128 * j:128 * j + 128], sm[:, 128 * (b0 + j):128 * (b0 + j) + 128], te, bt, sig=(j == k - 1))
                        tT = cp(S, eT[:, 128 * b0:128 * (b0 + k)], bank[:, 0:128 * k], t, et_free, rprev)
                        PA.put(bank, tT)
                    e_free = t
                    yield
                    bank, bt = PA.get()
                    for n in range(nb):
                        g, j = n // (i + 1), n % (i + 1)
                        t = mm(bank[half, 0:128], vtok[:, j, 64 * (4 * g + h):64 * (4 * g + h) + 64], eT[:, 128 * n:128 * n + 128],
                               n == 0, n == nb - 1, tT, bt, t_vtok, sig=(n == nb - 1))
                    et_free = t
                    t = cp(S, o_attn[half, hh, 128 * i:128 * i + 128], bank[half, 0:128], t)
                    PA.put(bank, t)
                    rw.setdefault("attn", []).append(t)
                    yield

        side = rwkv_side()
        drive_live = [qkv_main(), side]
        drive_main = drive_live[0]
        while True:
            try:
                next(drive_main)
            except StopIteration:
                break
            try:
                next(side)
            except StopIteration:
                pass
        mT = view3(P + 4096, 8, 256)
        tm = [view3(P + 8704 + 512 * i, 2, 256) for i in range(4)]
        t_m = {}
        mfree = [None] * 4

        def evac_up1(bank, n, tok):
            t = tt(V, mT[:, 2 * n:2 * n + 2, :], halves(bank), gates[:, 2 * n:2 * n + 2, :], ALU.mult, tok, t_gate)
            t_m[n] = t
            return [t]

        def evac_up2(bank, n, tok):
            t = tt(V, tm[n], halves(bank), gates[:, 8 + 2 * n:10 + 2 * n, :], ALU.mult, tok, t_gate)
            t_m[n] = tt(G, mT[:, 2 * n:2 * n + 2, :], mT[:, 2 * n:2 * n + 2, :], tm[n], ALU.add, t, t_m[n])
            return [t]

        wide = [([(256 * n, 256, 0)], [128, 128]) for n in range(4)]

        def gates_up():
            yield from gemm_f(w_in, [([(4000 + 256 * n, 256, 0)], [128, 128]) for n in range(8)], 8, evac_gate(gates, t_gate), uT, t_u)
            while len(rw.get("attn", [])) < 8:
                yield
            yield from gemm_f(A["w_attn_up"][0], wide, 2, evac_up1, o_attn, rw["attn"])

        drive(gates_up(), side, attn_side(0), side, attn_side(1))
        alone(gemm_f(A["w_rwkv_up"][0], wide, 4, evac_up2, o_rwkv, rw["out"]))

        H = view3(P + 7168, 2, 1024)
        XN = view3(P + 9216, 2, 1024)

        def full(W, lhs, dep, K):
            slots = [wload([wcols(W, 512 * n, 512, k, min(4, K - k), 0, 512)]) for k in range(0, K, 4) for n in range(2)]

            def block(i):
                banks = [PG.get(), PA.get()]
                for q, (wn, slot, wt) in enumerate(slots):
                    n, k0 = q % 2, 4 * (q // 2)
                    nk = min(4, K - k0)
                    w3 = slot[:, 0:512 * nk].rearrange("p (k n) -> p k n", k=nk)
                    b, bt = banks[n]
                    for kk in range(nk):
                        k = k0 + kk
                        t = mm(b, lhs[:, k, 128 * i:128 * i + 128], w3[:, kk, :], k == 0, k == K - 1,
                               dep[i], wt, bt, sig=(kk == nk - 1))
                        if kk % 2:
                            yield
                    if i == 1:
                        wfree(wn, t)
                return [b for b, _ in banks], t
            return block(0), block(1)

        def unbank(y, *r):
            PG.put(y[0], r)
            PA.put(y[1], r)

        def seam(i, y, t, gain, hsrc, gname, *toks):
            th, r = post_norm(i, y, gain, H, hsrc, XN, t, *toks)
            unbank(y, r)
            if gname is None:
                yield
                return (yield from turn_x(i, H, None, uT, th)), th
            tn = norm_x(i, H, XN, small(1), small(1), th)
            yield
            return (yield from turn_x(i, XN, gname, uT, tn)), th

        def seam_add(i, y, t, gname, *toks):
            r = [tt(V, H[:, i, 512 * n:512 * n + 512], H[:, i, 512 * n:512 * n + 512], y[n], ALU.add, t, toks) for n in range(2)]
            unbank(y, r)
            tn = norm_x(i, H, XN, small(1), small(1), r)
            yield
            return (yield from turn_x(i, XN, gname, uT, tn)), r[1]

        def late(dep, hs, i, g):
            a, b = yield from g
            dep[i] += a
            hs[i].append(b)

        t_u, t_h = [[], []], [[], []]
        t_mm = [t_m[n] for n in range(4)]
        g0, g1 = full(A["w_out"][0], mT, [t_mm, t_mm], 8)
        xr = view3(P + 19968, 2, 1024)
        t_xr = dma(SP, xr, x_d, sem("s_xr"), rw["out"])
        g_mix, g_ffn, g_ple = [gain_load(n, P + o, rw["out"], [t_m[q] for q in range(4)])
                               for n, o in (("mix_post_norm", 0), ("ffn_post_norm", 1024), ("ple_post_norm", 2048))]
        gain = g_mix
        y0, t = alone(g0)
        (y1, t1), _ = beside(g1, late(t_u, t_h, 0, seam(0, y0, t, gain, xr, "ffn_pre_norm", t_xr, t_m[3])), 6)
        s1 = late(t_u, t_h, 1, seam(1, y1, t1, gain, xr, "ffn_pre_norm", t_xr, t_m[3]))

        enter_phase("b", 8192, NX - 8192)
        hid = view3(P + 11776, 32, 256)
        def split(o, x, n, *toks):
            hi, lo = (phase["r"][:, o + q * n:o + q * n + n] for q in range(2))
            t = cp(S, hi, x, *toks)
            return hi, lo, tt(V, lo, x, hi.bitcast(F32), ALU.subtract, t)

        def mm3(o, l, r, start, stop, *toks, sig=False):
            mm(o, l[0], r[0], start, False, *toks)
            mm(o, l[0], r[1], False, False)
            return mm(o, l[1], r[0], False, stop, sig=sig)

        class Ranges:

            def __init__(self, W, cols, dep, evac):
                self.W, self.cols, self.dep, self.evac = W, cols, dep, evac
                self.used, self.at, self.pieces = [None] * 3, 0, []

            def start(self):
                assert self.dep[0] and self.dep[1]
                self.u = [phase["r"][:, 2048 * q:2048 * q + 2048].rearrange("p (k t) -> p k t", k=8) for q in range(2)]
                self.tu = []
                for i in range(2):
                    hi, lo = (x[:, :, 128 * i:128 * i + 128] for x in self.u)
                    x = uT[:, :, 128 * i:128 * i + 128]
                    t = cp(S, hi, x, self.dep[i])
                    self.tu.append(tt(V, lo, x, hi.bitcast(F32), ALU.subtract, t))
                    self.prepare()

            def prepare(self):
                j = self.at
                if j == 4 * len(self.cols):
                    return
                self.at += 1
                if j % 2 == 0:
                    self.slot = wload([wcols(self.W, self.cols[j // 4], 512, 4 * (j // 2 % 2), 4, 0, 512)])
                wn, slot, wt = self.slot
                hi, lo, t = split(4096 + 2048 * (j % 3), slot[:, 1024 * (j % 2):1024 * (j % 2) + 1024], 1024, wt, self.used[j % 3])
                if j % 2:
                    wfree(wn, t)
                self.pieces.append((hi, lo, t))

            def run(self):
                for r in range(len(self.cols)):
                    banks = [P4.get() for _ in range(2)]
                    for c in range(4):
                        j = 4 * r + c
                        self.prepare()
                        hi, lo, tw = self.pieces[j]
                        for i in range(2):
                            a = slice(128 * i, 128 * i + 128)
                            for kk in range(2):
                                k, w = 2 * c + kk, slice(512 * kk, 512 * kk + 512)
                                t = mm3(banks[i][0], (self.u[0][:, k, a], self.u[1][:, k, a]), (hi[:, w], lo[:, w]), k == 0,
                                        k == 7, self.tu, tw, banks[i][1], sig=(kk == 1))
                            if c == 3:
                                P4.put(banks[i][0], *self.evac(r, i, banks[i][0], t))
                        self.used[j % 3] = t
                        if c == 1:
                            turn_waiting()
                        yield

        def to_hid(x, c0, i, t, frees):
            bank, bt = PB.get()
            for c in range(4):
                tp = tr(quarters(bank)[:, c, :], x[:, 128 * c:128 * c + 128], t, bt, sig=(c == 3))
            frees[:] = [tp]
            t = cp(S, hid[:, c0:c0 + 4, 128 * i:128 * i + 128], quarters(bank), tp)
            PB.put(bank, t)
            for q in range(2):
                t_hid[c0 // 2 + q].append(t)
            yield

        def ff_in(W, head, ranges, tail, n0, evac):
            yield from gemm_f(W, head, 8, evac, uT, t_u, head=4, pool=P4, mid=ranges.start)
            yield from ranges.run()
            yield from gemm_f(W, tail, 8, lambda b, n, t: evac(b, n0 + n, t), uT, t_u, pool=P4)

        t_hid = [[] for _ in range(16)]
        rl = [view3(P + 512 * i, 2, 256) for i in range(2)]
        rlf = [None, None]

        def evac_relu2(bank, n, tok):
            t = act(rl[n % 2], halves(bank), ACT.Relu, tok, rlf[n % 2])
            t2 = tt(V, hid[:, 2 * n:2 * n + 2, :], halves(bank), rl[n % 2], ALU.mult, t)
            rlf[n % 2] = t2
            t_hid[n].append(t2)
            return [t2]

        stage = [[view(P + 3072 + 1024 * r + 512 * i, 512) for i in range(2)] for r in range(2)]
        st_free = [[[], []], [[], []]]

        def evac_relu2_t(r, i, bank, tok):
            st, free = stage[r % 2][i], st_free[r % 2][i]
            t = act(st, bank, ACT.Relu, tok, free)
            t = tt(V, st, bank, st, ALU.mult, t)
            waiting.append(to_hid(st, 8 + 4 * r, i, t, free))
            return [t]

        cols = [([(256 * n, 256, 0)], [128, 128]) for n in range(16)]
        ra = Ranges(A["w_ff_in"][0], [1024 + 512 * r for r in range(5)], t_u, evac_relu2_t)
        beside(ff_in(A["w_ff_in"][0], cols[:4], ra, cols[14:], 14, evac_relu2), s1, 5)

        def down(W, lhs, dep, K, rfree):
            banks = [[PG.get(), PA.get()] for _ in range(2)]

            def part(i, k0, slot, wt):
                w3 = slot.rearrange("p (k n) -> p k n", k=2)
                for kk in range(2):
                    k = k0 + kk
                    for n in range(2):
                        b, bt = banks[i][n]
                        t = mm(b, lhs[:, k, 128 * i:128 * i + 128], w3[:, kk, 512 * n:512 * n + 512], k == 0, k == K - 1,
                               dep[k // 2], wt, bt, sig=(kk == 1 and n == 1))
                return t

            used = [rfree] * 4
            for k in range(K - 8):
                if k % 2 == 0:
                    wn, slot, wt = wload([wcols(W, 0, 1024, k, 2, 0, 1024)])
                o = 2560 * (k % 4)
                wh, wl, tw = split(o, slot[:, 1024 * (k % 2):1024 * (k % 2) + 1024], 1024, wt, used[k % 4])
                if k % 2:
                    wfree(wn, tw)
                ah, al, ta = split(o + 2048, lhs[:, k, :], 256, dep[k // 2])
                for i in range(2):
                    for n in range(2):
                        b, bt = banks[i][n]
                        c, a = slice(512 * n, 512 * n + 512), slice(128 * i, 128 * i + 128)
                        t = mm3(b, (ah[:, a], al[:, a]), (wh[:, c], wl[:, c]), k == 0, False, tw, ta, bt,
                                sig=(i == 1 and n == 1))
                used[k % 4] = t
            tail = [(k0, wload([wcols(W, 0, 1024, k0, 2, 0, 1024)])) for k0 in range(K - 8, K, 2)]
            for k0, (wn, slot, wt) in tail:
                t = part(0, k0, slot, wt)

            def second():
                for k0, (wn, slot, wt) in tail:
                    t = part(1, k0, slot, wt)
                    wfree(wn, t)
                    yield
                return [b for b, _ in banks[1]], t
            return [b for b, _ in banks[0]], t, second()

        t_hT, t_h = [[], []], [[], []]
        gain = g_ffn
        y0, t, g1 = down(A["w_ff_out"][0], hid, t_hid, 32, ra.used)
        (y1, t1), _ = beside(g1, late(t_hT, t_h, 0, seam(0, y0, t, gain, H, None)), 2)
        s1 = late(t_hT, t_h, 1, seam(1, y1, t1, gain, H, None))
        g0, g1 = full(A["w_ple_gate"][0], uT, t_hT, 8)
        (z0, t), _ = beside(g0, s1, 5)
        gain = g_ple
        t_u, t_h2 = [[], []], [[], []]

        def ple_seam(i, z, t):
            te = []
            for n in range(2):
                c = slice(512 * n, 512 * n + 512)
                ta = act(XN[:, i, c], z[n], ACT.Sigmoid, t, t_hT, t_h)
                te.append(tt(V, pE[:, i, c], pE[:, i, c], XN[:, i, c], ALU.mult, ta, t_pe))
            unbank(z, ta)
            th, _ = post_norm(i, [pE[:, i, 0:512], pE[:, i, 512:1024]], gain, H, H, XN, te, ta)
            tn = norm_x(i, H, XN, small(1), small(1), th)
            yield
            return (yield from turn_x(i, XN, "norm_mix_2", uT, tn)), th

        (z1, t1), _ = beside(g1, late(t_u, t_h2, 0, ple_seam(0, z0, t)), 7)
        s1 = late(t_u, t_h2, 1, ple_seam(1, z1, t1))

        enter_phase("c", NX)
        w2in = A["w_in_2"][0]
        gate2 = view3(P + 11776, 24, 256)
        RC = view3(P + 17920, 11, 256)
        QA = view3(P + 20736, 4, 256)
        vt = view3(P + 21760, 2, 660)
        memK = view3(P + 25128, 2, 256)
        memV = view3(P + 25640, 2, 256)
        rz = [view3(P + 23080 + 1024 * i, 2, 256) for i in range(2)]
        rt = [view3(P + 23592 + 1024 * i, 2, 256) for i in range(2)]
        oC = view3(P, 6, 256)
        t_rc, t_qa, rprev2 = {}, [], [None, None]
        t_vt2 = []

        def evac_a(bank, n, tok):
            if n < 2:
                t = cp(S, QA[:, 2 * n:2 * n + 2, :], halves(bank), tok)
                t_qa.append(t)
                return [t]
            m = 1 if n == 7 else 2
            c = 2 * (n - 2)
            cc, sc = (C_COSC, C_SINC) if n == 7 else (C_COS, C_SIN)

            def done(t):
                rprev2[n % 2] = t
                for j in range(m):
                    t_rc[c + j] = t
            g = rope(bank, m, tok, RC[:, c:c + m, :], const(cc, 256), const(sc, 256),
                     rz[n % 2][:, 0:m, :], rt[n % 2][:, 0:m, :], rprev2[n % 2], done)
            waiting.append(g)
            return next(g)

        dup = lambda c, d: [(c, 64, d), (c, 64, d + 64)]
        plan2 = [([(0, 256, 0)], [128, 128]), ([(256, 256, 0)], [128, 128]), ([(768, 256, 0)], [128, 128]),
                 ([(1152, 256, 0)], [128, 128]), ([(1476, 256, 0)], [128, 128]),
                 (dup(1024, 0) + dup(1408, 128), [128, 128]), (dup(1860, 0) + dup(1988, 128), [128, 128]),
                 ([(1732, 128, 0)], [128])]

        VP = [(512, 256, 0), (1088, 64, 256), (1924, 64, 320), (2052, 76, 384), (1472, 4, 460)]
        beside(gemm_f(w2in, plan2, 8, evac_a, uT, t_u, head=4, pool=P4), s1, 5)
        banks = [PG.get() for _ in range(2)]
        slots = [([wcols(w2in, c0, w, k, 4, d0, 464) for c0, w, d0 in VP], 4) for k in (0, 4)]
        t = alone(gemm_t(slots, uT, t_u, banks, 464, 8))
        wsc, g12 = small(8), small(24)
        for i in range(2):
            b = banks[i][0]
            fr = [cp(S, vt[:, i, 0:256], b[:, 0:256], t)]
            fr.append(act(g12[:, 12 * i:12 * i + 12], b[:, 448:460], ACT.Sigmoid, t))
            for d in range(2):
                fr.append(cp(V, vt[:, i, 256:640].rearrange("p (n d v) -> p n d v", n=3, d=2)[:, :, d, :],
                             b[:, 256:448].rearrange("p (n v) -> p n v", n=3), t, fr[1]))
            fr.append(ts(V, wsc[:, 4 * i:4 * i + 4], b[:, 460:464], 0.0625, None, ALU.mult, None, t))
            PG.put(b, fr)
            t_vt2 += fr

        t_oc = {0: [], 1: [], 2: []}

        def stick():
            Z = view(P + 26152, 1536)
            SPL = view(P + 27688, 1536)
            TM = view(P + 29224, 1536)
            z4 = Z.rearrange("p (h t) -> p h t", h=4)
            s4 = SPL.rearrange("p (h t) -> p h t", h=4)
            st = const(C_ST, 384)
            tz = []
            for par in range(2):
                half = slice(64 * par, 64 * par + 64)
                b0, bt0 = PA.get()
                b1, bt1 = PA.get()
                for hh in range(2):
                    kT = QA[half, 2 + hh, :]
                    qT = QA[half, hh, :]
                    mm(b0[:, 256 * hh:256 * hh + 256], kT[:, 0:128], qT[:, 0:256], True, True, t_qa, bt0)
                    t = mm(b1[:, 128 * hh:128 * hh + 128], kT[:, 128:256], qT[:, 128:256], True, True, bt1, sig=True)
                zz = z4[:, par::2, :]
                ta = stt(zz[:, :, 0:256], halves(b0), 0.125, rep(st[:, 0:256], 2), ALU.mult, ALU.add, t)
                tb_ = stt(zz[:, :, 256:384], b1[:, 0:256].rearrange("p (h t) -> p h t", h=2), 0.125, rep(st[:, 256:384], 2),
                          ALU.mult, ALU.add, t)
                PA.put(b0, ta)
                PA.put(b1, tb_)
                tz += [ta, tb_]
                yield
            t = act(TM, Z, ACT.Abs, tz)
            t = act(TM, TM, ACT.Exp, t, scale=-1.0)
            t = act(TM, TM, ACT.Ln, t, bias=1.0)
            t_sp = stt(SPL, Z, 0.0, TM, ALU.max, ALU.add, t)
            yield
            LI, ONE = const(C_LI, 128), const(C_ONE, 128)
            tw = []
            for hp in range(2):
                hs = slice(2 * hp, 2 * hp + 2)
                b0, bt0 = PA.get()
                for q in range(2):
                    h = 2 * hp + q
                    mm(b0[:, 256 * q:256 * q + 256], LI, s4[:, h, 0:256], True, False, t_sp, bt0)
                    t = mm(b0[:, 256 * q + 128:256 * q + 256], ONE, s4[:, h, 256:384], False, True, sig=True)
                ta = tt(V, z4[:, hs, 0:256], z4[:, hs, 0:256], halves(b0), ALU.subtract, t)
                PA.put(b0, ta)
                b1, bt1 = PA.get()
                for q in range(2):
                    t = mm(b1[:, 128 * q:128 * q + 128], LI, s4[:, 2 * hp + q, 256:384], True, True, bt1, sig=True)
                tb_ = tt(V, z4[:, hs, 256:384], z4[:, hs, 256:384], b1[:, 0:256].rearrange("p (h t) -> p h t", h=2), ALU.subtract, t)
                PA.put(b1, tb_)
                tw += [ta, tb_]
                yield
            tw = act(Z, Z, ACT.Exp, tw)
            yield
            for par in range(2):
                half = slice(64 * par, 64 * par + 64)
                b0, bt0 = PA.get()
                for hh in range(2):
                    h = 2 * hh + par
                    o = 256 * hh
                    mm(b0[half, o:o + 256], vt[:, 0, 64 * h:64 * h + 64], z4[:, h, 0:256], True, False, tw, t_vt2, bt0)
                    t = mm(b0[half, o + 128:o + 256], vt[:, 1, 64 * h:64 * h + 64], z4[:, h, 256:384], False, True, sig=True)
                t = cp(S, oC[half, 0:2, :], halves(b0)[half], t)
                PA.put(b0, t)
                t_oc[0].append(t)
                yield

        def scores4(i, qc, kc, W, pool, *toks):
            banks = [pool.get() for _ in range(2)]
            ts_ = []
            for par in range(2):
                half = slice(64 * par, 64 * par + 64)
                b, bt = banks[par]
                for hh in range(2):
                    t = mm(b[:, 256 * hh:256 * hh + W], RC[half, qc + hh, 128 * i:128 * i + 128], RC[half, kc, 0:W],
                           True, True, toks, bt, sig=True)
                ts_.append(t)
            return banks, ts_

        def turn4(E, eT, W, te, pool, et_free, toks=None):
            out_ = []
            for j in range(W // 128):
                bank, bt = pool.get()
                for h in range(4):
                    t = tr(bank[:, 128 * h:128 * h + 128], E[:, h, 128 * j:128 * j + 128], te, bt, sig=(h == 3))
                tc_ = cp(S, eT[:, 512 * j:512 * j + 512], bank, t, et_free)
                pool.put(bank, tc_)
                out_.append(tc_)
            return t, out_

        def spread(bank, br, i, t, pool):
            fr = []
            for par in range(2):
                half = slice(64 * par, 64 * par + 64)
                fr.append(cp(V, oC[half, 2 * br:2 * br + 2, 128 * i:128 * i + 128], quarters(bank)[half, par::2, :], t))
            pool.put(bank, fr)
            t_oc[br] += fr

        ca = const(C_CA, 256)

        def dsa():
            W0 = P + 1536
            rel = view3(W0, 4, 256)
            acc, wk, add = view(W0 + 1024, 256), view(W0 + 1280, 256), view(W0 + 1536, 256)
            m8 = view(W0 + 1792, 8)
            E = view3(W0 + 1856, 4, 256)
            eT = view(W0 + 2880, 1024)
            nm, den, rden = small(4), small(4), small(4)
            r_free = e_free = et_free = a_free = None
            kr = [t_rc[2], t_rc[3], t_rc[7]]
            ks = [t_rc[0], t_rc[1], t_rc[6]]
            for i in range(2):
                W = 128 * (i + 1)
                msk = ca[:, 256 - W:256]
                banks, t = scores4(i, 2, 7, W, PA, kr)
                tr_ = []
                for par in range(2):
                    b = banks[par][0]
                    t1 = act(rel[:, par::2, 0:W], halves(b)[:, :, 0:W], ACT.Relu, t[par], r_free)
                    PA.put(b, t1)
                    tr_.append(t1)
                src = msk
                for h in range(4):
                    ta = stt(acc[:, 0:W], rel[:, h, 0:W], wsc[:, 4 * i + h:4 * i + h + 1], src, ALU.mult, ALU.add,
                             tr_, t_vt2, None if h == 0 else ta)
                    src = acc[:, 0:W]
                r_free = ta
                yield
                cur = acc
                for r in range(8):
                    a, w = acc[:, 0:W], cur[:, 0:W]
                    t = V(lambda e, w=w: e.max(m8, w), [ta])
                    ta = V(lambda e, a=a, w=w: e.match_replace(a, m8, w, TAKEN), [t])
                    if r % 2:
                        yield
                t = ts(V, add[:, 0:W], acc[:, 0:W], TAKEN, NEG, ALU.is_gt, ALU.mult, ta)
                ta = tt(V, add[:, 0:W], add[:, 0:W], msk, ALU.add, t)
                banks, t = scores4(i, 0, 6, W, PA, ks)
                te = []
                for h in range(4):
                    b = banks[h % 2][0]
                    hh = h // 2
                    free, t_ = softmax_e(E[:, h, 0:W], [(b[:, 256 * hh:256 * hh + W], add[:, 0:W], E[:, h, 0:W])],
                                         nm[:, h:h + 1], den[:, h:h + 1], rden[:, h:h + 1], None, t, ta, e_free)
                    te.append(t_)
                    if hh == 1:
                        PA.put(b, free)
                yield
                e_free, tT = turn4(E, eT, W, te, PA, et_free)
                yield
                bank, bt = PA.get()
                for j in range(i + 1):
                    t = mm(bank, vt[:, j, 256:384], eT[:, 512 * j:512 * j + 512], j == 0, j == i, tT, t_vt2, bt, sig=(j == i))
                et_free = t
                spread(bank, 1, i, t, PA)
                yield

        def nsa():
            blk = view(P + 5300, 480)
            tokT = RC[:, 10, :]
            b3 = blk.rearrange("p (l n) -> p l n", l=32)
            tb_ = []
            for n in range(15):
                tb_.append(tt(G, b3[:, :, n], tokT[:, 16 * n:16 * n + 32], vec("pos", 0, 32), ALU.add, t_rc[10]))
            tb_ = [tb_[-1]]
            yield
            bk, btk = PB.get()
            bv, btv = PB.get()
            for s in range(2):
                w1 = [(lambda sl, q=q: sl[64 * q:64 * q + 64, :].rearrange("p (l n) -> p l n", l=16),
                       A[nm_][0][1024 * s:1024 * s + 1024, :].rearrange("(l d) n -> d l n", d=64))
                      for q, nm_ in enumerate(("cmp_w1_k_2", "cmp_w1_v_2"))]
                wn, slot, wt = wload(w1)
                w3 = slot.rearrange("p (l n) -> p l n", l=16)
                for q, (b, bt) in enumerate(((bk, btk), (bv, btv))):
                    half = slice(64 * q, 64 * q + 64)
                    for l in range(16):
                        t = mm(b[0:15, 0:128], b3[half, 16 * s + l, :], w3[half, l, :], s == 0 and l == 0, s == 1 and l == 15,
                               tb_, wt, bt, sig=(l == 15))
                    if q == 0:
                        t_k = t
                wfree(wn, t)
                yield
            hd = view3(P + 5780, 2, 128)
            tmp = view3(P + 6036, 2, 128)
            th = []
            for q, (b, t_) in enumerate(((bk, t_k), (bv, t))):
                x, y = hd[0:15, q, :], tmp[0:15, q, :]
                t1 = cp(V, x, b[0:15, 0:128], t_)
                PB.put(b, t1)
                t2 = tt(V, y, x, x, ALU.mult, t1)
                t2 = ts(V, y, y, 0.044715, 1.0, ALU.mult, ALU.add, t2)
                t2 = tt(V, y, y, x, ALU.mult, t2)
                t2 = act(y, y, ACT.Sigmoid, t2, scale=2.0 * math.sqrt(2.0 / math.pi))
                th.append(tt(V, x, x, y, ALU.mult, t2))
            yield
            bank, bt = PB.get()
            for q in range(2):
                t = tr(bank[:, 16 * q:16 * q + 15], hd[0:15, q, :], th[q], bt, sig=True)
            hT_ = view(P + 6292, 32)
            t1 = [cp(V, hT_[:, 16 * q:16 * q + 15], bank[:, 16 * q:16 * q + 15], t) for q in range(2)]
            PB.put(bank, *t1)
            wn, slot, wt = wload([(lambda s, o=o: s[:, o:o + 64], A[nm_][0])
                                  for o, nm_ in ((0, "cmp_w2_k_2"), (64, "cmp_w2_k_2"), (128, "cmp_w2_v_2"), (192, "cmp_w2_v_2"))])
            bank, bt = PB.get()
            t = mm(bank[:, 0:15], slot[:, 0:128], hT_[:, 0:15], True, True, t1, wt, bt, sig=True)
            t2 = mm(bank[0:15, 128:256], hT_[:, 16:31], slot[:, 128:256], True, True, sig=True)
            wfree(wn, t2)
            kc = view(P + 6324, 16)
            vc = view(P + 6340, 128)
            t_kc = cp(V, kc[:, 0:15], bank[:, 0:15], t2)
            t_vc = cp(V, vc[0:15, :], bank[0:15, 128:256], t2)
            PB.put(bank, t_kc, t_vc)
            yield
            E = view3(P + 9216, 4, 256)
            eT = view(P + 10240, 1024)
            EC = view(P + 6468, 60).rearrange("p (h n) -> p h n", h=4)
            eTc = view(P + 6528, 512)
            nm, den, rden = small(4), small(4), small(4)
            mx = small(4)
            e_free = et_free = ec_free = None
            for i in range(2):
                W = 128 * (i + 1)
                msk = ca[:, 256 - W:256]
                o_bank, obt = PB.get()
                sb_, sbt = PB.get()
                sb2, sbt2 = PB.get()
                for par, (b, bt) in enumerate(((sb_, sbt), (sb2, sbt2))):
                    half = slice(64 * par, 64 * par + 64)
                    for hh in range(2):
                        t = mm(b[:, 16 * hh:16 * hh + 15], RC[half, 4 + hh, 128 * i:128 * i + 128], kc[half, 0:15], True, True,
                               t_kc, t_rc[4], bt, sig=True)
                    b3_ = b[:, 0:32].rearrange("p (h n) -> p h n", h=2)[:, :, 0:15]
                    tc_ = stt(EC[:, par::2, :], b3_, 0.125, rep(const(C_CMA + 15 * i, 15), 2), ALU.mult, ALU.add, t, ec_free)
                    PB.put(b, tc_)
                t = red(mx, EC, ALU.max, tc_)
                t = tt(V, EC, EC, bc(mx, 15), ALU.subtract, t)
                t = act(EC, EC, ACT.Exp, t)
                t = tt(V, EC, EC, rep(const(C_CMM + 15 * i, 15), 4), ALU.mult, t)
                t = red(mx, EC, ALU.add, t)
                t = ts(V, mx, mx, 1e-30, None, ALU.max, None, t)
                t = recip(mx, mx, t)
                gi = g12[:, 12 * i:12 * i + 12].rearrange("p (h b) -> p h b", b=3)
                t = tt(V, mx, mx, gi[:, :, 0], ALU.mult, t, t_vt2)
                t_ec = tt(V, EC, EC, bc(mx, 15), ALU.mult, t)
                yield
                bank, bt = PB.get()
                for h in range(4):
                    t = tr(bank[0:15, 128 * h:128 * h + 128], EC[:, h, :], t_ec, bt, sig=(h == 3))
                ec_free = t
                t = cp(S, eTc[0:15, :], bank[0:15, :], t, et_free)
                PB.put(bank, t)
                mm(o_bank, vc[0:15, :], eTc[0:15, :], True, False, t, t_vc, obt)
                yield
                for br in (1, 2):
                    banks, t = scores4(i, 4, 7 + br, W, PB, t_rc[4], t_rc[7 + br])
                    te = []
                    for h in range(4):
                        b = banks[h % 2][0]
                        hh = h // 2
                        free, t_ = softmax_e(E[:, h, 0:W], [(b[:, 256 * hh:256 * hh + W], msk, E[:, h, 0:W])],
                                             nm[:, h:h + 1], den[:, h:h + 1], rden[:, h:h + 1], gi[:, h, br:br + 1],
                                             t, t_vt2, e_free)
                        te.append(t_)
                        if hh == 1:
                            PB.put(b, free)
                    yield
                    e_free, tT = turn4(E, eT, W, te, PB, et_free)
                    yield
                    for j in range(i + 1):
                        lastmm = br == 2 and j == i
                        t = mm(o_bank, vt[:, j, 256 + 128 * br:384 + 128 * br], eT[:, 512 * j:512 * j + 512], False, lastmm,
                               tT, sig=(j == i))
                    et_free = t
                    yield
                spread(o_bank, 2, i, t, PB)

        t_g2 = []
        gate_main2 = gemm_f(w2in, [([(2128 + 256 * n, 256, 0)], [128, 128]) for n in range(12)], 8, evac_gate(gate2, t_g2), uT, t_u)

        drive(gate_main2, dsa(), nsa(), stick())

        mT = view3(P + 17920, 8, 256)
        tm = [view3(P + 19968 + 512 * i, 2, 256) for i in range(4)]
        t_m = {}
        tmr = [None] * 4

        def evac_up(br):
            def f(bank, n, tok):
                g = gate2[:, 8 * br + 2 * n:8 * br + 2 * n + 2, :]
                m = mT[:, 2 * n:2 * n + 2, :]
                if br == 0:
                    t_m[n] = t = tt(V, m, halves(bank), g, ALU.mult, tok, t_g2)
                    return [t]
                t = tt(V, tm[n], halves(bank), g, ALU.mult, tok, tmr[n])
                t_m[n] = tmr[n] = tt(G, m, m, tm[n], ALU.add, t, t_m[n])
                return [t]
            return f

        for br in range(3):
            alone(gemm_f(A["w_up_2"][0, br], wide, 2, evac_up(br), oC[:, 2 * br:2 * br + 2, :], t_oc[br]))

        mem_sb = view3(P + 26152, 2, 1024)
        mem_n = view3(P + 28200, 2, 1024)
        memT = view3(P + 22016, 8, 256)
        s_m = sem("s_m")
        t_mem = dma(SP, mem_sb, A["mem_2"][0].rearrange("(i p) d -> p i d", p=128), s_m, t_oc[0], t_oc[1], t_oc[2])
        t_mT = [[], []]

        def mem_norm():
            for i in range(2):
                t_mT[i] += yield from norm_t(i, mem_sb, mem_n, "norm_mem_kv_2", memT, t_mem, t_oc[0], t_oc[1], t_oc[2])

        t_mm = [t_m[n] for n in range(4)]
        g0, g1 = full(A["w_out_2"][0], mT, [t_mm, t_mm], 8)
        (y0, t), _ = beside(g0, mem_norm(), 3)
        t_u, t_h = [[], []], [[], []]
        (y1, t1), _ = beside(g1, late(t_u, t_h, 0, seam_add(0, y0, t, "norm_mem_q_2", t_h2)), 6)
        s1 = late(t_u, t_h, 1, seam_add(1, y1, t1, "norm_mem_q_2", t_h2))
        t_mk, t_mv = [], []

        def evac_mk(bank, n, tok):
            t_mk.append(cp(S, memK, halves(bank), tok))
            return [t_mk[-1]]

        w_kv = A["w_mem_kv_2"][0]

        def mem_kv():
            yield from gemm_f(w_kv, [([(0, 256, 0)], [128, 128])], 8, evac_mk, memT, t_mT)

        def mem_v():
            banks = [PG.get() for _ in range(2)]
            t = yield from gemm_t([([wcols(w_kv, 256, 256, 0, 8, 0, 256)], 8)], memT, t_mT, banks, 256, 8)
            for i in range(2):
                t_mv.append(cp(S, memV[:, i, :], banks[i][0][:, 0:256], t))
                PG.put(banks[i][0], t_mv[-1])

        beside(mem_kv(), s1, 5)
        mq = view3(P + 17920, 2, 256)
        oM = view3(P + 18432, 2, 256)
        t_mq = []

        def evac_mq(bank, n, tok):
            t_mq.append(cp(S, mq, halves(bank), tok))
            return [t_mq[-1]]

        alone(gemm_f(A["w_mem_q_2"][0], [([(0, 256, 0)], [128, 128])], 8, evac_mq, uT, t_u))
        t_om = []

        def mem_side(i):
            o = P + 11776 + 2048 * i
            E, eT = view3(o, 4, 256), view(o + 1024, 1024)
            nm, den, rden = small(4), small(4), small(4)
            zero = ca[:, 0:1].broadcast_to([128, 256])
            pool = (PA, PB)[i]
            banks = [pool.get() for _ in range(2)]
            te = []
            for par in range(2):
                half = slice(64 * par, 64 * par + 64)
                b, bt = banks[par]
                for hh in range(2):
                    t = mm(b[:, 256 * hh:256 * hh + 256], mq[half, hh, 128 * i:128 * i + 128], memK[half, hh, :], True, True,
                           t_mq, t_mk, bt, sig=True)
                for hh in range(2):
                    h = 2 * hh + par
                    free, t_ = softmax_e(E[:, h, :], [(b[:, 256 * hh:256 * hh + 256], zero, E[:, h, :])], nm[:, h:h + 1],
                                         den[:, h:h + 1], rden[:, h:h + 1], None, t)
                    te.append(t_)
                pool.put(b, free)
            yield
            _, tT = turn4(E, eT, 256, te, pool, None)
            yield
            e4 = eT.rearrange("p (j h t) -> p j h t", j=2, h=4)
            for par in range(2):
                half = slice(64 * par, 64 * par + 64)
                bank, bt = pool.get()
                for hh in range(2):
                    h = 2 * hh + par
                    for j in range(2):
                        t = mm(bank[half, 128 * hh:128 * hh + 128], memV[:, j, 64 * h:64 * h + 64], e4[:, j, h, :], j == 0, j == 1,
                               tT, t_mv, bt, sig=(j == 1))
                t = cp(S, oM[half, :, 128 * i:128 * i + 128], bank[half, 0:256].rearrange("p (h t) -> p h t", h=2), t)
                pool.put(bank, t)
                t_om.append(t)
            yield

        m0, m1 = mem_side(0), mem_side(1)
        next(m0)
        next(m1)
        alone(mem_v())
        drive(m0, m1)
        t_u, t_h2 = [[], []], [[], []]
        g0, g1 = full(A["w_mem_o_2"][0], oM, [t_om, t_om], 2)
        y0, t = alone(g0)
        (y1, t1), _ = beside(g1, late(t_u, t_h2, 0, seam_add(0, y0, t, "norm_ffn_2", t_h)), 99)
        s1 = late(t_u, t_h2, 1, seam_add(1, y1, t1, "norm_ffn_2", t_h))

        enter_phase("e", 5632, NX - 5632)
        hid = view3(P + 11776, 22, 256)
        t_hid = [[] for _ in range(11)]
        sl = [view(P + 2048 + 256 * i, 256) for i in range(2)]
        slf = [None, None]

        def evac_swiglu(bank, n, tok):
            a, b = bank[:, 0:256], bank[:, 256:512]
            s_ = sl[n % 2]
            t = act(s_, a, ACT.Sigmoid, tok, slf[n % 2])
            t = tt(V, s_, s_, a, ALU.mult, t)
            t = tt(V, hid[:, n, :], s_, b, ALU.mult, t)
            slf[n % 2] = t
            t_hid[n // 2].append(t)
            return [t]

        stage2 = [[view(P + 1024 * r + 512 * i, 512) for i in range(2)] for r in range(2)]
        st_free2 = [[[], []], [[], []]]
        t_a = {}

        def evac_swiglu_t(r, i, bank, tok):
            q = r // 2
            st, free = stage2[q % 2][i], st_free2[q % 2][i]
            if r % 2 == 0:
                t = act(st, bank, ACT.Sigmoid, tok, free)
                t_a[i] = tt(V, st, bank, st, ALU.mult, t)
                return [t_a[i]]
            t = tt(V, st, bank, st, ALU.mult, tok, t_a[i])
            waiting.append(to_hid(st, 4 + 4 * q, i, t, free))
            return [t]

        cols = [([(128 * n, 128, 0), (2816 + 128 * n, 128, 128)], [128, 128]) for n in range(22)]
        rb = Ranges(A["w_ffn_in_2"][0], [512 + 512 * q + 2816 * h for q in range(4) for h in range(2)], t_u, evac_swiglu_t)
        beside(ff_in(A["w_ffn_in_2"][0], cols[:4], rb, cols[20:], 20, evac_swiglu), s1, 5)
        gain = gain_load("norm_final_2", P + 4096, t_h2)
        y0, t, g1 = down(A["w_ffn_out_2"][0], hid, t_hid, 22, rb.used)

        s_out = sem("s_out")
        o_d = out[0].rearrange("(i p) d -> p i d", p=128)

        def final(i, y, t):
            ss, rs = small(1), small(1)
            r = [tt(V, H[:, i, 512 * n:512 * n + 512], H[:, i, 512 * n:512 * n + 512], y[n], ALU.add, t, t_h2) for n in range(2)]
            t = act(XN[:, i, :], H[:, i, :], ACT.Square, r, accum=ss)
            t = rstd(ss, rs, 1024, EPS, t)
            t = stt(XN[:, i, :], H[:, i, :], rs, gain[0], ALU.mult, ALU.mult, t, gain[1])
            return dma(SP, o_d[:, i, :], XN[:, i, :], s_out, t)

        final(0, y0, t)
        y1, t1 = alone(g1)
        SP.wait([final(1, y1, t1)])

        block = ctx.enter_context(nc.Block())

        @block.sync
        def _(e):
            SP.run(e)

        @block.gpsimd
        def _(e):
            G.run(e)

        @block.scalar
        def _(e):
            S.run(e)

        @block.tensor
        def _(e):
            PE.run(e)

        @block.vector
        def _(e):
            V.run(e)


_INS = ['x', 'p', 'mix_pre_norm', 'w_in', 'rwkv_mu', 'rwkv_w0', 'rwkv_w2', 'rwkv_a0', 'rwkv_a2', 'rwkv_g2', 'rwkv_k_k',
        'rwkv_k_a', 'rwkv_r_k', 'rwkv_ln_w', 'rwkv_ln_b', 'w_attn_up', 'w_rwkv_up', 'w_out', 'mix_post_norm',
        'ffn_pre_norm', 'w_ff_in', 'w_ff_out', 'ffn_post_norm', 'w_ple', 'w_ple_gate', 'ple_post_norm', 'mem_2',
        'norm_mix_2', 'w_in_2', 'cmp_pos_k_2', 'cmp_w1_k_2', 'cmp_w2_k_2', 'cmp_pos_v_2', 'cmp_w1_v_2', 'cmp_w2_v_2',
        'w_up_2', 'w_out_2', 'norm_mem_q_2', 'norm_mem_kv_2', 'w_mem_q_2', 'w_mem_kv_2', 'w_mem_o_2', 'norm_ffn_2',
        'w_ffn_in_2', 'w_ffn_out_2', 'norm_final_2']


def kernel(**inputs):
    import numpy as _np
    import concourse.bacc as _bacc
    from concourse import mybir as _mybir
    from concourse.bass_utils import run_bass_kernel_spmd as _run

    nc = _bacc.Bacc("TRN2", target_bir_lowering=False, num_devices=1)
    arrays, args = {}, {}
    for name in _INS:
        a = _np.ascontiguousarray(inputs[name])
        arrays[f"in_{name}_dram"] = a
        args[name] = nc.dram_tensor(f"in_{name}_dram", a.shape, _mybir.dt.from_np(a.dtype), kind="ExternalInput").ap()
    c = shape_constants()
    arrays["consts_dram"] = c
    consts = nc.dram_tensor("consts_dram", c.shape, _mybir.dt.float32, kind="ExternalInput").ap()
    out = nc.dram_tensor("out_0_dram", (1, 256, 1024), _mybir.dt.float32, kind="ExternalOutput").ap()
    arrays["vecs_dram"], arrays["pt_dram"] = vectors(inputs), p_by_features(inputs)
    vecs = nc.dram_tensor("vecs_dram", (128, 128), _mybir.dt.float32, kind="ExternalInput").ap()
    pt = nc.dram_tensor("pt_dram", (128, 2, 256), _mybir.dt.float32, kind="ExternalInput").ap()
    program(nc, args, consts, vecs, pt, out)
    r = _run(nc, [arrays], core_ids=[0])
    return r.results[0]["out_0_dram"]
```

```python
from contextlib import ExitStack
import math

import numpy as np
import concourse.bass as bass
from concourse import mybir

F32 = mybir.dt.float32
F32R = mybir.dt.float32r
ALU = mybir.AluOpType
ACT = mybir.ActivationFunctionType
AX = mybir.AxisListType.X

NEG = -1e30
TAKEN = -3e38
EPS = 1e-6
GN_EPS = 64e-5
S0 = math.exp(-0.5)

C_ID, C_SU, C_IU, C_LI, C_ONE, C_BLK, C_ROT, C_M0, C_M0T = [128 * i for i in range(9)]
C_LV = 128 * 9
C_MA = C_LV + 768
C_CA = C_MA + 768
C_ST = C_CA + 256
C_CMA = C_ST + 384
C_CMM = C_CMA + 30
C_COS = C_CMM + 30
C_SIN = C_COS + 256
C_COSC = C_SIN + 256
C_SINC = C_COSC + 256
C_END = C_SINC + 256

VEC = [("mix_pre_norm", 8), ("rwkv_mu", 14), ("rwkv_w0", 4), ("rwkv_a0", 4), ("rwkv_k_k", 4), ("rwkv_k_a", 4),
       ("rwkv_r_k", 4), ("rwkv_ln_w", 4), ("rwkv_ln_b", 4), ("ffn_pre_norm", 8), ("norm_mix_2", 8),
       ("norm_mem_q_2", 8), ("norm_mem_kv_2", 8), ("norm_ffn_2", 8), ("pos", 32)]
VOFF = {}
for _name, _n in VEC:
    VOFF[_name] = sum(n for m, n in VEC[:len(VOFF)])


def shape_constants():
    c = np.zeros((128, C_END), np.float32)
    i = np.arange(128)
    r, s = i[:, None], i[None, :]
    c[:, C_ID:C_ID + 128] = r == s
    c[:, C_SU:C_SU + 128] = r < s
    c[:, C_IU:C_IU + 128] = r <= s
    c[:, C_LI:C_LI + 128] = r >= s
    c[:, C_ONE:C_ONE + 128] = 1
    c[:, C_BLK:C_BLK + 128] = r // 64 == s // 64
    same = r // 64 == s // 64
    c[:, C_ROT:C_ROT + 128] = (same & (r % 64 < 32) & (s % 64 == r % 64 + 32)) * 1.0 \
        - (same & (r % 64 >= 32) & (s % 64 == r % 64 - 32)) * 1.0
    for n in range(7):
        b = 1 << n
        m = (r // (2 * b) == s // (2 * b)) & (r // b % 2 == 1) & (s // b % 2 == 0)
        if n == 0:
            c[:, C_M0:C_M0 + 128] = m
            c[:, C_M0T:C_M0T + 128] = m.T
        else:
            c[:, C_LV + 128 * (n - 1):C_LV + 128 * n] = m | (r == s)
    for n, keep in enumerate([s >= r, s <= r, (r - s) % 4 == 0, ((r - s) % 4 == 0) & (s <= r),
                              (r - s) % 16 == 0, ((r - s) % 16 == 0) & (s <= r)]):
        c[:, C_MA + 128 * n:C_MA + 128 * (n + 1)] = np.where(keep, 0, NEG)
    c[:, C_CA + 128:C_CA + 256] = np.where(s <= r, 0, NEG)
    c[:, C_ST:C_ST + 128] = np.where(r < s, 0, NEG)
    c[:, C_ST + 256:C_ST + 384] = np.where(r < s, 0, NEG)
    n = np.arange(15)[None, :] * 16 + 31
    for t in range(2):
        keep = n <= r + 128 * t
        c[:, C_CMA + 15 * t:C_CMA + 15 * (t + 1)] = np.where(keep, 0, NEG)
        c[:, C_CMM + 15 * t:C_CMM + 15 * (t + 1)] = keep
    inv = np.float32(10000.0) ** (-np.arange(0, 64, 2, dtype=np.float32) / np.float32(64))
    ang = (np.arange(256, dtype=np.float32)[None, :] * inv[:, None]).astype(np.float32)
    cos, sin = np.cos(ang), np.sin(ang)
    c[:, C_COS:C_COS + 256] = np.tile(cos, (4, 1))
    c[:, C_SIN:C_SIN + 256] = np.tile(sin, (4, 1))
    c[0:64, C_COSC:C_COSC + 256] = np.tile(cos, (2, 1))
    c[64:128, C_COSC:C_COSC + 256] = 1
    c[0:64, C_SINC:C_SINC + 256] = np.tile(sin, (2, 1))
    return c


def vectors(inputs):
    v = np.zeros((128, 128), np.float32)
    for name, n in VEC[:-1]:
        a, o = np.asarray(inputs[name]).reshape(-1), VOFF[name]
        if name == "rwkv_mu":
            v[:, o:o + 12] = a[:1536].reshape(12, 128).T
            v[0:64, o + 12] = a[1536:1600]
            v[0:96, o + 13] = a[1600:1696]
        else:
            v[:, o:o + n] = a.reshape(n, 128).T
    o = VOFF["pos"]
    v[0:64, o:o + 32] = np.asarray(inputs["cmp_pos_k_2"])[0].T
    v[64:128, o:o + 32] = np.asarray(inputs["cmp_pos_v_2"])[0].T
    return v


def p_by_features(inputs):
    return np.ascontiguousarray(np.asarray(inputs["p"])[0, 0].T.reshape(2, 128, 256).transpose(1, 0, 2))


class Engine:

    def __init__(self, sem):
        self.sem, self.n, self.todo, self.seen = sem, 0, [], {}

    def wait(self, toks):
        for t in toks:
            if t is None or len(t) == 0:
                continue
            if isinstance(t, list) or not isinstance(t[0], str):
                self.wait(t)
            elif self.seen.get(t[0], 0) < t[2]:
                self.seen[t[0]] = t[2]
                self.todo.append(lambda e, t=t: e.wait_ge(t[1], t[2]))

    def __call__(self, fn, toks, signal=True):
        self.wait(toks)
        if signal:
            self.n += 1
            self.todo.append(lambda e: fn(e).then_inc(self.sem[1], 1))
            return (self.sem[0], self.sem[1], self.n)
        self.todo.append(fn)
        return None

    def run(self, e):
        for f in self.todo:
            f(e)


class Banks:

    def __init__(self, banks):
        self.free = [(b, None) for b in banks]

    def get(self):
        return self.free.pop(0)

    def put(self, bank, *toks):
        self.free.append((bank, list(toks)))


def program(nc, A, consts, vecs, pt, out):
    with ExitStack() as ctx:
        def sem(name):
            return (name, ctx.enter_context(nc.semaphore(name)))

        PSUM = ctx.enter_context(nc.psum_tensor("psum", [128, 8, 512], F32))
        NR = 6
        OR, OC = 0, NR * 2048
        OV = OC + C_END + 4
        OS = OV + 128
        OU = OS + 512
        OPE = OU + 2048
        P = OPE + 2048
        PE, V, S, G = [Engine(sem(n)) for n in ("s_pe", "s_dve", "s_act", "s_pool")]
        SP = Engine(None)
        assert P % 8 == 0
        PARTS = [(OR + 2048 * n, 2048) for n in range(NR)] + [
            (OU, 2048), (P + 1536, 4096), (P + 3072, 3840), (P + 5120, 2048), (P + 11776, 8192), (P + 15360, 8192),
            (P + 17408, 10240), (P + 19968, 10240), (P + 25600, 4096), (P + 26152, 4096)]
        parts_mem = []
        for n, (off, size) in enumerate(PARTS):
            with ExitStack() as st:
                if off:
                    st.enter_context(nc.sbuf_tensor(f"before{n}", [128, off], F32))
                parts_mem.append(st.enter_context(nc.sbuf_tensor(f"parts{n}", [128, size], F32R)))
        low = ctx.enter_context(nc.sbuf_tensor("low", [128, P], F32))
        mid_ = ctx.enter_context(nc.sbuf_tensor("mid", [128, 11776], F32))
        high = ctx.enter_context(nc.sbuf_tensor("high", [128, 19488], F32))
        identb = ctx.enter_context(nc.sbuf_tensor("identb", [128, 128], mybir.dt.bfloat16))[:, :]

        def view(off, n):
            for x, a, b in ((low, 0, P), (mid_, P, P + 11776), (high, P + 11776, P + 31264)):
                if a <= off and off + n <= b:
                    return x[:, off - a:off - a + n]
            assert False, (off, n)

        def view3(off, a, b):
            return view(off, a * b).rearrange("p (a b) -> p a b", a=a)

        def rview(off, n):
            size, a, x = min((size, a, m) for m, (x, (a, size)) in enumerate(zip(parts_mem, PARTS)) if a <= off and off + n <= a + size)
            return parts_mem[x][:, off - a:off - a + n]

        def bc(ap, n):
            return ap.unsqueeze(2).broadcast_to([ap.shape[0], ap.shape[1], n])

        def rep(ap, n):
            return ap.unsqueeze(1).broadcast_to([ap.shape[0], n, ap.shape[1]])

        def tt(E, o, a, b, op, *toks):
            return E(lambda e: e.tensor_tensor(o, a, b, op), toks)

        def ts(E, o, a, s1, s2, op0, op1, *toks):
            if op1 is None:
                return E(lambda e: e.tensor_scalar(o, a, s1, None, op0), toks)
            return E(lambda e: e.tensor_scalar(o, a, s1, s2, op0, op1), toks)

        def stt(o, a, s, b, op0, op1, *toks):
            return V(lambda e: e.scalar_tensor_tensor(out=o, in0=a, scalar=s, in1=b, op0=op0, op1=op1), toks)

        def cp(E, o, a, *toks):
            if E is S:
                return S(lambda e: e.activation(o, a, ACT.Copy), toks)
            return E(lambda e: e.tensor_copy(o, a), toks)

        def act(o, a, f, *toks, bias=0.0, scale=1.0, accum=None):
            if accum is None:
                return S(lambda e: e.activation(o, a, f, bias=bias, scale=scale), toks)
            return S(lambda e: e.activation(o, a, f, bias=bias, scale=scale, accum_out=accum), toks)

        def red(o, a, op, *toks):
            return V(lambda e: e.tensor_reduce(o, a, AX, op), toks)

        def recip(o, a, *toks):
            return V(lambda e: e.reciprocal(o, a), toks)

        def mset(E, o, v, *toks):
            return E(lambda e: e.memset(o, v), toks)

        def mm(o, l, r, start, stop, *toks, sig=False):
            return PE(lambda e: e.matmul(o, l, r, start=start, stop=stop), toks, signal=sig)

        def tr(o, a, *toks, sig=False):
            n = a.shape[0]
            b = a.base_partition()
            idn = low[b:b + n, OC + C_ID + b:OC + C_ID + b + n]
            return PE(lambda e: e.transpose(o, a, idn), toks, signal=sig)

        dma_count = {}

        def dma(E, o, a, sm, *toks):
            E.wait(toks)
            dma_count[sm[0]] = dma_count.get(sm[0], 0) + 16
            E.todo.append(lambda e: e.dma_start(o, a).then_inc(sm[1], 16))
            return (sm[0], sm[1], dma_count[sm[0]])

        small_at = [OS]

        def small(n):
            o = small_at[0]
            small_at[0] += n
            assert small_at[0] <= OU, "small"
            return low[:, o:o + n]

        uT = view3(OU, 8, 256)
        ident = view(OC + C_ID, 128)

        def const(off, n):
            return low[:, OC + off:OC + off + n]

        def vec(name, i, n=1, p=128):
            o = OV + VOFF[name] + i
            return low[0:p, o:o + n]

        ring_sem = [sem(f"s_w{i}") for i in range(NR)]
        ring = [(n, None) for n in range(NR)]

        def wload(pieces):
            n, free = ring.pop(0)
            slot = view(OR + 2048 * n, 2048)
            for put, src in pieces:
                tok = dma(SP, put(slot), src, ring_sem[n], free)
            return n, slot, tok

        def wfree(n, *toks):
            ring.append((n, list(toks)))

        def wcols(W, c0, w, k0, nk, d0, width):
            src = W[128 * k0:128 * (k0 + nk), c0:c0 + w].rearrange("(k p) n -> p k n", p=128)
            return (lambda s: s[:, 0:nk * width].rearrange("p (k n) -> p k n", k=nk)[:, :, d0:d0 + w], src)

        PG = Banks([PSUM[:, i, :] for i in (0, 1)])
        PA = Banks([PSUM[:, i, :] for i in (2, 3, 4)])
        PB = Banks([PSUM[:, i, :] for i in (5, 6, 7)])

        class P4:
            @staticmethod
            def get():
                return (PG if PG.free else PA).get()

            @staticmethod
            def put(bank, *toks):
                (PG if len(PG.free) < 2 else PA).put(bank, *toks)


        def halves(bank):
            return bank.rearrange("p (a b) -> p a b", a=2)

        def quarters(bank):
            return bank.rearrange("p (a b) -> p a b", a=4)

        def gemm_f(W, plan, K, evac, rhs, dep, head=0, pool=None, mid=None):
            def load(n):
                wn, slot, wt = wload([wcols(W, c0, w, 0, K, d0, 256) for c0, w, d0 in plan[n][0]])
                return wn, slot[:, 0:K * 256].rearrange("p (k n) -> p k n", k=K), wt

            pool = pool or PG
            if head:
                got = []
                for n in range(head):
                    got.append((load(n), pool.get()))
                last = [None] * head
                for i in range(2):
                    for n in range(head):
                        (wn, w3, wt), (bank, bt) = got[n]
                        off = 0
                        for j, m in enumerate(plan[n][1]):
                            for k in range(K):
                                o = 256 * j + 128 * i
                                last[n] = mm(bank[0:m, o:o + 128], w3[:, k, off:off + m], rhs[:, k, 128 * i:128 * i + 128],
                                             k == 0, k == K - 1, dep[i], wt, bt, sig=(k == K - 1))
                            off += 128 if m == 128 else m
                            yield
                        if i == 1:
                            wfree(wn, last[n])
                            turn_waiting()
                            pool.put(bank, *evac(bank, n, last[n]))
                            if n == 0 and mid:
                                mid(0)
                            if n == head - 1 and mid:
                                mid(1)
            for n in range(head, len(plan)):
                wn, w3, wt = load(n)
                bank, bt = pool.get()
                off = 0
                for j, m in enumerate(plan[n][1]):
                    for k in range(K):
                        t = mm(bank[0:m, 256 * j:256 * j + 256], w3[:, k, off:off + m], rhs[:, k, :], k == 0, k == K - 1,
                               dep, wt, bt, sig=(k == K - 1))
                        if K == 8 and k == 3:
                            turn_waiting()
                            yield
                    off += 128 if m == 128 else m
                    if j + 1 < len(plan[n][1]):
                        yield
                wfree(wn, t)
                pool.put(bank, *evac(bank, n, t))
                yield

        SX = [0]

        def mm3(o, l, r, start, stop, *toks, sig=False):
            mm(o, l[0], r[0], start, False, *toks)
            mm(o, l[0], r[1], False, False)
            return mm(o, l[1], r[0], False, stop, sig=sig)

        class Stream:

            def __init__(self, slots):
                self.slots, self.at, self.ready, self.tu = slots, 0, [], [None, None]
                self.ul = rview(OU, 2048).rearrange("p (k t) -> p k t", k=8)
                self.taken, self.hi, self.used = [], [], []

            def take(self):
                n, free = ring.pop(0)
                self.taken.append(n)
                return rview(OR + 2048 * n, 2048), free

            def part(self, i, dep, fp32_done):
                if i == 0:
                    uh, self.uh_free = self.take()
                    self.uh = uh.rearrange("p (k t) -> p k t", k=8)
                a = slice(128 * i, 128 * i + 128)
                t = cp(S, self.uh[:, :, a], uT[:, :, a], dep, self.uh_free)
                self.tu[i] = (t, tt(V, self.ul[:, :, a], uT[:, :, a], self.uh[:, :, a].bitcast(F32), ALU.subtract, t, fp32_done))

            def prepare(self):
                j = self.at
                if j == len(self.slots):
                    self.after()
                    return
                self.at += 1
                pieces, nk, width, w = self.slots[j]
                wn, slot, wt = wload(pieces)
                whole = slot[:, 0:nk * width].rearrange("p (k n) -> p k n", k=nk)
                lo = rview(OR + 2048 * wn, nk * width).rearrange("p (k n) -> p k n", k=nk)
                if j < 2:
                    hi, free = self.take()
                    self.used.append(free)
                    self.hi.append(hi)
                hi = self.hi[j % 2][:, 0:nk * width].rearrange("p (k n) -> p k n", k=nk)
                ts_ = []
                for h in range(2):
                    r = slice(nk // 2 * h, nk // 2 * (h + 1))
                    t = cp(S, hi[:, r, 0:w], whole[:, r, 0:w], wt, self.used[j % 2])
                    ts_.append(tt((V, G)[h], lo[:, r, 0:w], whole[:, r, 0:w], hi[:, r, 0:w].bitcast(F32), ALU.subtract, t))
                self.ready.append((wn, hi, lo, ts_))

            def next(self):
                self.prepare()
                return self.ready.pop(0)

            def done(self, j, wn, t):
                wfree(wn, t)
                self.used[j % 2] = [t]

            def end(self, t):
                assert self.at == len(self.slots) and not self.ready
                for n in self.taken:
                    ring.insert(0, (n, [t]))

            def by_features(self, count, evac, pool=None, n0=0, widths=None):
                pool = pool or PG
                for n in range(n0, n0 + count):
                    j = self.at - 1
                    wn, hi, lo, tw = self.next()
                    bank, bt = pool.get()
                    off = 0
                    for q, m in enumerate(widths[n] if widths else [128, 128]):
                        o, c = bank[0:m, 256 * q:256 * q + 256], slice(off, off + m)
                        for k in range(8):
                            mm(o, hi[:, k, c], self.uh[:, k, :], k == 0, False, [x[0] for x in self.tu], tw[k // 4], bt)
                            mm(o, lo[:, k, c], self.uh[:, k, :], False, False)
                            if k == 5:
                                turn_waiting()
                                yield
                        for k in range(8):
                            t = mm(o, hi[:, k, c], self.ul[:, k, :], False, k == 7, [x[1] for x in self.tu], sig=(k == 7))
                        off += 128 if m == 128 else m
                        if q == 0:
                            yield
                    self.done(j, wn, t)
                    pool.put(bank, *evac(bank, n, t))
                    yield

            def by_tokens(self, count, w, evac):
                nk = 8 // count
                banks = [PG.get() for _ in range(2)]
                for s in range(count):
                    j = self.at - 1
                    wn, hi, lo, tw = self.next()
                    for i in range(2):
                        a, (b, bt) = slice(128 * i, 128 * i + 128), banks[i]
                        for kk in range(nk):
                            k = nk * s + kk
                            t = mm3(b[:, 0:w], (self.uh[:, k, a], self.ul[:, k, a]), (hi[:, kk, 0:w], lo[:, kk, 0:w]), k == 0,
                                    k == 7, self.tu, tw[kk // (nk // 2)], bt, sig=(kk == nk - 1))
                            if kk % 2 == 1:
                                turn_waiting()
                                yield
                        if s == count - 1:
                            PG.put(b, *evac(i, b, t))
                    self.done(j, wn, t)

        def gemm_t(slots, lhs, dep, banks, w, K):
            k = 0
            for pieces, nk in slots:
                wn, slot, wt = wload(pieces)
                w3 = slot[:, 0:nk * w].rearrange("p (k n) -> p k n", k=nk)
                for kk in range(nk):
                    for i in range(2):
                        b, bt = banks[i]
                        t = mm(b[:, 0:w], lhs[:, k, 128 * i:128 * i + 128], w3[:, kk, :], k == 0, k == K - 1,
                               dep, wt, bt, sig=(kk == nk - 1 and i == 1))
                    k += 1
                    if kk % 2 == 1:
                        turn_waiting()
                        yield
                wfree(wn, t)
            return t

        def rstd(ss, o, n, eps, *toks):
            t = ts(V, o, ss, 1.0 / n, eps, ALU.mult, ALU.add, *toks)
            return tt(G, o, o, mh.broadcast_to([128, o.shape[1]]), ALU.pow, t)

        def norm_x(i, src, xn, ss, rs, *toks):
            t = act(xn[:, i, :], src[:, i, :], ACT.Square, *toks, accum=ss)
            t = rstd(ss, rs, 1024, EPS, t)
            return ts(V, xn[:, i, :], src[:, i, :], rs, None, ALU.mult, None, t)

        def turn_x(i, x, gname, dst, t):
            last = []
            for b in range(2):
                bank, bt = PB.get()
                for c in range(4):
                    tp = tr(bank[:, 128 * c:128 * c + 128], x[:, i, 512 * b + 128 * c:512 * b + 128 * c + 128],
                            t, bt, sig=(c == 3))
                o = dst[:, 4 * b:4 * b + 4, 128 * i:128 * i + 128]
                if gname is None:
                    te = cp(S, o, quarters(bank), tp)
                else:
                    te = tt(V, o, quarters(bank), bc(vec(gname, 4 * b, 4), 128), ALU.mult, tp)
                PB.put(bank, te)
                last.append(te)
                yield
            return last

        def norm_t(i, src, xn, gname, dst, *toks):
            t = norm_x(i, src, xn, small(1), small(1), *toks)
            yield
            return (yield from turn_x(i, xn, gname, dst, t))

        def gain_load(gname, off, *toks):
            a = A[gname].rearrange("a n -> (a n)") if gname != "norm_final_2" else A[gname]
            dst = view(off, 1024)
            return dst, dma(SP, dst, a.partition_broadcast(128), sem("s_" + gname), toks)

        def post_norm(i, y, gain, h, hsrc, tmp, t, *toks):
            slot, wt = gain
            ss, rs = small(2), small(1)
            for n in range(2):
                tq = act(tmp[:, i, 512 * n:512 * n + 512], y[n], ACT.Square, t, accum=ss[:, n:n + 1])
            tq = tt(V, rs, ss[:, 0:1], ss[:, 1:2], ALU.add, tq)
            tq = rstd(rs, rs, 1024, EPS, tq)
            r = []
            for n in range(2):
                c = slice(512 * n, 512 * n + 512)
                r.append(stt(tmp[:, i, c], y[n], rs, slot[:, c], ALU.mult, ALU.mult, tq, wt))
            return tt(V, h[:, i, :], hsrc[:, i, :], tmp[:, i, :], ALU.add, r, toks), r

        def beside(main, side, lag):
            res = [None, None]
            live = [True, True]

            def step(q, g):
                if live[q]:
                    try:
                        next(g)
                    except StopIteration as e:
                        live[q], res[q] = False, e.value

            step(1, side)
            n = 0
            while live[0]:
                step(0, main)
                n += 1
                if n > lag:
                    step(1, side)
            while live[1]:
                step(1, side)
            return res

        waiting = []

        def turn_waiting():
            while waiting:
                alone(waiting.pop(0))

        def rope(bank, n, tok, dst, cos, sin, zs, t1, prev, done):
            t_z = cp(S, zs, halves(bank)[:, 0:n, :], tok, prev)
            t_c = tt(G, t1, zs, rep(cos, n), ALU.mult, t_z, prev)
            yield [t_z]
            b2, bt = PB.get()
            t_r = mm(b2[:, 0:256 * n], const(C_ROT, 128), zs, True, True, t_z, bt, sig=True)
            t_s = tt(V, dst, halves(b2)[:, 0:n, :], rep(sin, n), ALU.mult, t_r)
            PB.put(b2, t_s)
            done(tt(G, dst, dst, t1, ALU.add, t_s, t_c))

        def drive(main, *turns):
            turns, k, more = list(turns), 0, True
            while more or turns:
                if more:
                    try:
                        next(main)
                    except StopIteration:
                        more = False
                if turns:
                    g = turns[k % len(turns)]
                    try:
                        new = next(g)
                        k += 1
                        if isinstance(new, tuple):
                            turns += new
                    except StopIteration:
                        k %= len(turns)
                        turns = [x for x in turns[k:] + turns[:k] if x is not g]
                        k = 0

        def alone(g):
            while True:
                try:
                    next(g)
                except StopIteration as e:
                    return e.value

        s_i, s_c, s_x, s_v, s_p = sem("s_i"), sem("s_c"), [sem("s_x0"), sem("s_x1")], sem("s_v"), sem("s_p")
        mh = small(1)
        t_mh = mset(G, mh, -0.5)
        x_sb = view3(P + 24576, 2, 1024)
        xn = view3(P + 26624, 2, 1024)
        x_d = A["x"][0].rearrange("(i p) d -> p i d", p=128)
        pT = view3(P + 21504, 2, 256)
        t_p = dma(SP, pT, pt, s_p)
        ple_n, ple_w, t_pw = wload([wcols(A["w_ple"][0], 0, 1024, 0, 2, 0, 1024)])
        t_x = [dma(S, x_sb[:, i, :], x_d[:, i, :], s_x[i]) for i in range(2)]
        t_id = dma(S, const(0, 128), consts[:, 0:128], s_i)
        t_v = dma(S, view(OV, 128), vecs, s_v)
        t_c = dma(S, const(128, C_END - 128), consts[:, 128:C_END], s_c)
        lo, s_lo = view(P + 2048, 1024), sem("s_lo")
        for o, nm_ in ((lo[0:32, 0:512], "rwkv_w2"), (lo[32:64, 0:512], "rwkv_a2"), (lo[0:96, 512:1024], "rwkv_g2")):
            t_lo = dma(S, o, A[nm_][0], s_lo)
        omka = small(4)
        G.wait([t_mh])
        V.wait([t_v])
        t_omka = ts(V, omka, vec("rwkv_k_a", 0, 4), -1.0, 1.0, ALU.mult, ALU.add, t_v)

        pE = view3(OPE, 2, 1024)
        t_pe = []

        def ple_in():
            w3 = ple_w.rearrange("p (k n) -> p k n", k=2)
            for i in range(2):
                for n in range(2):
                    b, bt = PA.get()
                    for k in range(2):
                        t = mm(b, pT[:, k, 128 * i:128 * i + 128], w3[:, k, 512 * n:512 * n + 512], k == 0, k == 1, t_p, t_pw,
                               bt, sig=(k == 1))
                    t_pe.append(cp(S, pE[:, i, 512 * n:512 * n + 512], b, t))
                    PA.put(b, t_pe[-1])
                    yield
            wfree(ple_n, t)

        n0 = norm_t(0, x_sb, xn, "mix_pre_norm", uT, t_x[0])
        n1 = norm_t(1, x_sb, xn, "mix_pre_norm", uT, t_x[1])
        next(n0)
        next(n1)
        alone(ple_in())
        PE.wait([t_id])
        t_u = [alone(n0)]
        PE.wait([t_c])
        S.wait([t_v])

        R = P + 11776
        zm = view3(R, 14, 256)
        oE, oCS, oCSC, oQ, oQi, oQx, oA, oKK, oKM, oAR, oG, oBON, oVT, oBK = [
            P + 15360 + 1024 * i for i in range(10)] + [P + 26624, P + 27648, P + 28672, P + 29696]
        ZS = [view3(oQ + 514 * i, 2, 257) for i in range(2)]
        D = [view3(oQ + 1028 + 512 * i, 2, 256) for i in range(2)]
        t_zs0 = [mset(G, z[:, :, 0:1], 0.0) for z in ZS]
        w_in = A["w_in"][0]
        zprev = [None, None]
        t_zm = {}

        def evac_rwkv(bank, n, tok):
            b = n % 2
            z, d = ZS[b], D[b]
            if n < 6:
                ps = [(128, 0, 2)]
            else:
                ps = [(64, 0, 1), (96, 1, 1)]
            frees, last = [], None
            for p, j, m in ps:
                t1 = cp(S, z[0:p, j:j + m, 1:257], halves(bank)[0:p, j:j + m, :], tok, zprev[b], t_zs0)
                frees.append(t1)
                t2 = tt(G, d[0:p, j:j + m, :], z[0:p, j:j + m, 0:256], z[0:p, j:j + m, 1:257], ALU.subtract, t1, zprev[b])
                for q in range(m):
                    c = 2 * n + j + q
                    last = stt(zm[0:p, c, :], d[0:p, j + q, :], vec("rwkv_mu", c, 1, p), z[0:p, j + q, 1:257],
                               ALU.mult, ALU.add, t2)
                    t_zm[c] = last
            zprev[b] = last
            return frees

        B0 = 2304
        plan = [([(B0 + 256 * n, 256, 0)], [128, 128]) for n in range(6)]
        plan = plan[2:4] + plan[0:2] + plan[4:6]
        order = [2, 3, 0, 1, 4, 5]
        plan = [([(B0 + 1536, 160, 0)], [64, 96])] + plan
        order = [6] + order
        t_u.append([])

        def norm1():
            t_u[1] += yield from n1

        def fslots(W, plan):
            return [([wcols(W, c0, w, 0, 8, d0, 256) for c0, w, d0 in ps], 8, 256, max(d0 + w for _, w, d0 in ps))
                    for ps, _ in plan]

        def tslots(W, c0, n):
            return [([wcols(W, c0 + 512 * r, 512, k, 4, 0, 512)], 4, 512, 512) for r in range(n) for k in (0, 4)]

        VT1 = [(1536, 512, 4), (1536, 512, 4), (2048, 256, 8)]
        st1 = Stream(fslots(w_in, plan[2:] + [([(256 * n, 256, 0)], 0) for n in range(6)])
                     + [([wcols(w_in, c0, w, 4 * (n % 2), nk, 0, w)], nk, w, w) for n, (c0, w, nk) in enumerate(VT1)]
                     + tslots(w_in, 4000, 4))

        def stream_start(st, dep):
            def f(step):
                if step == 0:
                    st.part(0, dep[0], pe_now())
                    st.prepare()
                else:
                    st.part(1, dep[1], pe_now())
            return f

        def pe_now():
            return (PE.sem[0], PE.sem[1], PE.n)

        zg = gemm_f(w_in, plan[:2], 8, lambda b, n, t: evac_rwkv(b, order[n], t), uT, t_u, head=2,
                    mid=stream_start(st1, t_u))
        nn = norm1()
        for _ in range(2):
            next(zg)
        alone(nn)
        alone(zg)
        alone(st1.by_features(5, lambda b, n, t: evac_rwkv(b, order[n], t), n0=2, widths=[w for _, w in plan]))
        V.wait([t_c])
        G.wait([t_c, t_v])

        o_attn = view3(P + 30720, 2, 256)
        o_rwkv = view3(P + 13824, 4, 256)

        t_idb = cp(V, identb, ident, t_c)

        E4, CS, CSC, Q4, Qi, Qx, A4, KK, KM = [view(o, 1024) for o in (oE, oCS, oCSC, oQ, oQi, oQx, oA, oKK, oKM)]
        G4, BON = view(oG, 1024), view(oBON, 1024)
        TMP = view(oBK, 1024)

        def v4(x):
            return x.rearrange("p (c t) -> p c t", c=4)

        def v42(x):
            return x.rearrange("p (c i t) -> p c i t", c=4, i=2)

        def v8(x):
            return x.rearrange("p (c t) -> p c t", c=8)

        AR = view(oAR, 2048).rearrange("p (c i w t) -> p c i w t", c=4, i=2, w=2)
        VT = view3(oVT, 2, 512)
        BK = view3(oBK, 2, 512)
        zr, zk, zv = zm[:, 0:4, :], zm[:, 4:8, :], zm[:, 8:12, :]
        zk_f = view(R + 1024, 1024)
        zv_f = view(R + 2048, 1024)

        def chunk_pairs(mk, ev, pool, *toks):
            for b in range(2):
                bank, bt = pool.get()
                for j in range(2):
                    t = mk(bank[:, 256 * j:256 * j + 256], 2 * b + j, bt, toks, j == 1)
                pool.put(bank, *ev(bank, b, t))
                yield

        rw = {}

        def rwkv_side():
            t_th = act(zm[0:32, 12, :], zm[0:32, 12, :], ACT.Tanh, t_zm[12])
            t_sg = act(zm[0:96, 13, :], zm[0:96, 13, :], ACT.Sigmoid, t_zm[13])
            onez = view(oVT, 1024)
            t_one = mset(G, onez, 1.0)
            t_one = mset(G, onez.rearrange("p (c t) -> p c t", c=8)[:, :, 0:1], 0.0, t_one)
            yield
            te = []

            def ev_w(bank, b, t):
                for j in range(2):
                    te.append(act(E4[:, 512 * b + 256 * j:512 * b + 256 * j + 256], bank[:, 256 * j:256 * j + 256],
                                  ACT.Sigmoid, t, bias=vec("rwkv_w0", 2 * b + j)))
                return [te[-1]]

            yield from chunk_pairs(lambda o, c, bt, tk, sg: mm(o, lo[0:32, 128 * c:128 * c + 128], zm[0:32, 12, :], True, True,
                                                               bt, tk, sig=sg), ev_w, PB, t_th, t_lo)
            ta = []

            def ev_a(bank, b, t):
                for j in range(2):
                    ta.append(act(A4[:, 512 * b + 256 * j:512 * b + 256 * j + 256], bank[:, 256 * j:256 * j + 256],
                                  ACT.Sigmoid, t, bias=vec("rwkv_a0", 2 * b + j)))
                return [ta[-1]]

            yield from chunk_pairs(lambda o, c, bt, tk, sg: mm(o, lo[32:64, 128 * c:128 * c + 128], zm[32:64, 12, :], True, True,
                                                               bt, tk, sig=sg), ev_a, PB, t_zm[12], t_lo)
            tg = []

            def ev_g(bank, b, t):
                tg.append(cp(S, G4[:, 512 * b:512 * b + 512], bank, t))
                return [tg[-1]]

            yield from chunk_pairs(lambda o, c, bt, tk, sg: mm(o, lo[0:96, 512 + 128 * c:512 + 128 * c + 128], zm[0:96, 13, :],
                                                               True, True, bt, tk, sig=sg), ev_g, PB, t_sg, t_lo)
            t_cs = V(lambda e: e.tensor_tensor_scan(CS, onez, E4, 0.0, ALU.mult, ALU.add), [te, t_one])
            mid = v8(CS)[:, :, 63:64].broadcast_to([128, 8, 128])
            t_cc = tt(V, v8(CSC), v8(CS), mid, ALU.subtract, t_cs)
            fct = small(4)
            t_f = tt(V, fct.unsqueeze(2), v42(CSC)[:, :, 0, 127:128], v42(CS)[:, :, 1, 63:64], ALU.add, t_cc)
            t_qx = tt(G, Qx, CSC, E4, ALU.subtract, t_cc)
            t_q = act(Q4, CSC, ACT.Exp, t_cc, scale=-S0)
            t_qi = act(Qi, CSC, ACT.Exp, t_cc, scale=S0)
            t_qx = act(Qx, Qx, ACT.Exp, t_qx, scale=-S0)
            t_f = act(fct, fct, ACT.Exp, t_f, scale=-S0)
            zks = [t_zm[c] for c in range(12)]
            t_kk = tt(V, v4(KK), zk, bc(vec("rwkv_k_k", 0, 4), 256), ALU.mult, zks)
            t_k2 = tt(V, TMP, KK, KK, ALU.mult, t_kk)
            t_vt = []
            for i in range(2):
                bank, bt = PB.get()
                for c in range(4):
                    t = tr(bank[:, 128 * c:128 * c + 128], zm[:, 8 + c, 128 * i:128 * i + 128], bt, zks, sig=(c == 3))
                t = cp(S, VT[:, i, :], bank, t, t_cs)
                PB.put(bank, t)
                t_vt.append(t)
                yield
            yield
            yield
            tn = []

            def ev_n(bank, b, t):
                c = slice(512 * b, 512 * b + 512)
                t = ts(V, CS[:, c], bank, 1e-24, None, ALU.max, None, t)
                t2 = act(CS[:, c], CS[:, c], ACT.Sqrt, t)
                tn.append(recip(CS[:, c], CS[:, c], t2))
                return [t]

            yield from chunk_pairs(lambda o, c, bt, tk, sg: mm(o, const(C_BLK, 128), TMP[:, 256 * c:256 * c + 256], True, True,
                                                               bt, tk, sig=sg), ev_n, PB, t_k2, t_f)
            t_kn = tt(V, KK, KK, CS, ALU.mult, tn)
            for c in range(4):
                s = slice(256 * c, 256 * c + 256)
                t = act(KM[:, s], A4[:, s], ACT.Identity, ta, t_omka, scale=vec("rwkv_k_a", c), bias=omka[:, c:c + 1])
            t_km = tt(V, KM, KM, zk_f, ALU.mult, t)
            yield
            for c in range(4):
                t_ar = stt(AR[:, c, :, 0, :], v42(KK)[:, c], -1.0, v42(Qx)[:, c], ALU.mult, ALU.mult, t_kn, t_qx)
            t_b = tt(G, A4, A4, KK, ALU.mult, t_kn, t)
            t_b = tt(V, A4, A4, Qi, ALU.mult, t_b, t_qi)
            for c in range(4):
                t_r = tt(G, AR[:, c, :, 1, :], zm[:, c, :].rearrange("p (i t) -> p i t", i=2), v42(Q4)[:, c], ALU.mult, t_q)
            for c in range(4):
                t = stt(TMP[:, 256 * c:256 * c + 256], zm[:, c, :], vec("rwkv_r_k", c), KM[:, 256 * c:256 * c + 256],
                        ALU.mult, ALU.mult, t_km, tn)
            t_kt = tt(V, KM, KM, Qi, ALU.mult, t, t_qi)
            for _ in range(4):
                yield
            tb = []

            def ev_b(bank, b, t):
                c = slice(512 * b, 512 * b + 512)
                tb.append(tt(V, BON[:, c], bank, zv_f[:, c], ALU.mult, t))
                return [tb[-1]]

            yield from chunk_pairs(lambda o, c, bt, tk, sg: mm(o, const(C_BLK, 128), TMP[:, 256 * c:256 * c + 256], True, True,
                                                               bt, tk, sig=sg), ev_b, PB, t)
            t_bk = []
            for n, (src, tk) in enumerate(((A4, t_b), (KM, t_kt))):
                bank, bt = PB.get()
                for c in range(4):
                    t = tr(bank[:, 128 * c:128 * c + 128], src[:, 256 * c:256 * c + 128], bt, tk, sig=(c == 3))
                t = cp(S, BK[:, n, :], bank, t, tb)
                PB.put(bank, t)
                t_bk.append(t)
                yield
            H0 = view(R + 3072, 512).rearrange("p (c w v) -> p c w v", c=4, w=2)
            t_h0 = mset(G, view(R + 3072, 512), 0.0, t_ar, tg)
            chain_off = [(P + 15360, P + 16384, P + 17408, P + 17920, P + 18432),
                         (P + 18944, R, P + 19968, P + 20480, P + 20992)]
            RHS, U = view(oKK, 512), view(oKK + 512, 512)
            Y, YC = view(R + 1024, 512), view(R + 1536, 512)

            def h8(x):
                return x.rearrange("p (h v) -> p h v", h=8)

            for i in range(2):
                res = {}

                def chain(p):
                    half = slice(64 * p, 64 * p + 64)
                    LN, MN, Xa, Xt, T = [view(o, n) for o, n in zip(chain_off[p], (1024, 1024, 512, 512, 512))]
                    LN4, MN4 = [x.rearrange("p (c w t) -> p c w t", c=4, w=2) for x in (LN, MN)]
                    bt_ = v42(A4)[half, :, i, :]
                    kt_ = v42(KM)[half, :, i, :]
                    a_ = AR[half, :, i, :, :]
                    first = [t_ar, t_r, t_b, t_kt, rw.get("chain_free")]
                    msk = const(C_SU, 256).unsqueeze(1).broadcast_to([128, 2, 256])
                    for dst, src in ((LN, bt_), (MN, kt_)):
                        for b in range(2):
                            bank, bt = PB.get()
                            for j in range(2):
                                c = 2 * b + j
                                t = mm(bank[:, 256 * j:256 * j + 256], src[:, c, :], a_[:, c, :, :].rearrange("p w t -> p (w t)"),
                                       True, True, first, bt, sig=(j == 1))
                            t = tt(V, halves(dst[:, 512 * b:512 * b + 512]), halves(bank), msk, ALU.mult, t)
                            PB.put(bank, t)
                        t_dst = t
                        yield
                    bank, bt = PB.get()
                    for c in range(4):
                        t = mm(bank[:, 128 * c:128 * c + 128], a_[:, c, 0, :], bt_[:, c, :], True, True, bt, sig=(c == 3))
                    t = tt(V, quarters(Xa), quarters(bank), rep(const(C_M0, 128), 4), ALU.mult, t, first)
                    PB.put(bank, t)
                    tx = tt(G, quarters(Xa), quarters(Xa), rep(ident, 4), ALU.add, t)
                    t = tt(V, quarters(Xt), LN4[:, :, 0, :], rep(const(C_M0T, 128), 4), ALU.mult, t_dst)
                    txt = tt(G, quarters(Xt), quarters(Xt), rep(ident, 4), ALU.add, t)
                    yield
                    tmm = None
                    for lv in range(6):
                        bank, bt = PB.get()
                        mm(quarters(bank), identb, rep(identb, 4), True, False, bt, t_idb)
                        for c in range(4):
                            o = bank[:, 128 * c:128 * c + 128]
                            t = mm(o, LN4[:, c, 0, :], Xa[:, 128 * c:128 * c + 128], False, c == 3, tx, t_dst, sig=(c == 3))
                        tT = tt(V, quarters(T), quarters(bank), rep(const(C_LV + 128 * lv, 128), 4), ALU.mult, t, tmm)
                        PB.put(bank, tT)
                        yield
                        bank, bt = PB.get()
                        for c in range(4):
                            s = slice(128 * c, 128 * c + 128)
                            t = mm(bank[:, s], T[:, s], Xt[:, s], True, True, tT, txt, bt, sig=(c == 3))
                        if lv < 5:
                            bank2, bt = PB.get()
                            for c in range(4):
                                s = slice(128 * c, 128 * c + 128)
                                t2 = mm(bank2[:, s], Xt[:, s], T[:, s], True, True, tT, txt, bt, sig=(c == 3))
                            tmm = t2
                            txt = cp(S, Xt, bank, t2)
                            tx = cp(S, Xa, bank2, t2)
                            PB.put(bank2, tx)
                        else:
                            txt = cp(S, Xt, bank, t)
                        PB.put(bank, txt)
                        yield
                    res[p] = (LN4, MN4, Xt, [txt, t_dst])

                gs = [chain(0), chain(1)]
                while gs:
                    for g in list(gs):
                        try:
                            next(g)
                        except StopIteration:
                            gs.remove(g)
                    yield
                both = [res[0][3], res[1][3], t_vt]
                bank, bt = PB.get()
                for h in range(8):
                    c, p = h // 2, h % 2
                    o = bank[:, 64 * h:64 * h + 64]
                    t = mm(o, res[p][1][:, c, 0, :], VT[:, i, 64 * h:64 * h + 64], True, i == 0, both, bt, sig=(h == 7))
                    if i == 1:
                        t = mm(o, AR[:, c, 1, 0, :], H0[:, c, p, :], False, True, t_h0, sig=(h == 7))
                t = cp(V, RHS, bank, t, rw.get("rhs_free"))
                PB.put(bank, t)
                yield
                bank, bt = PB.get()
                for h in range(8):
                    c, p = h // 2, h % 2
                    t = mm(bank[:, 64 * h:64 * h + 64], res[p][2][:, 128 * c:128 * c + 128], RHS[:, 64 * h:64 * h + 64],
                           True, True, t, bt, sig=(h == 7))
                t_U = cp(V, U, bank, t)
                PB.put(bank, t_U)
                yield
                bank, bt = PB.get()
                for h in range(8):
                    c, p = h // 2, h % 2
                    s = slice(64 * h, 64 * h + 64)
                    mm(bank[:, s], res[p][0][:, c, 1, :], U[:, s], True, False, t_U, bt)
                    t = mm(bank[:, s], res[p][1][:, c, 1, :], VT[:, i, s], False, i == 0, sig=(h == 7))
                    if i == 1:
                        t = mm(bank[:, s], AR[:, c, 1, 1, :], H0[:, c, p, :], False, True, sig=(h == 7))
                rw["chain_free"] = t
                tY = cp(S, Y, bank, t, rw.get("y_free"))
                PB.put(bank, tY)
                if i == 0:
                    bank, bt = PB.get()
                    for h in range(8):
                        c, p = h // 2, h % 2
                        s = slice(64 * h, 64 * h + 64)
                        o = bank[64 * p:64 * p + 64, 64 * c:64 * c + 64]
                        mm(o, BK[:, 0, s], U[:, s], True, False, t_bk, bt)
                        t = mm(o, BK[:, 1, s], VT[:, 0, s], False, True, sig=(h == 7))
                    hb = bank[:, 0:256].rearrange("p (c v) -> p c v", c=4)
                    for p in range(2):
                        q = slice(64 * p, 64 * p + 64)
                        t_hh = tt(V, H0[q, :, p, :], hb[q], bc(fct[q, :], 64), ALU.mult, t, t_f, t_h0)
                    t_h0 = t_hh
                    PB.put(bank, t_hh)
                    rw["rhs_free"] = t
                mean, var = small(8), small(8)
                t = red(mean, h8(Y), ALU.add, tY)
                t = ts(V, mean, mean, 1.0 / 64, None, ALU.mult, None, t)
                t = tt(V, h8(Y), h8(Y), bc(mean, 64), ALU.subtract, t)
                t = act(YC, Y, ACT.Square, t)
                t = red(var, h8(YC), ALU.add, t)
                t = rstd(var, var, 64, GN_EPS, t)
                t = tt(V, h8(YC), h8(Y), bc(var, 64), ALU.mult, t)
                rw["y_free"] = t
                yield
                yield
                yield
                bank, bt = PB.get()
                for c in range(4):
                    tp = tr(bank[:, 128 * c:128 * c + 128], YC[:, 128 * c:128 * c + 128], t, bt, sig=(c == 3))
                for c in range(4):
                    t = act(o_rwkv[:, c, 128 * i:128 * i + 128], bank[:, 128 * c:128 * c + 128], ACT.Identity, tp, tb, t_vt,
                            scale=vec("rwkv_ln_w", c), bias=vec("rwkv_ln_b", c))
                PB.put(bank, t)
                rw["y_free"] = tp
                o_ = o_rwkv[:, :, 128 * i:128 * i + 128]
                t = tt(V, o_, o_, v4(BON)[:, :, 128 * i:128 * i + 128], ALU.add, t)
                t = tt(V, o_, o_, v4(G4)[:, :, 128 * i:128 * i + 128], ALU.mult, t, tg)
                out_dep[i].append(t)
                yield
            rw["out"] = t

        qk = view3(P + 4096, 12, 256)
        vtok = view3(P + 7168, 2, 768)
        rz = [view3(P + 8704 + 1024 * i, 2, 256) for i in range(2)]
        rt = [view3(P + 9216 + 1024 * i, 2, 256) for i in range(2)]
        t_qk, rprev, t_vtok = [], [None, None], []

        def evac_qk(bank, n, tok):
            def done(t):
                rprev[n % 2] = t
                t_qk.append(t)
            g = rope(bank, 2, tok, qk[:, 2 * n:2 * n + 2, :], const(C_COS, 256), const(C_SIN, 256),
                     rz[n % 2], rt[n % 2], rprev[n % 2], done)
            waiting.append(g)
            return next(g)

        gates = view3(P, 2, 2048)
        t_gate = []

        def gate_ranges(st, n, dst, lst):
            for r in range(n):
                def evac(i, bank, tok):
                    lst.append(act(dst(r, i), bank, ACT.Sigmoid, tok, t_v))
                    return [lst[-1]]
                yield from st.by_tokens(2, 512, evac)
            st.end(pe_now())

        def qkv_main():
            yield from st1.by_features(6, evac_qk)
            for c0, w in ((1536, 512), (2048, 256)):
                def evac_v(i, bank, t):
                    t_vtok.append(cp(S, vtok[:, i, c0 - 1536:c0 - 1536 + w], bank[:, 0:w], t))
                    return [t_vtok[-1]]
                yield from st1.by_tokens(w // 256, w, evac_v)

        def softmax_e(e, pieces, nm, den, rden, gate, *toks):
            t = None
            for n, (ps, mask, dst) in enumerate(pieces):
                init = 3e38 if n == 0 else nm[:, n - 1:n]
                t = V(lambda e_, ps=ps, mask=mask, dst=dst, init=init, n=n: e_.tensor_tensor_reduce(
                    dst, ps, mask, -0.125, init, ALU.add, ALU.min, nm[:, n:n + 1]), [toks, t])
            free = t
            t = act(e, e, ACT.Exp, t, scale=-1.0, bias=nm[:, len(pieces) - 1:len(pieces)], accum=den)
            t = recip(rden, den, t)
            if gate is not None:
                t = tt(V, rden, rden, gate, ALU.mult, t)
            t = ts(V, e, e, rden, None, ALU.mult, None, t)
            return free, t

        def softmax4(E, banks, W, mask, nm, den, rden, gate, pool, *toks):
            te = []
            for h in range(4):
                b, o = banks[h % 2][0], 256 * (h // 2)
                t = V(lambda e_, h=h, b=b, o=o: e_.tensor_tensor_reduce(
                    E[:, h, :], b[:, o:o + W], mask, -0.125, 3e38, ALU.add, ALU.min, nm[:, h:h + 1]), [toks])
                te.append(act(E[:, h, :], E[:, h, :], ACT.Exp, t, scale=-1.0, bias=nm[:, h:h + 1], accum=den[:, h:h + 1]))
                if h >= 2:
                    pool.put(b, t)
            t = recip(rden, den, te)
            if gate is not None:
                t = tt(V, rden, rden, gate, ALU.mult, t)
            return tt(V, E, E, bc(rden, W), ALU.mult, t)

        def attn_side(par):
            sm = view(P + 8704 + 1536 * par, 768)
            eT = view(P + 8704 + 1536 * par + 768, 768)
            e_free = et_free = None
            half = slice(64 * par, 64 * par + 64)
            nm, den, rden = small(2), small(1), small(1)
            ma = const(C_MA, 768)
            for i in range(2):
                for hh in range(2):
                    h = 2 * hh + par
                    W = 128 * (i + 1)
                    banks = [PA.get() for _ in range(i + 1)]
                    for g in range(3):
                        b, bt = banks[(g * W) // 512]
                        o = (g * W) % 512
                        t = mm(b[:, o:o + W], qk[half, 2 * g + hh, 128 * i:128 * i + 128], qk[half, 6 + 2 * g + hh, 0:W],
                               True, True, t_qk, bt, sig=True)
                    if i == 0:
                        pieces = [(banks[0][0][:, 0:384].rearrange("p (g t) -> p g t", g=3),
                                   ma.rearrange("p (g w t) -> p g w t", g=3, w=2)[:, :, 1, :],
                                   sm[:, 0:384].rearrange("p (g t) -> p g t", g=3))]
                    else:
                        pieces = [(banks[0][0], ma[:, 0:512], sm[:, 0:512]), (banks[1][0][:, 0:256], ma[:, 512:768], sm[:, 512:768])]
                    free, te = softmax_e(sm[:, 0:3 * W], pieces, nm, den, rden, None, t, e_free, rprev)
                    for b, _ in banks:
                        PA.put(b, free)
                    yield
                    nb = 3 * (i + 1)
                    for b0 in range(0, nb, 4):
                        k = min(4, nb - b0)
                        bank, bt = PA.get()
                        for j in range(k):
                            t = tr(bank[:, 128 * j:128 * j + 128], sm[:, 128 * (b0 + j):128 * (b0 + j) + 128], te, bt, sig=(j == k - 1))
                        tT = cp(S, eT[:, 128 * b0:128 * (b0 + k)], bank[:, 0:128 * k], t, et_free, rprev)
                        PA.put(bank, tT)
                    e_free = t
                    yield
                    bank, bt = PA.get()
                    for n in range(nb):
                        g, j = n // (i + 1), n % (i + 1)
                        t = mm(bank[half, 0:128], vtok[:, j, 64 * (4 * g + h):64 * (4 * g + h) + 64], eT[:, 128 * n:128 * n + 128],
                               n == 0, n == nb - 1, tT, bt, t_vtok, sig=(n == nb - 1))
                    et_free = t
                    t = cp(S, o_attn[half, hh, 128 * i:128 * i + 128], bank[half, 0:128], t)
                    PA.put(bank, t)
                    rw.setdefault("attn", []).append(t)
                    yield

        out_dep = [[], []]
        got1 = []
        st1.after = lambda: got1.extend(up_loads(A["w_attn_up"][0], 2))
        side = rwkv_side()
        qkv = qkv_main()
        while True:
            try:
                next(qkv)
            except StopIteration:
                break
            try:
                next(side)
            except StopIteration:
                pass

        mt = view3(P + 4096, 2, 1024)
        tm = [view(P + 8704 + 512 * i, 512) for i in range(4)]
        t_m = {}

        def up_loads(W, K):
            return [wload([wcols(W, 0, 1024, k, 2, 0, 1024)]) for k in range(0, K, 2)]

        def up(W, K, lhs, dep, evac, got=None):
            slots = got or up_loads(W, K)
            for i in range(2):
                for n in range(2):
                    b, bt = PG.get()
                    for k in range(K):
                        wn, slot, wt = slots[k // 2]
                        t = mm(b, lhs[:, k, 128 * i:128 * i + 128], slot[:, 1024 * (k % 2) + 512 * n:1024 * (k % 2) + 512 * n + 512],
                               k == 0, k == K - 1, dep[i], wt, bt, sig=(k == K - 1))
                    if i == 1 and n == 1:
                        for wn, _, _ in slots:
                            wfree(wn, t)
                    PG.put(b, *evac(i, n, b, t))
                    yield

        def half_of(x, i, n):
            return x[:, i, 512 * n:512 * n + 512]

        def evac_up1(i, n, bank, tok):
            t_m[i, n] = tt(V, half_of(mt, i, n), bank, half_of(gates, i, n), ALU.mult, tok, t_gate)
            return [t_m[i, n]]

        def evac_up2(i, n, bank, tok):
            x = tm[2 * i + n]
            t = tt(V, x, bank, half_of(gates, i, 2 + n), ALU.mult, tok, t_gate)
            t_m[i, n] = tt(V, half_of(mt, i, n), half_of(mt, i, n), x, ALU.add, t, t_m[i, n])
            return [t]

        def gates_up():
            yield from gate_ranges(st1, 4, lambda r, i: gates[:, i, 512 * r:512 * r + 512], t_gate)
            while len(rw.get("attn", [])) < 8:
                yield
            yield from up(A["w_attn_up"][0], 2, o_attn, [rw["attn"]] * 2, evac_up1, got1)
            for _ in range(2):
                assert out_dep[0]
                next(ups)
                yield

        ups = up(A["w_rwkv_up"][0], 4, o_rwkv, out_dep, evac_up2)
        drive(gates_up(), side, attn_side(0), attn_side(1), side)
        def turned(i, x, hi, lo, t, th, tl):
            a = slice(128 * i, 128 * i + 128)
            for b in range(2):
                bank, bt = PB.get()
                for c in range(4):
                    tp = tr(quarters(bank)[:, c, :], x[:, i, 512 * b + 128 * c:512 * b + 128 * c + 128], t, bt, sig=(c == 3))
                h = hi[:, 4 * b:4 * b + 4, a]
                th.append(cp(S, h, quarters(bank), tp))
                tl.append(tt(V, lo[:, 4 * b:4 * b + 4, a], quarters(bank), h.bitcast(F32), ALU.subtract, th[-1]))
                PB.put(bank, tl[-1])
                yield

        def full3(W, o, lhs, th, tl):
            slots = [None] * 4

            def prepare(q, *free):
                wn, slot, wt = wload([wcols(W, 512 * (q % 2), 512, 4 * (q // 2), 4, 0, 512)])
                hi, lo, tw = rview(o[q], 2048), rview(OR + 2048 * wn, 2048), []
                for h in range(2):
                    c = slice(1024 * h, 1024 * h + 1024)
                    t = cp(S, hi[:, c], slot[:, c], wt, free)
                    tw.append(tt((V, G)[h], lo[:, c], slot[:, c], hi[:, c].bitcast(F32), ALU.subtract, t))
                slots[q] = (wn, hi, lo, tw)

            def block(i):
                banks = [PG.get(), PA.get()]
                a = slice(128 * i, 128 * i + 128)
                for q in range(4):
                    wn, hi, lo, tw = slots[q]
                    b, bt = banks[q % 2]
                    for kk in range(4):
                        k, c = 4 * (q // 2) + kk, slice(512 * kk, 512 * kk + 512)
                        mm(b, lhs[0][:, k, a], hi[:, c], k == 0, False, th[i], tw[kk // 2], bt)
                        mm(b, lhs[0][:, k, a], lo[:, c], False, False)
                        if kk % 2:
                            yield
                for q, (wn, hi, lo, tw) in enumerate(slots):
                    for kk in range(4):
                        k, c = 4 * (q // 2) + kk, slice(512 * kk, 512 * kk + 512)
                        t = mm(banks[q % 2][0], lhs[1][:, k, a], hi[:, c], False, k == 7, tl[i], sig=(kk == 3))
                    if i == 1:
                        wfree(wn, t)
                    if q < 3:
                        yield
                return [b for b, _ in banks], t
            return block(0), block(1), prepare

        def parts(o_hi, o_lo):
            return [rview(o, 2048).rearrange("p (k t) -> p k t", k=8) for o in (o_hi, o_lo)]

        mHi, mLo = parts(P + 25600, P + 27648)
        t_mh, t_ml = [[], []], [[], []]
        g0, g1, prepare = full3(A["w_out"][0], [P + 15360 + 2048 * q for q in range(4)], (mHi, mLo), t_mh, t_ml)
        prepare(0, rw["out"], rw["y_free"])
        prepare(1, rw["out"], rw["y_free"])
        next(ups)
        prepare(2, rw["out"], rw["y_free"])
        alone(turned(0, mt, mHi, mLo, [t_m[0, 0], t_m[0, 1]], t_mh[0], t_ml[0]))
        prepare(3, rw["out"], rw["y_free"])
        alone(ups)

        H = view3(P + 7168, 2, 1024)
        XN = view3(P + 9216, 2, 1024)

        def full(W, lhs, dep, K):
            slots = [wload([wcols(W, 512 * n, 512, k, min(4, K - k), 0, 512)]) for k in range(0, K, 4) for n in range(2)]

            def block(i):
                banks = [PG.get(), PA.get()]
                for q, (wn, slot, wt) in enumerate(slots):
                    n, k0 = q % 2, 4 * (q // 2)
                    nk = min(4, K - k0)
                    w3 = slot[:, 0:512 * nk].rearrange("p (k n) -> p k n", k=nk)
                    b, bt = banks[n]
                    for kk in range(nk):
                        k = k0 + kk
                        t = mm(b, lhs[:, k, 128 * i:128 * i + 128], w3[:, kk, :], k == 0, k == K - 1,
                               dep[i], wt, bt, sig=(kk == nk - 1))
                        if kk % 2:
                            yield
                    if i == 1:
                        wfree(wn, t)
                return [b for b, _ in banks], t
            return block(0), block(1)

        def unbank(y, *r):
            PG.put(y[0], r)
            PA.put(y[1], r)

        def seam(i, y, t, gain, hsrc, gname, *toks):
            th, r = post_norm(i, y, gain, H, hsrc, XN, t, *toks)
            unbank(y, r)
            if gname is None:
                yield
                return (yield from turn_x(i, H, None, uT, th)), th
            tn = norm_x(i, H, XN, small(1), small(1), th)
            yield
            return (yield from turn_x(i, XN, gname, uT, tn)), th

        def seam_add(i, y, t, gname, *toks):
            r = [tt(V, H[:, i, 512 * n:512 * n + 512], H[:, i, 512 * n:512 * n + 512], y[n], ALU.add, t, toks) for n in range(2)]
            unbank(y, r)
            tn = norm_x(i, H, XN, small(1), small(1), r)
            yield
            return (yield from turn_x(i, XN, gname, uT, tn)), r[1]

        def late(dep, hs, i, g):
            a, b = yield from g
            dep[i] += a
            hs[i].append(b)

        t_u, t_h = [[], []], [[], []]
        xr = view3(P + 23552, 2, 1024)
        t_xr = dma(SP, xr, x_d, sem("s_xr"), rw["out"], rw["y_free"])
        g_mix, g_ffn, g_ple = [gain_load(n, P + o, list(t_m.values()))
                               for n, o in (("mix_post_norm", 0), ("ffn_post_norm", 1024), ("ple_post_norm", 2048))]
        gain = g_mix
        (y0, t), _ = beside(g0, turned(1, mt, mHi, mLo, [t_m[1, 0], t_m[1, 1]], t_mh[1], t_ml[1]), 4)
        (y1, t1), _ = beside(g1, late(t_u, t_h, 0, seam(0, y0, t, gain, xr, "ffn_pre_norm", t_xr)), 9)
        s1 = late(t_u, t_h, 1, seam(1, y1, t1, gain, xr, "ffn_pre_norm", t_xr))

        SX[0] = P + 19968
        hid = view3(P + 11776, 32, 256)
        def split(o, x, n, *toks):
            hi, lo = (rview(SX[0] + o + q * n, n) for q in range(2))
            t = cp(S, hi, x, *toks)
            if n < 1024:
                return hi, lo, tt(V, lo, x, hi.bitcast(F32), ALU.subtract, t)
            return hi, lo, [tt(E, lo[:, c], x[:, c], hi[:, c].bitcast(F32), ALU.subtract, t)
                            for E, c in ((V, slice(0, 640)), (G, slice(640, 1024)))]

        class Down:

            def __init__(self, W, lhs, dep, K, o, o_tail):
                self.W, self.lhs, self.dep, self.K, self.o, self.o_tail = W, lhs, dep, K, o, o_tail
                self.at, self.ready = 0, []

            def prepare(self):
                k = self.at
                if k == self.K:
                    return
                self.at += 1
                if k % 2 == 0:
                    self.slot = wload([wcols(self.W, 0, 1024, k, 2, 0, 1024)])
                wn, slot, wt = self.slot
                if k < self.K - 8:
                    o, free = self.o + 1280 * (k % 3), self.used[k % 3]
                else:
                    o, free = self.o_tail + 1280 * (k - self.K + 8), self.tail_free
                w, a = slot[:, 1024 * (k % 2):1024 * (k % 2) + 1024], self.lhs[:, k, :]
                wh, wl = rview(o, 1024), rview(OR + 2048 * wn + 1024 * (k % 2), 1024)
                ah, al = rview(o + 1024, 256), rview(P + 11776 + 256 * k, 256)
                t = cp(S, wh, w, wt, free)
                ts_ = [tt(E, wl[:, c], w[:, c], wh[:, c].bitcast(F32), ALU.subtract, t)
                       for E, c in ((V, slice(0, 640)), (G, slice(640, 1024)))]
                t = cp(S, ah, a, self.dep[k // 2])
                ts_.append(tt(V, al, a, ah.bitcast(F32), ALU.subtract, t))
                self.ready.append((wn, wh, wl, ah, al, ts_))

            def part(self, i, k):
                wn, wh, wl, ah, al, ts_ = self.ready[k]
                a = slice(128 * i, 128 * i + 128)
                for n in range(2):
                    b, bt = self.banks[i][n]
                    c = slice(512 * n, 512 * n + 512)
                    t = mm3(b, (ah[:, a], al[:, a]), (wh[:, c], wl[:, c]), k == 0, k == self.K - 1, ts_, bt, sig=(n == 1))
                if i == 1 and k % 2:
                    wfree(wn, t)
                return t

            def first(self):
                self.banks = [[PG.get(), PA.get()] for _ in range(2)]
                for k in range(self.K):
                    while self.at < min(k + 3, self.K):
                        self.prepare()
                    t = self.part(0, k)
                    if k < self.K - 8:
                        self.used[k % 3] = self.part(1, k)
                return [b for b, _ in self.banks[0]], t

            def second(self):
                for k in range(self.K - 8, self.K):
                    t = self.part(1, k)
                    if k % 2:
                        yield
                return [b for b, _ in self.banks[1]], t

        class Ranges:

            def __init__(self, W, cols, dep, evac):
                self.W, self.cols, self.dep, self.evac = W, cols, dep, evac
                self.used, self.at, self.pieces = [None] * 3, 0, []

            def start(self, step):
                if step:
                    return
                assert self.dep[0] and self.dep[1]
                self.u = [rview(SX[0] + 2048 * q, 2048).rearrange("p (k t) -> p k t", k=8) for q in range(2)]
                self.tu = []
                for i in range(2):
                    hi, lo = (x[:, :, 128 * i:128 * i + 128] for x in self.u)
                    x = uT[:, :, 128 * i:128 * i + 128]
                    t = cp(S, hi, x, self.dep[i])
                    self.tu.append(tt(V, lo, x, hi.bitcast(F32), ALU.subtract, t))
                    self.prepare()

            def prepare(self):
                j = self.at
                if j == 4 * len(self.cols):
                    return
                self.at += 1
                if j % 2 == 0:
                    self.slot = wload([wcols(self.W, self.cols[j // 4], 512, 4 * (j // 2 % 2), 4, 0, 512)])
                wn, slot, wt = self.slot
                hi, lo, t = split(4096 + 2048 * (j % 3), slot[:, 1024 * (j % 2):1024 * (j % 2) + 1024], 1024, wt, self.used[j % 3])
                if j % 2:
                    wfree(wn, t)
                self.pieces.append((hi, lo, t))

            def run(self):
                for r in range(len(self.cols)):
                    banks = [P4.get() for _ in range(2)]
                    for c in range(4):
                        j = 4 * r + c
                        self.prepare()
                        hi, lo, tw = self.pieces[j]
                        for i in range(2):
                            a = slice(128 * i, 128 * i + 128)
                            for kk in range(2):
                                k, w = 2 * c + kk, slice(512 * kk, 512 * kk + 512)
                                t = mm3(banks[i][0], (self.u[0][:, k, a], self.u[1][:, k, a]), (hi[:, w], lo[:, w]), k == 0,
                                        k == 7, self.tu, tw, banks[i][1], sig=(kk == 1))
                            if c == 3:
                                P4.put(banks[i][0], *self.evac(r, i, banks[i][0], t))
                        self.used[j % 3] = t
                        if c == 1:
                            turn_waiting()
                        yield

        def to_hid(x, c0, i, t, frees):
            bank, bt = PB.get()
            for c in range(4):
                tp = tr(quarters(bank)[:, c, :], x[:, 128 * c:128 * c + 128], t, bt, sig=(c == 3))
            frees[:] = [tp]
            t = cp(S, hid[:, c0:c0 + 4, 128 * i:128 * i + 128], quarters(bank), tp)
            PB.put(bank, t)
            for q in range(2):
                t_hid[c0 // 2 + q].append(t)
            yield

        def ff_in(W, head, ranges, tail, n0, evac, dn, *free):
            yield from gemm_f(W, head, 8, evac, uT, t_u, head=4, pool=P4, mid=ranges.start)
            yield from ranges.run()
            yield from gemm_f(W, tail[:1], 8, lambda b, n, t: evac(b, n0 + n, t), uT, t_u, pool=P4)
            assert not waiting
            dn.tail_free = ranges.used
            dn.used = [[ranges.used, free] for _ in range(3)]
            dn.prepare()
            dn.prepare()
            yield from gemm_f(W, tail[1:], 8, lambda b, n, t: evac(b, n0 + 1 + n, t), uT, t_u, pool=P4)

        t_hid = [[] for _ in range(16)]
        rl = [view3(P + 512 * i, 2, 256) for i in range(2)]
        rlf = [None, None]

        def evac_relu2(bank, n, tok):
            t = act(rl[n % 2], halves(bank), ACT.Relu, tok, rlf[n % 2])
            t2 = tt(V, hid[:, 2 * n:2 * n + 2, :], halves(bank), rl[n % 2], ALU.mult, t)
            rlf[n % 2] = t2
            t_hid[n].append(t2)
            return [t2]

        stage = [[view(P + 3072 + 1024 * r + 512 * i, 512) for i in range(2)] for r in range(2)]
        st_free = [[[], []], [[], []]]

        def evac_relu2_t(r, i, bank, tok):
            st, free = stage[r % 2][i], st_free[r % 2][i]
            t = act(st, bank, ACT.Relu, tok, free)
            t = tt(V, st, bank, st, ALU.mult, t)
            waiting.append(to_hid(st, 8 + 4 * r, i, t, free))
            return [t]

        cols = [([(256 * n, 256, 0)], [128, 128]) for n in range(16)]
        ra = Ranges(A["w_ff_in"][0], [1024 + 512 * r for r in range(5)], t_u, evac_relu2_t)
        dn = Down(A["w_ff_out"][0], hid, t_hid, 32, P + 3072, P + 19968)
        beside(ff_in(A["w_ff_in"][0], cols[:4], ra, cols[14:], 14, evac_relu2, dn, st_free), s1, 5)

        t_hT, t_h = [[], []], [[], []]
        gain = g_ffn
        y0, t = dn.first()
        gh, gl = parts(P + 5120, OU)
        t_gh, t_gl = [[], []], [[], []]

        def seam_h(i, y, t):
            th, r = post_norm(i, y, gain, H, H, XN, t)
            unbank(y, r)
            yield
            yield from turned(i, H, gh, gl, th, t_gh[i], t_gl[i])
            t_h[i].append(th)

        g0, gz, prepare = full3(A["w_ple_gate"][0], [P + 11776, P + 13824, P + 15872, P + 3072], (gh, gl), t_gh, t_gl)
        prepare(0, t)
        prepare(1, t)
        (y1, t1), _ = beside(dn.second(), seam_h(0, y0, t), 3)
        prepare(2, t)
        prepare(3, t)
        s1 = seam_h(1, y1, t1)
        (z0, t), _ = beside(g0, s1, 8)
        g1 = gz
        gain = g_ple
        t_u, t_h2 = [[], []], [[], []]

        def ple_seam(i, z, t):
            te = []
            for n in range(2):
                c = slice(512 * n, 512 * n + 512)
                ta = act(XN[:, i, c], z[n], ACT.Sigmoid, t, t_gh, t_h)
                te.append(tt(V, pE[:, i, c], pE[:, i, c], XN[:, i, c], ALU.mult, ta, t_pe))
            unbank(z, ta)
            th, _ = post_norm(i, [pE[:, i, 0:512], pE[:, i, 512:1024]], gain, H, H, XN, te, ta)
            tn = norm_x(i, H, XN, small(1), small(1), th)
            yield
            return (yield from turn_x(i, XN, "norm_mix_2", uT, tn)), th

        (z1, t1), _ = beside(g1, late(t_u, t_h2, 0, ple_seam(0, z0, t)), 10)
        s1 = late(t_u, t_h2, 1, ple_seam(1, z1, t1))

        w2in = A["w_in_2"][0]
        gate2 = [view3(P + 11776 + 2048 * b, 2, 1024) for b in range(3)]
        RC = view3(P + 17920, 11, 256)
        QA = view3(P + 20736, 4, 256)
        vt = view3(P + 21760, 2, 660)
        memK = view3(P + 25128, 2, 256)
        memV = view3(P + 25640, 2, 256)
        rz = [view3(P + 23080 + 1024 * i, 2, 256) for i in range(2)]
        rt = [view3(P + 23592 + 1024 * i, 2, 256) for i in range(2)]
        oC = view3(P, 6, 256)
        t_rc, t_qa, rprev2 = {}, [], [None, None]
        t_vt2 = []

        def evac_a(bank, n, tok):
            if n < 2:
                t = cp(S, QA[:, 2 * n:2 * n + 2, :], halves(bank), tok)
                t_qa.append(t)
                return [t]
            m = 1 if n == 7 else 2
            c = 2 * (n - 2)
            cc, sc = (C_COSC, C_SINC) if n == 7 else (C_COS, C_SIN)

            def done(t):
                rprev2[n % 2] = t
                for j in range(m):
                    t_rc[c + j] = t
            g = rope(bank, m, tok, RC[:, c:c + m, :], const(cc, 256), const(sc, 256),
                     rz[n % 2][:, 0:m, :], rt[n % 2][:, 0:m, :], rprev2[n % 2], done)
            waiting.append(g)
            return next(g)

        dup = lambda c, d: [(c, 64, d), (c, 64, d + 64)]
        plan2 = [([(0, 256, 0)], [128, 128]), ([(256, 256, 0)], [128, 128]), ([(768, 256, 0)], [128, 128]),
                 ([(1152, 256, 0)], [128, 128]), ([(1476, 256, 0)], [128, 128]),
                 (dup(1024, 0) + dup(1408, 128), [128, 128]), (dup(1860, 0) + dup(1988, 128), [128, 128]),
                 ([(1732, 128, 0)], [128])]

        VP = [(512, 256, 0), (1088, 64, 256), (1924, 64, 320), (2052, 76, 384), (1472, 4, 460)]
        st2 = Stream(fslots(w2in, plan2[4:]) + [([wcols(w2in, c0, w, k, 4, d0, 464) for c0, w, d0 in VP], 4, 464, 464) for k in (0, 4)]
                     + tslots(w2in, 2128, 6))

        def main_a():
            yield from gemm_f(w2in, plan2[:4], 8, evac_a, uT, t_u, head=4, pool=P4, mid=stream_start(st2, t_u))

        beside(main_a(), s1, 5)
        wsc, g12 = small(8), small(24)

        def evac_vt2(i, b, t):
            fr = [cp(S, vt[:, i, 0:256], b[:, 0:256], t)]
            fr.append(act(g12[:, 12 * i:12 * i + 12], b[:, 448:460], ACT.Sigmoid, t))
            for d in range(2):
                fr.append(cp(V, vt[:, i, 256:640].rearrange("p (n d v) -> p n d v", n=3, d=2)[:, :, d, :],
                             b[:, 256:448].rearrange("p (n v) -> p n v", n=3), t, fr[1]))
            fr.append(ts(V, wsc[:, 4 * i:4 * i + 4], b[:, 460:464], 0.0625, None, ALU.mult, None, t))
            t_vt2.extend(fr)
            return fr

        def main_b():
            yield from st2.by_features(4, evac_a, n0=4, widths=[w for _, w in plan2])
            yield from st2.by_tokens(2, 464, evac_vt2)

        t_oc = {0: [], 1: [], 2: []}

        def stick():
            Z = view(P + 26152, 1536)
            SPL = view(P + 27688, 1536)
            TM = view(P + 29224, 1536)
            z4 = Z.rearrange("p (h t) -> p h t", h=4)
            s4 = SPL.rearrange("p (h t) -> p h t", h=4)
            st = const(C_ST, 384)
            tz = []
            for par in range(2):
                half = slice(64 * par, 64 * par + 64)
                b0, bt0 = PA.get()
                b1, bt1 = PA.get()
                for hh in range(2):
                    kT = QA[half, 2 + hh, :]
                    qT = QA[half, hh, :]
                    mm(b0[:, 256 * hh:256 * hh + 256], kT[:, 0:128], qT[:, 0:256], True, True, t_qa, bt0)
                    t = mm(b1[:, 128 * hh:128 * hh + 128], kT[:, 128:256], qT[:, 128:256], True, True, bt1, sig=True)
                zz = z4[:, par::2, :]
                ta = stt(zz[:, :, 0:256], halves(b0), 0.125, rep(st[:, 0:256], 2), ALU.mult, ALU.add, t)
                tb_ = stt(zz[:, :, 256:384], b1[:, 0:256].rearrange("p (h t) -> p h t", h=2), 0.125, rep(st[:, 256:384], 2),
                          ALU.mult, ALU.add, t)
                PA.put(b0, ta)
                PA.put(b1, tb_)
                tz += [ta, tb_]
                yield
            t = act(TM, Z, ACT.Abs, tz)
            t = act(TM, TM, ACT.Exp, t, scale=-1.0)
            t = act(TM, TM, ACT.Ln, t, bias=1.0)
            t_sp = stt(SPL, Z, 0.0, TM, ALU.max, ALU.add, t)
            yield
            LI, ONE = const(C_LI, 128), const(C_ONE, 128)
            tw = []
            for hp in range(2):
                hs = slice(2 * hp, 2 * hp + 2)
                b0, bt0 = PA.get()
                for q in range(2):
                    h = 2 * hp + q
                    mm(b0[:, 256 * q:256 * q + 256], LI, s4[:, h, 0:256], True, False, t_sp, bt0)
                    t = mm(b0[:, 256 * q + 128:256 * q + 256], ONE, s4[:, h, 256:384], False, True, sig=True)
                ta = tt(V, z4[:, hs, 0:256], z4[:, hs, 0:256], halves(b0), ALU.subtract, t)
                PA.put(b0, ta)
                b1, bt1 = PA.get()
                for q in range(2):
                    t = mm(b1[:, 128 * q:128 * q + 128], LI, s4[:, 2 * hp + q, 256:384], True, True, bt1, sig=True)
                tb_ = tt(V, z4[:, hs, 256:384], z4[:, hs, 256:384], b1[:, 0:256].rearrange("p (h t) -> p h t", h=2), ALU.subtract, t)
                PA.put(b1, tb_)
                tw += [ta, tb_]
                yield
            tw = act(Z, Z, ACT.Exp, tw)
            yield
            while len(t_vt2) < 10:
                yield
            for par in range(2):
                half = slice(64 * par, 64 * par + 64)
                b0, bt0 = PA.get()
                for hh in range(2):
                    h = 2 * hh + par
                    o = 256 * hh
                    mm(b0[half, o:o + 256], vt[:, 0, 64 * h:64 * h + 64], z4[:, h, 0:256], True, False, tw, t_vt2, bt0)
                    t = mm(b0[half, o + 128:o + 256], vt[:, 1, 64 * h:64 * h + 64], z4[:, h, 256:384], False, True, sig=True)
                t = cp(S, oC[half, 0:2, :], halves(b0)[half], t)
                PA.put(b0, t)
                t_oc[0].append(t)
                yield

        def scores4(i, qc, kc, W, pool, *toks):
            banks = [pool.get() for _ in range(2)]
            ts_ = []
            for par in range(2):
                half = slice(64 * par, 64 * par + 64)
                b, bt = banks[par]
                for hh in range(2):
                    t = mm(b[:, 256 * hh:256 * hh + W], RC[half, qc + hh, 128 * i:128 * i + 128], RC[half, kc, 0:W],
                           True, True, toks, bt, sig=True)
                ts_.append(t)
            return banks, ts_

        def turn4(E, eT, W, te, pool, et_free, toks=None):
            out_ = []
            for j in range(W // 128):
                bank, bt = pool.get()
                for h in range(4):
                    t = tr(bank[:, 128 * h:128 * h + 128], E[:, h, 128 * j:128 * j + 128], te, bt, sig=(h == 3))
                tc_ = cp(S, eT[:, 512 * j:512 * j + 512], bank, t, et_free)
                pool.put(bank, tc_)
                out_.append(tc_)
            return t, out_

        def spread(bank, br, i, t, pool):
            fr = []
            for par in range(2):
                half = slice(64 * par, 64 * par + 64)
                fr.append(cp(V, oC[half, 2 * br:2 * br + 2, 128 * i:128 * i + 128], quarters(bank)[half, par::2, :], t))
            pool.put(bank, fr)
            t_oc[br] += fr

        ca = const(C_CA, 256)

        def dsa(i):
            W = 128 * (i + 1)
            o_rel, o_acc, o_e, o_et = ((P + 11264, P + 30760, P + 25128, P + 25640),
                                       (P + 1536, P + 2560, P + 3392, P + 4416))[i]
            rel, E, eT = view3(o_rel, 4, W), view3(o_e, 4, W), view(o_et, 4 * W)
            acc, add, m8 = view(o_acc, W), view(o_acc + W, W), small(8)
            nm, den, rden = small(4), small(4), small(4)
            kr = [t_rc[2], t_rc[3], t_rc[7]]
            ks = [t_rc[0], t_rc[1], t_rc[6]]
            msk = ca[:, 256 - W:256]
            banks, t = scores4(i, 2, 7, W, PA, kr)
            tr_ = []
            for par in range(2):
                b = banks[par][0]
                t1 = act(rel[:, par::2, 0:W], halves(b)[:, :, 0:W], ACT.Relu, t[par])
                PA.put(b, t1)
                tr_.append(t1)
            src = msk
            for h in range(4):
                ta = stt(acc[:, 0:W], rel[:, h, 0:W], wsc[:, 4 * i + h:4 * i + h + 1], src, ALU.mult, ALU.add,
                         tr_, t_vt2, None if h == 0 else ta)
                src = acc[:, 0:W]
            yield
            cur = acc
            for r in range(8):
                a, w = acc[:, 0:W], cur[:, 0:W]
                t = V(lambda e, w=w: e.max(m8, w), [ta])
                ta = V(lambda e, a=a, w=w: e.match_replace(a, m8, w, TAKEN), [t])
                if r % 2:
                    yield
            t = ts(V, add[:, 0:W], acc[:, 0:W], TAKEN, NEG, ALU.is_gt, ALU.mult, ta)
            ta = tt(V, add[:, 0:W], add[:, 0:W], msk, ALU.add, t)
            banks, t = scores4(i, 0, 6, W, PA, ks)
            te = softmax4(E, banks, W, add, nm, den, rden, None, PA, t, ta)
            yield
            _, tT = turn4(E, eT, W, te, PA, None)
            yield
            bank, bt = PA.get()
            for j in range(i + 1):
                t = mm(bank, vt[:, j, 256:384], eT[:, 512 * j:512 * j + 512], j == 0, j == i, tT, t_vt2, bt, sig=(j == i))
            spread(bank, 1, i, t, PA)
            yield

        s_w1 = [sem("s_w10"), sem("s_w11")]

        def nsa_keys():
            blk = view(P + 5300, 480)
            tokT = RC[:, 10, :]
            b3 = blk.rearrange("p (l n) -> p l n", l=32)
            tb_ = []
            for n in range(15):
                tb_.append(tt(G, b3[:, :, n], tokT[:, 16 * n:16 * n + 32], vec("pos", 0, 32), ALU.add, t_rc[10]))
            tb_ = [tb_[-1]]
            yield
            bk, btk = PB.get()
            bv, btv = PB.get()
            w3 = view3(P + 23080, 16, 128)
            t = [t_rc[c] for c in range(11)]
            for s in range(2):
                for q, nm_ in enumerate(("cmp_w1_k_2", "cmp_w1_v_2")):
                    wt = dma(SP, w3[64 * q:64 * q + 64], A[nm_][0][1024 * s:1024 * s + 1024, :].rearrange("(l d) n -> d l n", d=64),
                             s_w1[s], t)
                for q, (b, bt) in enumerate(((bk, btk), (bv, btv))):
                    half = slice(64 * q, 64 * q + 64)
                    for l in range(16):
                        t = mm(b[0:15, 0:128], b3[half, 16 * s + l, :], w3[half, l, :], s == 0 and l == 0, s == 1 and l == 15,
                               tb_, wt, bt, sig=(l == 15))
                    if q == 0:
                        t_k = t
                yield
            hd = view3(P + 5780, 2, 128)
            tmp = view3(P + 6036, 2, 128)
            th = []
            for q, (b, t_) in enumerate(((bk, t_k), (bv, t))):
                x, y = hd[0:15, q, :], tmp[0:15, q, :]
                t1 = cp(V, x, b[0:15, 0:128], t_)
                PB.put(b, t1)
                t2 = tt(V, y, x, x, ALU.mult, t1)
                t2 = ts(V, y, y, 0.044715, 1.0, ALU.mult, ALU.add, t2)
                t2 = tt(V, y, y, x, ALU.mult, t2)
                t2 = act(y, y, ACT.Sigmoid, t2, scale=2.0 * math.sqrt(2.0 / math.pi))
                th.append(tt(V, x, x, y, ALU.mult, t2))
            yield
            bank, bt = PB.get()
            for q in range(2):
                t = tr(bank[:, 16 * q:16 * q + 15], hd[0:15, q, :], th[q], bt, sig=True)
            hT_ = view(P + 6292, 32)
            t1 = [cp(V, hT_[:, 16 * q:16 * q + 15], bank[:, 16 * q:16 * q + 15], t) for q in range(2)]
            PB.put(bank, *t1)
            wn, slot, wt = wload([(lambda s, o=o: s[:, o:o + 64], A[nm_][0])
                                  for o, nm_ in ((0, "cmp_w2_k_2"), (64, "cmp_w2_k_2"), (128, "cmp_w2_v_2"), (192, "cmp_w2_v_2"))])
            bank, bt = PB.get()
            t = mm(bank[:, 0:15], slot[:, 0:128], hT_[:, 0:15], True, True, t1, wt, bt, sig=True)
            t2 = mm(bank[0:15, 128:256], hT_[:, 16:31], slot[:, 128:256], True, True, sig=True)
            wfree(wn, t2)
            kc = view(P + 6324, 16)
            vc = view(P + 6340, 128)
            t_kc = cp(V, kc[:, 0:15], bank[:, 0:15], t2)
            t_vc = cp(V, vc[0:15, :], bank[0:15, 128:256], t2)
            PB.put(bank, t_kc, t_vc)
            yield nsa(0, kc, vc, t_kc, t_vc), nsa(1, kc, vc, t_kc, t_vc)

        def nsa(i, kc, vc, t_kc, t_vc):
            W = 128 * (i + 1)
            o_e, o_et, o_ec, o_etc = ((P + 23080, P + 23592, P + 24616, P + 24104),
                                      (P + 9216, P + 10240, P + 6468, P + 6528))[i]
            E, eT = view3(o_e, 4, W), view(o_et, 4 * W)
            EC = view(o_ec, 60).rearrange("p (h n) -> p h n", h=4)
            eTc = view(o_etc, 512)
            nm, den, rden = small(4), small(4), small(4)
            mx = small(4)
            e_free = et_free = ec_free = None
            msk = ca[:, 256 - W:256]
            o_bank, obt = PB.get()
            sb_, sbt = PA.get()
            sb2, sbt2 = PA.get()
            for par, (b, bt) in enumerate(((sb_, sbt), (sb2, sbt2))):
                half = slice(64 * par, 64 * par + 64)
                for hh in range(2):
                    t = mm(b[:, 16 * hh:16 * hh + 15], RC[half, 4 + hh, 128 * i:128 * i + 128], kc[half, 0:15], True, True,
                           t_kc, t_rc[4], bt, sig=True)
                b3_ = b[:, 0:32].rearrange("p (h n) -> p h n", h=2)[:, :, 0:15]
                tc_ = stt(EC[:, par::2, :], b3_, 0.125, rep(const(C_CMA + 15 * i, 15), 2), ALU.mult, ALU.add, t, ec_free)
                PA.put(b, tc_)
            t = red(mx, EC, ALU.max, tc_)
            t = tt(V, EC, EC, bc(mx, 15), ALU.subtract, t)
            t = act(EC, EC, ACT.Exp, t)
            t = tt(V, EC, EC, rep(const(C_CMM + 15 * i, 15), 4), ALU.mult, t)
            t = red(mx, EC, ALU.add, t)
            t = ts(V, mx, mx, 1e-30, None, ALU.max, None, t)
            t = recip(mx, mx, t)
            gi = g12[:, 12 * i:12 * i + 12].rearrange("p (h b) -> p h b", b=3)
            t = tt(V, mx, mx, gi[:, :, 0], ALU.mult, t, t_vt2)
            t_ec = tt(V, EC, EC, bc(mx, 15), ALU.mult, t)
            yield
            bank, bt = PA.get()
            for h in range(4):
                t = tr(bank[0:15, 128 * h:128 * h + 128], EC[:, h, :], t_ec, bt, sig=(h == 3))
            ec_free = t
            t = cp(S, eTc[0:15, :], bank[0:15, :], t, et_free)
            PA.put(bank, t)
            mm(o_bank, vc[0:15, :], eTc[0:15, :], True, False, t, t_vc, obt)
            yield
            for br in (1, 2):
                banks, t = scores4(i, 4, 7 + br, W, PA, t_rc[4], t_rc[7 + br])
                te = softmax4(E, banks, W, msk, nm, den, rden, gi[:, :, br], PA, t, t_vt2, e_free)
                yield
                e_free, tT = turn4(E, eT, W, te, PA, et_free)
                yield
                for j in range(i + 1):
                    lastmm = br == 2 and j == i
                    t = mm(o_bank, vt[:, j, 256 + 128 * br:384 + 128 * br], eT[:, 512 * j:512 * j + 512], False, lastmm,
                           tT, sig=(j == i))
                et_free = t
                yield
            spread(o_bank, 2, i, t, PB)

        t_g2 = []
        gate_main2 = gate_ranges(st2, 6, lambda r, i: half_of(gate2[r // 2], i, r % 2), t_g2)
        alone(main_b())
        got2 = []
        st2.after = lambda: got2.extend(up_loads(A["w_up_2"][0, 0], 2))
        drive(gate_main2, nsa_keys(), dsa(1), dsa(0), stick())

        mt = view3(P + 17920, 2, 1024)
        tm = [view(P + 24064 + 512 * i, 512) for i in range(2)]
        t_m = {}
        tmr = [None] * 2

        def evac_up(br):
            def f(i, n, bank, tok):
                m, g = half_of(mt, i, n), half_of(gate2[br], i, n)
                if br == 0:
                    t_m[i, n] = t = tt(V, m, bank, g, ALU.mult, tok, t_g2)
                    return [t]
                t = tt(V, tm[n], bank, g, ALU.mult, tok, tmr[n])
                t_m[i, n] = tmr[n] = tt(V, m, m, tm[n], ALU.add, t, t_m[i, n])
                return [t]
            return f

        all_oc = [t_oc[0], t_oc[1], t_oc[2]]
        mHi, mLo = parts(P + 1536, P + 3584)
        t_mh, t_ml = [[], []], [[], []]
        ups = [up(A["w_up_2"][0, br], 2, oC[:, 2 * br:2 * br + 2, :], [t_oc[br]] * 2, evac_up(br), got2 if br == 0 else None) for br in range(3)]
        for _ in range(3):
            next(ups[0])
        g0, g1, prepare = full3(A["w_out_2"][0], [P + 26152, P + 28200, P + 19968, P + 11776], (mHi, mLo), t_mh, t_ml)
        prepare(0, all_oc)
        alone(ups[0])
        gate0_free = list(t_m.values())
        next(ups[1])
        prepare(1, all_oc)
        for _ in range(2):
            next(ups[1])
        prepare(2, all_oc)
        alone(ups[1])
        gate1_free = list(t_m.values())
        next(ups[2])
        prepare(3, gate0_free)
        for _ in range(2):
            next(ups[2])
        alone(turned(0, mt, mHi, mLo, [t_m[0, 0], t_m[0, 1]], t_mh[0], t_ml[0]))
        alone(ups[2])

        mem_sb = view3(P + 13824, 2, 1024)
        mem_n = XN
        memT = view3(P + 22016, 8, 256)
        s_m = sem("s_m")
        t_mem = dma(SP, mem_sb, A["mem_2"][0].rearrange("(i p) d -> p i d", p=128), s_m, gate1_free)
        t_mT = [[], []]

        def mem_norm():
            for i in range(2):
                t_mT[i] += yield from norm_t(i, mem_sb, mem_n, "norm_mem_kv_2", memT, t_mem, t_oc[0], t_oc[1], t_oc[2])

        def fill():
            yield from turned(1, mt, mHi, mLo, [t_m[1, 0], t_m[1, 1]], t_mh[1], t_ml[1])
            yield from mem_norm()

        (y0, t), _ = beside(g0, fill(), 3)
        t_u, t_h = [[], []], [[], []]
        (y1, t1), _ = beside(g1, late(t_u, t_h, 0, seam_add(0, y0, t, "norm_mem_q_2", t_h2)), 9)
        s1 = late(t_u, t_h, 1, seam_add(1, y1, t1, "norm_mem_q_2", t_h2))
        t_mk, t_mv = [], []

        def evac_mk(bank, n, tok):
            t_mk.append(cp(S, memK, halves(bank), tok))
            return [t_mk[-1]]

        w_kv = A["w_mem_kv_2"][0]

        def mem_kv():
            yield from gemm_f(w_kv, [([(0, 256, 0)], [128, 128])], 8, evac_mk, memT, t_mT)

        def mem_v():
            banks = [PG.get() for _ in range(2)]
            t = yield from gemm_t([([wcols(w_kv, 256, 256, 0, 8, 0, 256)], 8)], memT, t_mT, banks, 256, 8)
            for i in range(2):
                t_mv.append(cp(S, memV[:, i, :], banks[i][0][:, 0:256], t))
                PG.put(banks[i][0], t_mv[-1])

        beside(mem_kv(), s1, 5)
        mq = view3(P + 17920, 2, 256)
        oM = view3(P + 18432, 2, 256)
        t_mq = []

        def evac_mq(bank, n, tok):
            t_mq.append(cp(S, mq, halves(bank), tok))
            return [t_mq[-1]]

        alone(gemm_f(A["w_mem_q_2"][0], [([(0, 256, 0)], [128, 128])], 8, evac_mq, uT, t_u))
        t_om = []

        def mem_side(i):
            o = P + 11776 + 2048 * i
            E, eT = view3(o, 4, 256), view(o + 1024, 1024)
            nm, den, rden = small(4), small(4), small(4)
            zero = ca[:, 0:1].broadcast_to([128, 256])
            pool = (PA, PB)[i]
            banks = [pool.get() for _ in range(2)]
            for par in range(2):
                half = slice(64 * par, 64 * par + 64)
                b, bt = banks[par]
                for hh in range(2):
                    t = mm(b[:, 256 * hh:256 * hh + 256], mq[half, hh, 128 * i:128 * i + 128], memK[half, hh, :], True, True,
                           t_mq, t_mk, bt, sig=True)
            te = softmax4(E, banks, 256, zero, nm, den, rden, None, pool, t)
            yield
            _, tT = turn4(E, eT, 256, te, pool, None)
            yield
            e4 = eT.rearrange("p (j h t) -> p j h t", j=2, h=4)
            for par in range(2):
                half = slice(64 * par, 64 * par + 64)
                bank, bt = pool.get()
                for hh in range(2):
                    h = 2 * hh + par
                    for j in range(2):
                        t = mm(bank[half, 128 * hh:128 * hh + 128], memV[:, j, 64 * h:64 * h + 64], e4[:, j, h, :], j == 0, j == 1,
                               tT, t_mv, bt, sig=(j == 1))
                t = cp(S, oM[half, :, 128 * i:128 * i + 128], bank[half, 0:256].rearrange("p (h t) -> p h t", h=2), t)
                pool.put(bank, t)
                t_om.append(t)
            yield

        m0, m1 = mem_side(0), mem_side(1)
        next(m0)
        next(m1)
        alone(mem_v())
        drive(m0, m1)
        t_u, t_h2 = [[], []], [[], []]
        g0, g1 = full(A["w_mem_o_2"][0], oM, [t_om, t_om], 2)
        y0, t = alone(g0)
        (y1, t1), _ = beside(g1, late(t_u, t_h2, 0, seam_add(0, y0, t, "norm_ffn_2", t_h)), 99)
        s1 = late(t_u, t_h2, 1, seam_add(1, y1, t1, "norm_ffn_2", t_h))

        SX[0] = P + 17408
        hid = view3(P + 11776, 22, 256)
        t_hid = [[] for _ in range(11)]
        sl = [view(P + 2048 + 256 * i, 256) for i in range(2)]
        slf = [None, None]

        def evac_swiglu(bank, n, tok):
            a, b = bank[:, 0:256], bank[:, 256:512]
            s_ = sl[n % 2]
            t = act(s_, a, ACT.Sigmoid, tok, slf[n % 2])
            t = tt(V, s_, s_, a, ALU.mult, t)
            t = tt(V, hid[:, n, :], s_, b, ALU.mult, t)
            slf[n % 2] = t
            t_hid[n // 2].append(t)
            return [t]

        stage2 = [[view(P + 1024 * r + 512 * i, 512) for i in range(2)] for r in range(2)]
        st_free2 = [[[], []], [[], []]]
        t_a = {}

        def evac_swiglu_t(r, i, bank, tok):
            q = r // 2
            st, free = stage2[q % 2][i], st_free2[q % 2][i]
            if r % 2 == 0:
                t = act(st, bank, ACT.Sigmoid, tok, free)
                t_a[i] = tt(V, st, bank, st, ALU.mult, t)
                return [t_a[i]]
            t = tt(V, st, bank, st, ALU.mult, tok, t_a[i])
            waiting.append(to_hid(st, 4 + 4 * q, i, t, free))
            return [t]

        cols = [([(128 * n, 128, 0), (2816 + 128 * n, 128, 128)], [128, 128]) for n in range(22)]
        rb = Ranges(A["w_ffn_in_2"][0], [512 + 512 * q + 2816 * h for q in range(4) for h in range(2)], t_u, evac_swiglu_t)
        dn = Down(A["w_ffn_out_2"][0], hid, t_hid, 22, P + 3072, P + 17408)
        beside(ff_in(A["w_ffn_in_2"][0], cols[:4], rb, cols[20:], 20, evac_swiglu, dn), s1, 5)
        gain = gain_load("norm_final_2", P + 28672, t_h2)
        y0, t = dn.first()
        g1 = dn.second()

        s_out = sem("s_out")
        o_d = out[0].rearrange("(i p) d -> p i d", p=128)

        def final(i, y, t):
            ss, rs = small(1), small(1)
            r = [tt(V, H[:, i, 512 * n:512 * n + 512], H[:, i, 512 * n:512 * n + 512], y[n], ALU.add, t, t_h2) for n in range(2)]
            t = act(XN[:, i, :], H[:, i, :], ACT.Square, r, accum=ss)
            t = rstd(ss, rs, 1024, EPS, t)
            t = stt(XN[:, i, :], H[:, i, :], rs, gain[0], ALU.mult, ALU.mult, t, gain[1])
            return dma(SP, o_d[:, i, :], XN[:, i, :], s_out, t)

        final(0, y0, t)
        y1, t1 = alone(g1)
        SP.wait([final(1, y1, t1)])

        block = ctx.enter_context(nc.Block())

        @block.sync
        def _(e):
            SP.run(e)

        @block.gpsimd
        def _(e):
            G.run(e)

        @block.scalar
        def _(e):
            S.run(e)

        @block.tensor
        def _(e):
            PE.run(e)

        @block.vector
        def _(e):
            V.run(e)


_INS = ['x', 'p', 'mix_pre_norm', 'w_in', 'rwkv_mu', 'rwkv_w0', 'rwkv_w2', 'rwkv_a0', 'rwkv_a2', 'rwkv_g2', 'rwkv_k_k',
        'rwkv_k_a', 'rwkv_r_k', 'rwkv_ln_w', 'rwkv_ln_b', 'w_attn_up', 'w_rwkv_up', 'w_out', 'mix_post_norm',
        'ffn_pre_norm', 'w_ff_in', 'w_ff_out', 'ffn_post_norm', 'w_ple', 'w_ple_gate', 'ple_post_norm', 'mem_2',
        'norm_mix_2', 'w_in_2', 'cmp_pos_k_2', 'cmp_w1_k_2', 'cmp_w2_k_2', 'cmp_pos_v_2', 'cmp_w1_v_2', 'cmp_w2_v_2',
        'w_up_2', 'w_out_2', 'norm_mem_q_2', 'norm_mem_kv_2', 'w_mem_q_2', 'w_mem_kv_2', 'w_mem_o_2', 'norm_ffn_2',
        'w_ffn_in_2', 'w_ffn_out_2', 'norm_final_2']


def kernel(**inputs):
    import numpy as _np
    import concourse.bacc as _bacc
    from concourse import mybir as _mybir
    from concourse.bass_utils import run_bass_kernel_spmd as _run

    nc = _bacc.Bacc("TRN2", target_bir_lowering=False, num_devices=1)
    arrays, args = {}, {}
    for name in _INS:
        a = _np.ascontiguousarray(inputs[name])
        arrays[f"in_{name}_dram"] = a
        args[name] = nc.dram_tensor(f"in_{name}_dram", a.shape, _mybir.dt.from_np(a.dtype), kind="ExternalInput").ap()
    c = shape_constants()
    arrays["consts_dram"] = c
    consts = nc.dram_tensor("consts_dram", c.shape, _mybir.dt.float32, kind="ExternalInput").ap()
    out = nc.dram_tensor("out_0_dram", (1, 256, 1024), _mybir.dt.float32, kind="ExternalOutput").ap()
    arrays["vecs_dram"], arrays["pt_dram"] = vectors(inputs), p_by_features(inputs)
    vecs = nc.dram_tensor("vecs_dram", (128, 128), _mybir.dt.float32, kind="ExternalInput").ap()
    pt = nc.dram_tensor("pt_dram", (128, 2, 256), _mybir.dt.float32, kind="ExternalInput").ap()
    program(nc, args, consts, vecs, pt, out)
    r = _run(nc, [arrays], core_ids=[0])
    return r.results[0]["out_0_dram"]
```
